# Optimizing a Trainium2 kernel written in Bass

```python
import jax, jax.numpy as jnp
from jax import lax
import numpy as np
import jax
import jax.numpy as jnp

D_MODEL = 1024
BATCH = 1
SEQ = 512
DEPTH = 2

N_MIXERS = 2
SB_HEADS = 16
SB_HEAD_DIM = D_MODEL // SB_HEADS
Q_BLOCK = 128
D_RNN = (D_MODEL * 5) // 4
LRU_BLOCKS = 10
LRU_BLOCK_W = D_RNN // LRU_BLOCKS
CONV_W = 4
LRU_C = 8.0
D_FF = ((8 * D_MODEL // 3 + 127) // 128) * 128
N_SUB = 3
MACARON_W = 0.5
EPS = 1e-6
N_SB_LAYERS = (DEPTH + 1) // 2
N_LRU_LAYERS = DEPTH // 2


def rmsnorm(x, g):
    xf = x.astype(jnp.float32)
    inv = lax.rsqrt(jnp.mean(xf * xf, axis=-1, keepdims=True) + EPS)
    return (xf * inv).astype(x.dtype) * g

def sublayer_input(x, g, mod_j):
    shift, scale, gate = mod_j[:, 0], mod_j[:, 1], mod_j[:, 2]
    h = rmsnorm(x, g) * (1 + scale[:, None, :]) + shift[:, None, :]
    return h, (1 + gate)[:, None, :]

def swiglu(h, w_gu, w_down):
    g, u = jnp.split(h @ w_gu, 2, axis=-1)
    return (jax.nn.silu(g) * u) @ w_down

def stick_breaking_attention(h, w_qkv, w_o):
    B, S, _ = h.shape
    qkv = (h @ w_qkv).reshape(B, S, 3, SB_HEADS, SB_HEAD_DIM)
    qkv = jnp.transpose(qkv, (2, 0, 3, 1, 4)).astype(jnp.float32)
    q = qkv[0] * (SB_HEAD_DIM ** -0.5)
    k, v = qkv[1], qkv[2]
    outs = []
    for blk in range(S // Q_BLOCK):
        t0 = blk * Q_BLOCK
        L = t0 + Q_BLOCK
        z = jnp.einsum('bhqd,bhkd->bhqk', q[:, :, t0:L], k[:, :, :L])
        t_idx = t0 + jnp.arange(Q_BLOCK)
        s_idx = jnp.arange(L)
        mask = s_idx[None, :] < t_idx[:, None]
        log_keep = jnp.where(mask, jax.nn.log_sigmoid(-z), 0.0)
        later = lax.cumsum(log_keep, axis=3, reverse=True) - log_keep
        w = jnp.where(mask, jnp.exp(jax.nn.log_sigmoid(z) + later), 0.0)
        outs.append(jnp.einsum('bhqk,bhkd->bhqd', w, v[:, :, :L]))
    o = jnp.concatenate(outs, axis=2)
    o = jnp.transpose(o, (0, 2, 1, 3)).reshape(B, S, D_MODEL).astype(h.dtype)
    return o @ w_o

def _lin_rec_combine(left, right):
    a1, b1 = left
    a2, b2 = right
    return a1 * a2, a2 * b1 + b2

def rglru_block(h, w_in, conv_w, conv_b, w_r, b_r, w_i, b_i, lam, w_out):
    B, S, _ = h.shape
    gate, xb = jnp.split(h @ w_in, 2, axis=-1)
    xp = jnp.pad(xb, ((0, 0), (CONV_W - 1, 0), (0, 0)))
    xc = conv_b + xp[:, 0:S] * conv_w[0]
    for tap in range(1, CONV_W):
        xc = xc + xp[:, tap:tap + S] * conv_w[tap]
    xblk = xc.reshape(B, S, LRU_BLOCKS, LRU_BLOCK_W)
    r = jax.nn.sigmoid(jnp.einsum('bsnk,nkj->bsnj', xblk, w_r).reshape(B, S, D_RNN) + b_r)
    i = jax.nn.sigmoid(jnp.einsum('bsnk,nkj->bsnj', xblk, w_i).reshape(B, S, D_RNN) + b_i)
    log_a = -LRU_C * r.astype(jnp.float32) * jax.nn.softplus(-lam.astype(jnp.float32))
    a = jnp.exp(log_a)
    b = jnp.sqrt(-jnp.expm1(2.0 * log_a)) * (i * xc).astype(jnp.float32)
    _, hs = lax.associative_scan(_lin_rec_combine, (a, b), axis=1)
    y = jax.nn.gelu(gate) * hs.astype(h.dtype)
    return y @ w_out

def first_inputs(seed: int = 0) -> dict:
    key = jax.random.key(seed)
    ks = jax.random.split(key, 24)
    D = D_MODEL
    f32 = jnp.float32
    nrm = lambda k, shape, s: jax.random.normal(k, shape, f32) * s
    x = nrm(ks[0], (BATCH, SEQ, D), 1.0)
    c = nrm(ks[1], (BATCH, D), 1.0)
    mod_w = nrm(ks[2], (DEPTH, D, N_SUB * 3 * D), 0.2 * D ** -0.5)
    mod_b = nrm(ks[3], (DEPTH, N_SUB * 3 * D), 0.05)
    norm_g = 1.0 + nrm(ks[4], (DEPTH, N_SUB, D), 0.02)
    ffn_w_gu = nrm(ks[5], (DEPTH, 2, D, 2 * D_FF), D ** -0.5)
    ffn_w_down = nrm(ks[6], (DEPTH, 2, D_FF, D), D_FF ** -0.5)
    sb_w_qkv = nrm(ks[7], (N_SB_LAYERS, D, 3 * D), D ** -0.5)
    sb_w_o = nrm(ks[8], (N_SB_LAYERS, D, D), D ** -0.5)
    lru_w_in = nrm(ks[9], (N_LRU_LAYERS, D, 2 * D_RNN), D ** -0.5)
    lru_conv_w = nrm(ks[10], (N_LRU_LAYERS, CONV_W, D_RNN), CONV_W ** -0.5)
    lru_conv_b = nrm(ks[11], (N_LRU_LAYERS, D_RNN), 0.02)
    lru_w_r = nrm(ks[12], (N_LRU_LAYERS, LRU_BLOCKS, LRU_BLOCK_W, LRU_BLOCK_W), LRU_BLOCK_W ** -0.5)
    lru_b_r = nrm(ks[13], (N_LRU_LAYERS, D_RNN), 0.1)
    lru_w_i = nrm(ks[14], (N_LRU_LAYERS, LRU_BLOCKS, LRU_BLOCK_W, LRU_BLOCK_W), LRU_BLOCK_W ** -0.5)
    lru_b_i = nrm(ks[15], (N_LRU_LAYERS, D_RNN), 0.1)
    a_c = jax.random.uniform(ks[16], (N_LRU_LAYERS, D_RNN), f32, 0.9, 0.999)
    a0 = a_c ** (1.0 / LRU_C)
    lru_lambda = jnp.log(a0) - jnp.log1p(-a0)
    lru_w_out = nrm(ks[17], (N_LRU_LAYERS, D_RNN, D), D_RNN ** -0.5)
    final_norm_g = 1.0 + nrm(ks[18], (D,), 0.02)
    return {"x": x, "c": c, "mod_w": mod_w, "mod_b": mod_b, "norm_g": norm_g,
            "ffn_w_gu": ffn_w_gu, "ffn_w_down": ffn_w_down,
            "sb_w_qkv": sb_w_qkv, "sb_w_o": sb_w_o,
            "lru_w_in": lru_w_in, "lru_conv_w": lru_conv_w, "lru_conv_b": lru_conv_b,
            "lru_w_r": lru_w_r, "lru_b_r": lru_b_r, "lru_w_i": lru_w_i, "lru_b_i": lru_b_i,
            "lru_lambda": lru_lambda, "lru_w_out": lru_w_out, "final_norm_g": final_norm_g}

def first_block(x, c, mod_w, mod_b, norm_g, ffn_w_gu, ffn_w_down, sb_w_qkv, sb_w_o,
              lru_w_in, lru_conv_w, lru_conv_b, lru_w_r, lru_b_r, lru_w_i, lru_b_i,
              lru_lambda, lru_w_out, final_norm_g):
    B = x.shape[0]
    c_act = jax.nn.silu(c)
    for layer in range(DEPTH):
        mod = (c_act @ mod_w[layer] + mod_b[layer]).reshape(B, N_SUB, 3, D_MODEL)
        h, g = sublayer_input(x, norm_g[layer, 0], mod[:, 0])
        x = x + MACARON_W * g * swiglu(h, ffn_w_gu[layer, 0], ffn_w_down[layer, 0])
        h, g = sublayer_input(x, norm_g[layer, 1], mod[:, 1])
        j = layer // N_MIXERS
        if layer % N_MIXERS == 0:
            y = stick_breaking_attention(h, sb_w_qkv[j], sb_w_o[j])
        else:
            y = rglru_block(h, lru_w_in[j], lru_conv_w[j], lru_conv_b[j], lru_w_r[j], lru_b_r[j],
                            lru_w_i[j], lru_b_i[j], lru_lambda[j], lru_w_out[j])
        x = x + g * y
        h, g = sublayer_input(x, norm_g[layer, 2], mod[:, 2])
        x = x + MACARON_W * g * swiglu(h, ffn_w_gu[layer, 1], ffn_w_down[layer, 1])
    return rmsnorm(x, final_norm_g)


HEAD_DIM = 64
ROPE_THETA = 10000.0
RMS_EPS = 1e-6
N_BRANCH = 3

A_HEADS = 6
A_WIDTH = A_HEADS * HEAD_DIM
A_BLOCK = 256
A_TOPK = 3
A_QCHUNK = 32

B_HEADS = 6
B_WIDTH = B_HEADS * HEAD_DIM
B_KV_DIM = HEAD_DIM
B_TOPK = 256
B_IDX_HEADS = 4
B_IDX_DIM = HEAD_DIM
B_QCHUNK = 128

C_GROUPS = ((128, 1), (512, 4), (2048, 16))
C_SLOTS = 4
C_HEADS = C_SLOTS * len(C_GROUPS)
C_WIDTH = C_SLOTS * HEAD_DIM
C_BLOCK = 128

IN_SPLITS = (A_WIDTH, A_WIDTH, A_WIDTH, A_WIDTH,
             B_WIDTH, B_KV_DIM, B_KV_DIM, B_WIDTH, B_IDX_HEADS * B_IDX_DIM, B_IDX_DIM, B_IDX_HEADS,
             C_HEADS * HEAD_DIM, C_HEADS * HEAD_DIM, C_HEADS * HEAD_DIM, C_WIDTH,
             N_BRANCH * D_MODEL)
IN_WIDTH = sum(IN_SPLITS)
IN_OFFSETS = tuple(int(o) for o in np.cumsum(IN_SPLITS)[:-1])


def rmsnorm_2(x, g):
    xf = x.astype(jnp.float32)
    y = xf * lax.rsqrt(jnp.mean(xf * xf, axis=-1, keepdims=True) + RMS_EPS)
    return (y * g.astype(jnp.float32)).astype(x.dtype)

def rope_tables(seq_len):
    inv_freq = 1.0 / (ROPE_THETA ** (jnp.arange(0, HEAD_DIM, 2, dtype=jnp.float32) / HEAD_DIM))
    ang = jnp.arange(seq_len, dtype=jnp.float32)[:, None] * inv_freq[None, :]
    return jnp.cos(ang), jnp.sin(ang)

def apply_rope(x, cos, sin):
    half = HEAD_DIM // 2
    c = cos[None, :, None, :].astype(x.dtype)
    s = sin[None, :, None, :].astype(x.dtype)
    x1, x2 = x[..., :half], x[..., half:]
    return jnp.concatenate([x1 * c - x2 * s, x1 * s + x2 * c], axis=-1)

def moba_attention(q, k, v):
    bsz, seq, nh, hd = q.shape
    scale = hd ** -0.5
    n_blk = -(-seq // A_BLOCK)
    pad = n_blk * A_BLOCK - seq
    qh = q.transpose(0, 2, 1, 3)
    kb = jnp.pad(k.transpose(0, 2, 1, 3), ((0, 0), (0, 0), (0, pad), (0, 0))).reshape(bsz, nh, n_blk, A_BLOCK, hd)
    vb = jnp.pad(v.transpose(0, 2, 1, 3), ((0, 0), (0, 0), (0, pad), (0, 0))).reshape(bsz, nh, n_blk, A_BLOCK, hd)
    k_mean = jnp.mean(kb.astype(jnp.float32), axis=3)
    topk = max(1, min(A_TOPK, n_blk - 1))
    b_ix = jnp.arange(bsz)[:, None, None, None]
    h_ix = jnp.arange(nh)[None, :, None, None]
    blk_ids = jnp.arange(n_blk)
    n_sel = topk * A_BLOCK

    def chunk(ci):
        t0 = ci * A_QCHUNK
        own = t0 // A_BLOCK
        t_pos = t0 + jnp.arange(A_QCHUNK)
        qc = lax.dynamic_slice_in_dim(qh, t0, A_QCHUNK, axis=2)
        k_own = lax.dynamic_index_in_dim(kb, own, axis=2, keepdims=False)
        v_own = lax.dynamic_index_in_dim(vb, own, axis=2, keepdims=False)
        kpos_own = own * A_BLOCK + jnp.arange(A_BLOCK)
        s_own = jnp.einsum('bhqd,bhkd->bhqk', qc, k_own, preferred_element_type=jnp.float32) * scale
        s_own = jnp.where(kpos_own[None, :] <= t_pos[:, None], s_own, -jnp.inf)
        gate = jnp.einsum('bhqd,bhnd->bhqn', qc.astype(jnp.float32), k_mean)
        gate = jnp.where(blk_ids < own, gate, -jnp.inf)
        g_val, g_idx = lax.top_k(gate, topk)
        sel_ok = jnp.isfinite(g_val)
        k_sel = kb[b_ix, h_ix, g_idx]
        v_sel = vb[b_ix, h_ix, g_idx]
        s_sel = jnp.einsum('bhqd,bhqnkd->bhqnk', qc, k_sel, preferred_element_type=jnp.float32) * scale
        s_sel = jnp.where(sel_ok[..., None], s_sel, -jnp.inf)
        scores = jnp.concatenate([s_sel.reshape(bsz, nh, A_QCHUNK, n_sel), s_own], axis=-1)
        p = jax.nn.softmax(scores, axis=-1).astype(v.dtype)
        p_sel = p[..., :n_sel].reshape(bsz, nh, A_QCHUNK, topk, A_BLOCK)
        out = jnp.einsum('bhqnk,bhqnkd->bhqd', p_sel, v_sel)
        return out + jnp.einsum('bhqk,bhkd->bhqd', p[..., n_sel:], v_own)

    outs = lax.map(chunk, jnp.arange(seq // A_QCHUNK))
    return outs.transpose(1, 0, 3, 2, 4).reshape(bsz, seq, nh, hd)

def dsa_attention(q, k, v, iq, ik, iw):
    bsz, seq, nh, hd = q.shape
    scale = hd ** -0.5
    n_keep = min(B_TOPK, seq // 4)
    b_ix = jnp.arange(bsz)[:, None, None]
    key_pos = jnp.arange(seq)
    iw = iw.astype(jnp.float32) * (B_IDX_HEADS * B_IDX_DIM) ** -0.5

    def chunk(ci):
        t0 = ci * B_QCHUNK
        t_pos = t0 + jnp.arange(B_QCHUNK)
        iq_c = lax.dynamic_slice_in_dim(iq, t0, B_QCHUNK, axis=1)
        iw_c = lax.dynamic_slice_in_dim(iw, t0, B_QCHUNK, axis=1)
        logit = jnp.einsum('bqhd,bsd->bqhs', iq_c, ik, preferred_element_type=jnp.float32)
        idx_score = jnp.einsum('bqhs,bqh->bqs', jax.nn.relu(logit), iw_c)
        idx_score = jnp.where(key_pos[None, :] <= t_pos[:, None], idx_score, -jnp.inf)
        _, sel = lax.top_k(idx_score, n_keep)
        sel_ok = sel <= t_pos[None, :, None]
        k_g = k[b_ix, sel]
        v_g = v[b_ix, sel]
        qc = lax.dynamic_slice_in_dim(q, t0, B_QCHUNK, axis=1)
        s = jnp.einsum('bqhd,bqkd->bqhk', qc, k_g, preferred_element_type=jnp.float32) * scale
        s = jnp.where(sel_ok[:, :, None, :], s, -jnp.inf)
        p = jax.nn.softmax(s, axis=-1).astype(v.dtype)
        return jnp.einsum('bqhk,bqkd->bqhd', p, v_g)

    outs = lax.map(chunk, jnp.arange(seq // B_QCHUNK))
    return outs.transpose(1, 0, 2, 3, 4).reshape(bsz, seq, nh, hd)

def dilated_group(q, k, v, steps, dil):
    bsz, seq, nh, hd = q.shape
    n_sub = seq // dil
    n_blk = -(-n_sub // C_BLOCK)
    pad = n_blk * C_BLOCK - n_sub

    def to_sub(t):
        t = t.reshape(bsz, n_sub, dil, nh, hd).transpose(0, 2, 3, 1, 4)
        return jnp.pad(t, ((0, 0), (0, 0), (0, 0), (0, pad), (0, 0)))

    def band(t):
        tb = jnp.pad(to_sub(t), ((0, 0), (0, 0), (0, 0), (C_BLOCK, 0), (0, 0)))
        tb = tb.reshape(bsz, dil, nh, n_blk + 1, C_BLOCK, hd)
        return jnp.concatenate([tb[:, :, :, :-1], tb[:, :, :, 1:]], axis=4)

    qs = to_sub(q).reshape(bsz, dil, nh, n_blk, C_BLOCK, hd)
    kw = band(k)
    vw = band(v)
    s = jnp.einsum('brhnqd,brhnkd->brhnqk', qs, kw, preferred_element_type=jnp.float32) * hd ** -0.5
    blk = jnp.arange(n_blk)[:, None, None]
    qi = jnp.arange(C_BLOCK)[None, :, None]
    ki = jnp.arange(2 * C_BLOCK)[None, None, :]
    dist = C_BLOCK + qi - ki
    ok = (dist >= 0) & (dist <= steps) & (blk * C_BLOCK + ki >= C_BLOCK)
    s = jnp.where(ok, s, -jnp.inf)
    lse = jax.nn.logsumexp(s, axis=-1)
    p = jnp.exp(s - lse[..., None]).astype(v.dtype)
    o = jnp.einsum('brhnqk,brhnkd->brhnqd', p, vw)
    o = o.reshape(bsz, dil, nh, n_blk * C_BLOCK, hd)[:, :, :, :n_sub]
    o = o.transpose(0, 3, 1, 2, 4).reshape(bsz, seq, nh, hd)
    lse = lse.reshape(bsz, dil, nh, n_blk * C_BLOCK)[..., :n_sub]
    lse = lse.transpose(0, 3, 1, 2).reshape(bsz, seq, nh)
    return o, lse

def dilated_mixture(q, k, v):
    outs = []
    lses = []
    for g, (window, dil) in enumerate(C_GROUPS):
        sl = slice(g * C_SLOTS, (g + 1) * C_SLOTS)
        o, l = dilated_group(q[:, :, sl], k[:, :, sl], v[:, :, sl], window // dil, dil)
        outs.append(o)
        lses.append(l)
    w = jax.nn.softmax(jnp.stack(lses, axis=0), axis=0)
    return jnp.sum(w[..., None] * jnp.stack(outs, axis=0), axis=0).astype(q.dtype)

def hybrid_layer(x, norm_g, w_in, w_br_a, w_br_b, w_br_c, w_out, cos, sin):
    bsz, seq, _ = x.shape
    h = rmsnorm_2(x, norm_g)
    proj = h @ w_in
    (a_q, a_k, a_v, a_g, b_q, b_k, b_v, b_g, i_q, i_k, i_w,
     c_q, c_k, c_v, c_g, m_g) = jnp.split(proj, IN_OFFSETS, axis=-1)

    def heads(t, n):
        return t.reshape(bsz, seq, n, -1)

    def rope1(t):
        return apply_rope(t[:, :, None, :], cos, sin)[:, :, 0, :]

    ya = moba_attention(apply_rope(heads(a_q, A_HEADS), cos, sin),
                        apply_rope(heads(a_k, A_HEADS), cos, sin),
                        heads(a_v, A_HEADS))
    ya = ya.reshape(bsz, seq, A_WIDTH) * jax.nn.silu(a_g)
    yb = dsa_attention(apply_rope(heads(b_q, B_HEADS), cos, sin), rope1(b_k), b_v,
                       apply_rope(heads(i_q, B_IDX_HEADS), cos, sin), rope1(i_k), i_w)
    yb = yb.reshape(bsz, seq, B_WIDTH) * jax.nn.silu(b_g)
    yc = dilated_mixture(apply_rope(heads(c_q, C_HEADS), cos, sin),
                         apply_rope(heads(c_k, C_HEADS), cos, sin),
                         heads(c_v, C_HEADS))
    yc = yc.reshape(bsz, seq, C_WIDTH) * jax.nn.silu(c_g)
    gates = jax.nn.sigmoid(m_g).reshape(bsz, seq, N_BRANCH, D_MODEL)
    merged = (gates[:, :, 0] * (ya @ w_br_a)
              + gates[:, :, 1] * (yb @ w_br_b)
              + gates[:, :, 2] * (yc @ w_br_c))
    return x + merged @ w_out

def second_inputs(seed: int = 0) -> dict:
    key = jax.random.key(seed)
    ks = jax.random.split(key, 8)
    x = jax.random.normal(ks[0], (BATCH, SEQ, D_MODEL), jnp.float32)
    norm_g = 1.0 + 0.02 * jax.random.normal(ks[1], (DEPTH, D_MODEL), jnp.float32)
    w_in = jax.random.normal(ks[2], (DEPTH, D_MODEL, IN_WIDTH), jnp.float32) * D_MODEL ** -0.5
    w_br_a = jax.random.normal(ks[3], (DEPTH, A_WIDTH, D_MODEL), jnp.float32) * A_WIDTH ** -0.5
    w_br_b = jax.random.normal(ks[4], (DEPTH, B_WIDTH, D_MODEL), jnp.float32) * B_WIDTH ** -0.5
    w_br_c = jax.random.normal(ks[5], (DEPTH, C_WIDTH, D_MODEL), jnp.float32) * C_WIDTH ** -0.5
    w_out = jax.random.normal(ks[6], (DEPTH, D_MODEL, D_MODEL), jnp.float32) * D_MODEL ** -0.5
    final_norm_g = 1.0 + 0.02 * jax.random.normal(ks[7], (D_MODEL,), jnp.float32)
    return {'x': x, 'norm_g': norm_g, 'w_in': w_in, 'w_br_a': w_br_a, 'w_br_b': w_br_b,
            'w_br_c': w_br_c, 'w_out': w_out, 'final_norm_g': final_norm_g}

def second_block(x, norm_g, w_in, w_br_a, w_br_b, w_br_c, w_out, final_norm_g):
    cos, sin = rope_tables(x.shape[1])
    for layer in range(DEPTH):
        x = hybrid_layer(x, norm_g[layer], w_in[layer], w_br_a[layer], w_br_b[layer],
                         w_br_c[layer], w_out[layer], cos, sin)
    return rmsnorm_2(x, final_norm_g)


def setup_inputs(seed=0):
    out = dict(first_inputs(seed))
    for name, value in second_inputs(seed + 1).items():
        if name != "x":
            out[name + "_2"] = value
    return out


def reference(
    x, c, mod_w, mod_b, norm_g, ffn_w_gu, ffn_w_down, sb_w_qkv, sb_w_o, lru_w_in, lru_conv_w,
    lru_conv_b, lru_w_r, lru_b_r, lru_w_i, lru_b_i, lru_lambda, lru_w_out, final_norm_g,
    norm_g_2, w_in_2, w_br_a_2, w_br_b_2, w_br_c_2, w_out_2, final_norm_g_2,
):
    x = first_block(
        x, c, mod_w, mod_b, norm_g, ffn_w_gu, ffn_w_down, sb_w_qkv, sb_w_o, lru_w_in,
        lru_conv_w, lru_conv_b, lru_w_r, lru_b_r, lru_w_i, lru_b_i, lru_lambda, lru_w_out,
        final_norm_g,
    )
    return second_block(
        x, norm_g_2, w_in_2, w_br_a_2, w_br_b_2, w_br_c_2, w_out_2, final_norm_g_2,
    )


_drawn_inputs = setup_inputs


def setup_inputs(seed=0):
    import zlib

    import numpy as np

    out = dict(_drawn_inputs(seed))
    spreads = {}
    factors = {'lru_b_r': 5.628, 'norm_g_2': 5.272, 'final_norm_g_2': 2.808}
    for name, (base, spread) in spreads.items():
        noise = np.random.default_rng([zlib.crc32(name.encode()), seed]).standard_normal(out[name].shape)
        drawn = base * np.exp(spread * noise) if base else spread * noise
        out[name] = jnp.asarray(drawn.astype(out[name].dtype))
    for name, factor in factors.items():
        out[name] = (out[name] * factor).astype(out[name].dtype)
    return out
```

```python
from contextlib import ExitStack

import numpy as np

import concourse.bass as bass
from concourse import mybir

F32 = mybir.dt.float32
F32R = mybir.dt.float32r
ALU = mybir.AluOpType
ACT = mybir.ActivationFunctionType
AX = mybir.AxisListType

P = 128
MASKED = -1.0e30
NOT_CAUSAL = -3.0e38
PICKED = -3.4e38
PICKED_BELOW = -3.2e38


class Operands:

    def matmul(self, *a, **k):
        return lambda e: e.matmul(*a, **k)

    def transpose(self, *a, **k):
        return lambda e: e.transpose(*a, **k)

    def activation(self, *a, **k):
        return lambda e: e.activation(*a, **k)

    def copy(self, *a, **k):
        return lambda e: e.copy(*a, **k)

    def mul(self, *a, **k):
        return lambda e: e.mul(*a, **k)

    def tensor_tensor(self, *a, **k):
        return lambda e: e.tensor_tensor(*a, **k)

    def tensor_scalar(self, *a, **k):
        return lambda e: e.tensor_scalar(*a, **k)

    def scalar_tensor_tensor(self, *a, **k):
        return lambda e: e.scalar_tensor_tensor(*a, **k)

    def tensor_tensor_scan(self, *a, **k):
        return lambda e: e.tensor_tensor_scan(*a, **k)

    def tensor_copy(self, *a, **k):
        return lambda e: e.tensor_copy(*a, **k)

    def tensor_reduce(self, *a, **k):
        return lambda e: e.tensor_reduce(*a, **k)

    def reciprocal(self, *a, **k):
        return lambda e: e.reciprocal(*a, **k)

    def max(self, *a, **k):
        return lambda e: e.max(*a, **k)

    def match_replace(self, *a, **k):
        return lambda e: e.match_replace(*a, **k)

    def memset(self, *a, **k):
        return lambda e: e.memset(*a, **k)

    def affine_select(self, *a, **k):
        return lambda e: e.affine_select(*a, **k)


class Queue:

    def __init__(self, semaphore):
        self.semaphore, self.value, self.items, self.waited = semaphore, 0, [], {}

    def wait(self, after):
        for producer in after:
            if isinstance(producer, list):
                self.wait(producer)
            elif producer is not None:
                sem, value = producer
                if value > self.waited.get(id(sem), 0):
                    self.waited[id(sem)] = value
                    self.items.append(lambda e, sem=sem, value=value: e.wait_ge(sem, value))

    def do(self, make, after=(), signal=True):
        self.wait(after)
        step = make(Operands())
        if not signal:
            self.items.append(step)
            return None
        self.value += 1
        self.items.append(lambda e: step(e).then_inc(self.semaphore, 1))
        return (self.semaphore, self.value)

    def load(self, out, in_, sem, counts, after=()):
        self.wait(after)
        counts[id(sem)] = counts.get(id(sem), 0) + 16
        self.items.append(lambda e: e.dma_start(out, in_).then_inc(sem, 16))
        return (sem, counts[id(sem)])

    def last(self):
        return (self.semaphore, self.value) if self.value else None

    def play(self, engine):
        for item in self.items:
            item(engine)


def build(nc, t, out):
    S, D = t["x"].shape[1:]
    KD = D // P
    NT = S // P
    FF = t["ffn_w_down"].shape[2]
    RNN = t["lru_w_out"].shape[1]
    HD = 64
    PANEL = 2 * P
    RAW = KD * PANEL
    SCALE = HD ** -0.5
    EPS = 1e-6
    TRI = S * (NT + 1) // 2
    ROW_AT = {3: 0, 2: 512, 0: 896, 1: 1024}
    COL_AT = {0: 0, 1: 512, 3: 896, 2: 1024}

    with ExitStack() as ctx:
        def sb(name, shape, dt=F32):
            return ctx.enter_context(nc.sbuf_tensor(name, shape, dt))

        def sem(name):
            return ctx.enter_context(nc.semaphore(name))

        xT = sb("xT", [P, KD, S])
        H = (sb("h_high", [P, KD, S], F32R), sb("h_low", [P, KD, S], F32R))
        Y = (sb("y_high", [P, KD, S], F32R), sb("y_low", [P, KD, S], F32R))
        NRAW, NW = 3, 2
        raw = [sb(f"raw{i}", [P, RAW]) for i in range(NRAW)]
        W = [(sb(f"w_high{i}", [P, RAW], F32R), sb(f"w_low{i}", [P, RAW], F32R)) for i in range(NW)]
        ident = sb("ident", [P, P])
        ones = sb("ones", [P, P])
        neg_tri = sb("neg_tri", [P, P])
        neg_ones = sb("neg_ones", [P, P])
        causal = sb("causal", [P, TRI])
        rope_c = sb("rope_c", [P, S])
        rope_s = sb("rope_s", [P, S])
        mod_acc = sb("mod_acc", [P, D])
        inv = sb("inv", [P, S])
        vec = sb("vec", [P, 336])
        small = sb("small", [P, 96])
        AREA = 13312
        area = sb("area", [P, AREA])
        psum = ctx.enter_context(nc.psum_tensor("psum", [P, 8, 512], F32))
        flat = psum[:, :, :].rearrange("p b c -> p (b c)")

        pe, act, dve, pool, sp = (Queue(sem(f"{n}_done")) for n in ("pe", "act", "dve", "pool", "sp"))
        s_raw = [sem(f"raw_loaded{i}") for i in range(NRAW)]
        s_in, s_tab, s_swap, s_out, s_gate_w = sem("x_loaded"), sem("tables_loaded"), sem("swapped"), sem("stored"), sem("gate_w_loaded")
        s_dup = sem("copied_half")
        counts = {}
        state = {}

        def fence():
            return [q.last() for q in (pe, act, dve, pool)]

        class Carver:

            def __init__(self):
                self.at = 0

            def new(self, *shape):
                n = int(np.prod(shape))
                assert self.at + n <= AREA, (self.at, n)
                a = area[:, self.at:self.at + n]
                self.at += n
                if len(shape) == 2:
                    a = a.rearrange("p (a b) -> p a b", a=shape[0])
                if len(shape) == 3:
                    a = a.rearrange("p (a b c) -> p a b c", a=shape[0], b=shape[1])
                return a

        groups = [
            [("c", KD), ("norm_g", 6 * KD), ("final_norm_g", KD), ("norm_g_2", 2 * KD), ("final_norm_g_2", KD)],
            [("mod_b", 9 * KD)],
            [("mod_b", 9 * KD)],
            [("lru_conv_w", 4 * RNN // P), ("lru_conv_b", RNN // P), ("lru_b_r", RNN // P),
             ("lru_b_i", RNN // P), ("lru_lambda", RNN // P)],
        ]
        col = {}
        at = 0
        for g, names in enumerate(groups):
            for name, n in names:
                col[f"{name}{g - 1 if name == 'mod_b' else ''}"] = at
                at += n
        col["c_act"] = at
        col["decay"] = at + KD
        assert col["decay"] + RNN // P <= 336
        mods = [sb(f"mod{i}", [P, 9 * KD]) for i in range(2)]

        def v(name, i=0, n=1):
            return vec[:, col[name] + i:col[name] + i + n]

        bank_free = [[] for _ in range(8)]
        pairs = [0]

        def take_pair():
            b = 2 * (pairs[0] % 4)
            pairs[0] += 1
            return b, [bank_free[b], bank_free[b + 1]]

        class Stream:

            def __init__(self, plan, mod_plan, lead):
                self.asked = []
                self.plan = None
                if plan is not None:
                    merged, rest = list(mod_plan[:lead]), list(mod_plan[lead:])
                    for k in plan:
                        merged.append(("w", k))
                        if rest:
                            merged.append(rest.pop(0))
                    self.plan = merged
                self.loaded = self.split = 0
                self.raw_free = [None] * NRAW
                self.w_free = [None] * NW
                self.n_split = 0
                self.n_taken = 0
                self.ready = {}
                self.raw_ready = {}

            def load_next(self):
                if self.loaded >= len(self.plan):
                    return
                kind, pieces = self.plan[self.loaded]
                s = self.loaded % NRAW
                for off, n, k, src in pieces:
                    dst = raw[s][:, off:off + n].rearrange("p (k n) -> p k n", k=k)
                    tok = sp.load(dst, src, s_raw[s], counts, after=[self.raw_free[s]])
                self.raw_ready[self.loaded] = tok
                self.loaded += 1

            def split_next(self):
                while self.split < len(self.plan):
                    i = self.split
                    while self.loaded <= i:
                        self.load_next()
                    kind, pieces = self.plan[i]
                    s = i % NRAW
                    self.split += 1
                    got = self.raw_ready.pop(i)
                    if kind == "w":
                        n = sum(p[1] for p in pieces)
                        w = self.n_split % NW
                        high, low = W[w]
                        th = act.do(lambda e: e.copy(high[:, :n], raw[s][:, :n]), after=[got, self.w_free[w]])
                        tl = dve.do(lambda e: e.tensor_tensor(low[:, :n], raw[s][:, :n], high[:, :n].bitcast(F32), ALU.subtract),
                                    after=[th])
                        self.raw_free[s] = tl
                        self.ready[self.n_split] = (w, [th, tl])
                        self.n_split += 1
                        self.load_next()
                        return
                    self.mod_step(kind, s, got)
                    self.load_next()

            def mod_step(self, kind, s, got):
                _, layer, sub, part, kp = kind
                for k in range(2):
                    w = raw[s][:, k * D:(k + 1) * D]
                    c = v("c_act", 2 * kp + k)
                    if kp == 0 and k == 0:
                        tok = dve.do(lambda e: e.tensor_scalar(mod_acc[:, :], w, c, None, ALU.mult),
                                     after=[got, state["c_act"], state.get("mod_read")])
                    else:
                        tok = dve.do(lambda e: e.scalar_tensor_tensor(mod_acc[:, :], w, c, mod_acc[:, :], ALU.mult, ALU.add),
                                     after=[got, dve.last()])
                self.raw_free[s] = tok
                if kp == KD // 2 - 1:
                    b, free = take_pair()
                    for j in range(KD):
                        tp = pe.do(lambda e, j=j: e.matmul(psum[:, b, j:j + 1], mod_acc[:, j * P:(j + 1) * P], ones[:, 0:1],
                                                           start=True, stop=True), after=[tok, free, state["consts"]], signal=j == KD - 1)
                    state["mod_read"] = tp
                    o = (3 * sub + part) * KD
                    td = dve.do(lambda e: e.tensor_tensor(mods[layer][:, o:o + KD], psum[:, b, 0:KD], v(f"mod_b{layer}", o, KD), ALU.add),
                                after=[tp, state["vec"]])
                    bank_free[b] = [td]
                    state[("mod", layer, sub, part)] = td

            def take(self, pieces):
                if self.plan is None:
                    self.asked.append(pieces)
                    i = self.n_taken
                    self.n_taken += 1
                    return W[0], [], lambda tok: None
                i = self.n_taken
                self.n_taken += 1
                while self.n_split <= i:
                    self.split_next()
                if self.n_split == i + 1 and i > 0:
                    self.split_next()
                w, toks = self.ready.pop(i)

                def done(tok):
                    self.w_free[w] = tok
                return W[w], toks, done

        def piece(src, k, off=0):
            n = src.shape[1] * k
            return (off, n, k, src.rearrange("(k p) n -> p k n", p=P))

        def mod_panels():
            plan = []
            for layer in range(2):
                for sub in range(3):
                    for part in range(3):
                        for kp in range(KD // 2):
                            c0 = (3 * sub + part) * D
                            src = t["mod_w"][layer, 2 * kp * P:(2 * kp + 2) * P, c0:c0 + D]
                            plan.append((("m", layer, sub, part, kp), [piece(src, 2)]))
            return plan

        def product(X, ready, src_pieces, ks, n, free, widths=(P, P), base=None, first=True, last=True):
            (wh, wl), wt, done = stream.take(src_pieces)
            if base is None:
                base, free = take_pair()
            wv = [w[:, :len(ks) * n].rearrange("p (k n) -> p k n", n=n) for w in (wh, wl)]
            combos = ((0, 0), (0, 1), (1, 0))
            for i, k in enumerate(ks):
                c0 = 0
                for m, width in enumerate(widths):
                    for a, b in combos:
                        end = i == len(ks) - 1 and m == len(widths) - 1 and (a, b) == combos[-1]
                        tok = pe.do(lambda e, i=i, k=k, m=m, a=a, b=b, c0=c0, width=width: e.matmul(
                            psum[0:width, base + m, :], wv[a][:, i, c0:c0 + width], X[b][:, k, :],
                            start=(i == 0 and (a, b) == (0, 0)), stop=(i == len(ks) - 1 and (a, b) == combos[-1])),
                            after=[wt, ready[k], free], signal=end)
                    c0 += width
            done(tok)
            return base, tok

        def product_tok(X, ready, src_pieces, n):
            (wh, wl), wt, done = stream.take(src_pieces)
            base, free = take_pair()
            wv = [w[:, :KD * n].rearrange("p (k n) -> p k n", n=n) for w in (wh, wl)]
            for tt in range(NT):
                for k in range(KD):
                    for a, b in ((0, 0), (0, 1), (1, 0)):
                        end = tt == NT - 1 and k == KD - 1 and (a, b) == (1, 0)
                        o = (base + tt // 2) * 512 + (tt % 2) * PANEL
                        tok = pe.do(lambda e, tt=tt, k=k, a=a, b=b, o=o: e.matmul(
                            flat[:, o:o + n], X[b][:, k, tt * P:(tt + 1) * P], wv[a][:, k, :],
                            start=(k == 0 and (a, b) == (0, 0)), stop=(k == KD - 1 and (a, b) == (1, 0))),
                            after=[wt, ready[k], free], signal=end)
            done(tok)
            view = flat[:, base * 512:(base + 2) * 512].rearrange("p (t c) -> p t c", c=PANEL)[:, :, :n]
            return base, view, tok

        def free_pair(base, toks):
            bank_free[base] = bank_free[base + 1] = list(toks)

        def norm(x_ready, dst, gain, shift=None, old_reads=(), split=True):
            f = fence()
            c = Carver()
            sq = c.new(2, S)
            ssum = c.new(S)
            tmp = c.new(2, S)
            used = [None, None]
            tsum = None
            for j in range(KD):
                if j == 0:
                    tsum = act.do(lambda e: e.activation(ssum, xT[:, 0, :], ACT.Square), after=[x_ready[0], f])
                    continue
                ts = act.do(lambda e, j=j: e.activation(sq[:, j % 2, :], xT[:, j, :], ACT.Square),
                            after=[x_ready[j], f, used[j % 2]])
                eng = pool if j % 2 else dve
                tsum = eng.do(lambda e, j=j: e.tensor_tensor(ssum, ssum, sq[:, j % 2, :], ALU.add), after=[ts, tsum])
                used[j % 2] = tsum
            b, free = take_pair()
            tp = pe.do(lambda e: e.matmul(psum[:, b, :], ones[:, :], ssum, start=True, stop=True), after=[tsum, free])
            tr = act.do(lambda e: e.activation(inv[:, :], psum[:, b, :], ACT.Sqrt, bias=small[:, 0:1], scale=1.0 / D),
                        after=[tp, state["consts"], f])
            mean = sq[:, 0, :]
            tv = dve.do(lambda e: e.tensor_scalar(mean, psum[:, b, :], 1.0 / D, EPS, ALU.mult, ALU.add), after=[tr, tsum])
            free_pair(b, [tr, tv])
            y2 = sq[:, 1, :]
            ti = dve.do(lambda e: e.reciprocal(inv[:, :], inv[:, :]), after=[tr])
            ti = dve.do(lambda e: e.tensor_tensor(y2, inv[:, :], inv[:, :], ALU.mult), after=[ti, tsum])
            ti = dve.do(lambda e: e.scalar_tensor_tensor(y2, y2, -0.5, mean, ALU.mult, ALU.mult), after=[ti, tv])
            ti = dve.do(lambda e: e.scalar_tensor_tensor(inv[:, :], y2, 1.5, inv[:, :], ALU.add, ALU.mult), after=[ti])
            toks = []
            used = [None, None]
            for j in range(KD):
                if not split:
                    toks.append([dve.do(lambda e, j=j: e.scalar_tensor_tensor(dst[:, j, :], xT[:, j, :], gain(j), inv[:, :], ALU.mult, ALU.mult),
                                        after=[ti, x_ready[j], tsum, f])])
                    continue
                s = j % 2
                td = dve.do(lambda e, j=j, s=s: e.scalar_tensor_tensor(tmp[:, s, :], xT[:, j, :], gain(j), inv[:, :], ALU.mult, ALU.mult),
                            after=[ti, used[s], f, state.get("gain")])
                high, low = dst
                if shift is None:
                    th = act.do(lambda e, j=j, s=s: e.copy(high[:, j, :], tmp[:, s, :]), after=[td, old_reads])
                    tl = dve.do(lambda e, j=j, s=s: e.tensor_tensor(low[:, j, :], tmp[:, s, :], high[:, j, :].bitcast(F32), ALU.subtract),
                                after=[th, td, old_reads])
                else:
                    th = act.do(lambda e, j=j, s=s: e.activation(high[:, j, :], tmp[:, s, :], ACT.Identity, bias=shift(j)), after=[td, old_reads])
                    tl = dve.do(lambda e, j=j, s=s: e.scalar_tensor_tensor(low[:, j, :], tmp[:, s, :], shift(j), high[:, j, :].bitcast(F32),
                                                                           ALU.add, ALU.subtract), after=[th, td, old_reads])
                used[s] = tl
                toks.append([th, tl])
            return toks

        def split_into(X, j, src, after, old_reads, parts=slice(0, P)):
            th = act.do(lambda e: e.copy(X[0][parts, j, :], src), after=[after, old_reads])
            tl = dve.do(lambda e: e.tensor_tensor(X[1][parts, j, :], src, X[0][parts, j, :].bitcast(F32), ALU.subtract),
                        after=[th, after, old_reads])
            return [th, tl]

        gs = sb("gain_in", [P, KD])
        gg = sb("gain_out", [P, KD])

        def gains(layer, sub, weight):
            m = mods[layer]
            o = 3 * sub * KD
            need = [state.get(("mod", layer, sub, part)) for part in range(3)]
            t1 = dve.do(lambda e: e.scalar_tensor_tensor(gs[:, :], m[:, o + KD:o + 2 * KD], 1.0, v("norm_g", (3 * layer + sub) * KD, KD),
                                                         ALU.add, ALU.mult), after=[need, state["vec"], fence()])
            t2 = dve.do(lambda e: e.tensor_scalar(gg[:, :], m[:, o + 2 * KD:o + 3 * KD], 1.0, weight, ALU.add, ALU.mult), after=[need, t1])
            state["gain"] = t2
            return (lambda j: gs[:, j:j + 1]), (lambda j: m[:, o + j:o + j + 1]), (lambda j: gg[:, j:j + 1])

        def add_to_x(base, tok, j0, gate, x_ready):
            toks = []
            for m in range(2):
                j = j0 + m
                if gate is None:
                    td = dve.do(lambda e, m=m, j=j: e.tensor_tensor(xT[:, j, :], xT[:, j, :], psum[:, base + m, :], ALU.add),
                                after=[tok, x_ready[j]])
                else:
                    td = dve.do(lambda e, m=m, j=j: e.scalar_tensor_tensor(xT[:, j, :], psum[:, base + m, :], gate(j), xT[:, j, :],
                                                                           ALU.mult, ALU.add), after=[tok, x_ready[j]])
                x_ready[j] = [td]
                toks.append(td)
            free_pair(base, toks)

        def project_back(X, ready, w, row0, nk, gate, x_ready):
            for c in range(D // PANEL):
                src = w[row0:row0 + nk * P, c * PANEL:(c + 1) * PANEL]
                base, tok = product(X, ready, [piece(src, nk)], range(nk), PANEL, None)
                add_to_x(base, tok, 2 * c, gate, x_ready)
            return tok

        def ffn(layer, which, sub, x_ready):
            gain, shift, gate = gains(layer, sub, 0.5)
            hr = norm(x_ready, H, gain, shift, old_reads=fence())
            w_gu, w_down = t["ffn_w_gu"][layer, which], t["ffn_w_down"][layer, which]
            f = fence()
            c = Carver()
            c.at = 5 * S
            sil = [c.new(S) for _ in range(4)]
            prod = [c.new(S) for _ in range(4)]
            sil_free, prod_free = [None] * 4, [None] * 4
            n = 0
            y_reads = f
            for row in range(0, FF // P, KD):
                nk = min(KD, FF // P - row)
                yr = []
                for c0 in range(row, row + nk, 2):
                    bg, tg = product(H, hr, [piece(w_gu[:, c0 * P:c0 * P + PANEL], KD)], range(KD), PANEL, None)
                    bu, tu = product(H, hr, [piece(w_gu[:, FF + c0 * P:FF + c0 * P + PANEL], KD)], range(KD), PANEL, None)
                    gt, ut = [], []
                    for m in range(2):
                        s = n % 4
                        n += 1
                        a1 = act.do(lambda e, m=m, s=s: e.activation(sil[s], psum[:, bg + m, :], ACT.Silu), after=[tg, sil_free[s], f])
                        d1 = dve.do(lambda e, m=m, s=s: e.tensor_tensor(prod[s], sil[s], psum[:, bu + m, :], ALU.mult),
                                    after=[a1, tu, prod_free[s], f])
                        sil_free[s] = d1
                        both = split_into(Y, c0 - row + m, prod[s], d1, y_reads)
                        prod_free[s] = both
                        gt.append(a1)
                        ut.append(d1)
                        yr.append(both)
                    free_pair(bg, gt)
                    free_pair(bu, ut)
                y_reads = [project_back(Y, yr, w_down, row * P, nk, gate, x_ready)]

        def stick_breaking(x_ready):
            gain, shift, gate = gains(0, 1, 1.0)
            hr = norm(x_ready, H, gain, shift, old_reads=fence())
            w_qkv, w_o = t["sb_w_qkv"][0], t["sb_w_o"][0]
            G = 4
            f = fence()
            c = Carver()
            c.at = 0
            q, k, vv = c.new(G, S), c.new(G, S), c.new(NT, G * P)
            tmp = [c.new(TRI) for _ in range(2)]
            sp_ = [c.new(TRI) for _ in range(2)]
            yr = [None] * KD
            for g in range(KD // G):
                f = fence()
                ready = {}
                for part, dst in ((0, q), (1, k)):
                    for c0 in range(0, G, 2):
                        src = w_qkv[:, part * D + (g * G + c0) * P:part * D + (g * G + c0) * P + PANEL]
                        base, tok = product(H, hr, [piece(src, KD)], range(KD), PANEL, None)
                        ta = act.do(lambda e, dst=dst, c0=c0, base=base, part=part: e.mul(dst[:, c0:c0 + 2, :], psum[:, base:base + 2, :],
                                                                                      SCALE if part == 0 else 1.0), after=[tok, f])
                        free_pair(base, [ta])
                        ready[part, c0] = ready[part, c0 + 1] = ta
                for c0 in range(0, G, 2):
                    src = w_qkv[:, 2 * D + (g * G + c0) * P:2 * D + (g * G + c0) * P + PANEL]
                    base, view, tok = product_tok(H, hr, [piece(src, KD)], PANEL)
                    ta = act.do(lambda e, c0=c0, view=view: e.copy(vv[:, :, c0 * P:c0 * P + PANEL], view), after=[tok, f])
                    free_pair(base, [ta])
                    ready[2, c0] = ready[2, c0 + 1] = ta
                zfree = [f, f]
                tmp_free, sp_free = [f, f], [f, f]
                o_free = {6: bank_free[6], 7: bank_free[7]}
                for b in range(8):
                    zfree = [zfree[0], zfree[1]] + []
                banks_before = [bank_free[b] for b in range(8)]
                st = {}

                def scores(h):
                    s, ti, r0 = h % 2, h // 2, (h % 2) * HD
                    for i in range(NT):
                        tz = pe.do(lambda e, i=i: e.matmul(
                            flat[:, s * 1536 + COL_AT[i]:s * 1536 + COL_AT[i] + S - P * i],
                            k[r0:r0 + HD, ti, i * P:(i + 1) * P], q[r0:r0 + HD, ti, i * P:S],
                            start=(i != 3), stop=True, skip_group_check=True),
                            after=[zfree[s], banks_before, ready[0, ti], ready[1, ti]], signal=i == NT - 1)
                    z = flat[:, s * 1536:s * 1536 + TRI]
                    a0 = act.do(lambda e: e.activation(tmp[s], z, ACT.Abs), after=[tz, tmp_free[s]])
                    a1 = act.do(lambda e: e.activation(tmp[s], tmp[s], ACT.Exp, scale=-1.0), after=[a0])
                    a2 = act.do(lambda e: e.activation(tmp[s], tmp[s], ACT.Ln, bias=1.0), after=[a1])
                    d2 = dve.do(lambda e: e.scalar_tensor_tensor(sp_[s], z, 0.0, tmp[s], ALU.max, ALU.add), after=[a2, tz, sp_free[s]])
                    for i in range(NT):
                        blk = sp_[s][:, COL_AT[i]:COL_AT[i] + P]
                        tm = pool.do(lambda e, blk=blk: e.affine_select(out=blk, in_=blk, pattern=[[1, P]], compare_op=ALU.is_gt, fill=0.0,
                                                                        base=0, channel_multiplier=-1), after=[d2])
                    st[h] = (tm, d2)

                def weigh(h):
                    s, ti, r0 = h % 2, h // 2, (h % 2) * HD
                    tm, d2 = st[h]
                    for i in range(NT):
                        for j in range(i, NT):
                            o = s * 1536 + COL_AT[i] + P * (j - i)
                            tc = pe.do(lambda e, i=i, j=j, o=o: e.matmul(
                                flat[:, o:o + S - P * j], neg_tri[:, :] if i == j else neg_ones[:, :],
                                sp_[s][:, COL_AT[j]:COL_AT[j] + S - P * j], start=False, stop=True, skip_group_check=True),
                                after=[tm, d2], signal=(i, j) == (NT - 1, NT - 1))
                    sp_free[s] = tc
                    a1 = act.do(lambda e: e.activation(tmp[s], flat[:, s * 1536:s * 1536 + TRI], ACT.Exp), after=[tc, d2])
                    zfree[s] = a1
                    for i in range(NT):
                        blk = tmp[s][:, COL_AT[i]:COL_AT[i] + P]
                        tm = pool.do(lambda e, blk=blk: e.affine_select(out=blk, in_=blk, pattern=[[1, P]], compare_op=ALU.is_gt, fill=0.0,
                                                                        base=0, channel_multiplier=-1), after=[a1])
                    ob = 6 + ti % 2
                    for i in range(NT):
                        to = pe.do(lambda e, i=i: e.matmul(
                            psum[r0:r0 + HD, ob, i * P:S], vv[:, i, ti * P + r0:ti * P + r0 + HD], tmp[s][:, COL_AT[i]:COL_AT[i] + S - P * i],
                            start=(i == 0), stop=(i == NT - 1), skip_group_check=True), after=[tm, a1, ready[2, ti], o_free[ob]], signal=i == NT - 1)
                    tmp_free[s] = to
                    if h % 2:
                        yr[g * G + ti] = split_into(Y, g * G + ti, psum[:, ob, :], to, f)
                        o_free[ob] = yr[g * G + ti]

                scores(0)
                for h in range(2 * G):
                    if h + 1 < 2 * G:
                        scores(h + 1)
                    weigh(h)
                end = fence()
                for b in range(8):
                    bank_free[b] = end
            project_back(Y, yr, w_o, 0, KD, gate, x_ready)

        def rglru(x_ready):
            gain, shift, gate = gains(1, 1, 1.0)
            hr = norm(x_ready, H, gain, shift, old_reads=fence())
            w_in, w_out = t["lru_w_in"][0], t["lru_w_out"][0]
            NB = RNN // P
            f = fence()
            c = Carver()
            c.at = 5 * S
            w_r, w_i = c.new(NB, P), c.new(NB, P)
            gel, xc, rr, ii, aa, th = (c.new(2, S) for _ in range(6))
            xpad = c.new(2, S + 3)
            sp.load(w_r, t["lru_w_r"][0].rearrange("n k j -> k n j"), s_gate_w, counts, after=[f])
            tw = sp.load(w_i, t["lru_w_i"][0].rearrange("n k j -> k n j"), s_gate_w, counts, after=[f])
            tz = dve.do(lambda e: e.memset(xpad[:, :, 0:3], 0.0), after=[f])
            y_reads = f
            free = {}
            for part0 in range(0, NB, KD):
                nk = min(KD, NB - part0)
                yr = []
                for n0 in range(part0, part0 + nk, 2):
                    base, tok = product(H, hr, [piece(w_in[:, n0 * P:n0 * P + PANEL], KD)], range(KD), PANEL, None)
                    tg = act.do(lambda e, base=base: e.activation(gel, psum[:, base:base + 2, :], ACT.Gelu_apprx_tanh),
                                after=[tok, f, free.get("gel")])
                    free_pair(base, [tg])
                    base, tok = product(H, hr, [piece(w_in[:, RNN + n0 * P:RNN + n0 * P + PANEL], KD)], range(KD), PANEL, None)
                    tx = act.do(lambda e, base=base: e.copy(xpad[:, :, 3:S + 3], psum[:, base:base + 2, :]), after=[tok, f, free.get("xpad")])
                    free_pair(base, [tx])
                    br, fr = take_pair()
                    bi, fi = take_pair()
                    tr, ts = [], []
                    for m in range(2):
                        n = n0 + m
                        td = dve.do(lambda e, m=m, n=n: e.tensor_scalar(xc[:, m, :], xpad[:, m, 0:S], v("lru_conv_w", n), v("lru_conv_b", n),
                                                                        ALU.mult, ALU.add), after=[tx, tz, free.get("xc")])
                        for tap in range(1, 4):
                            td = dve.do(lambda e, m=m, n=n, tap=tap: e.scalar_tensor_tensor(
                                xc[:, m, :], xpad[:, m, tap:tap + S], v("lru_conv_w", tap * NB + n), xc[:, m, :], ALU.mult, ALU.add), after=[td])
                        tr.append(pe.do(lambda e, m=m, n=n: e.matmul(psum[:, br + m, :], w_r[:, n, :], xc[:, m, :], start=True, stop=True),
                                        after=[td, tw, fr]))
                        ts.append(pe.do(lambda e, m=m, n=n: e.matmul(psum[:, bi + m, :], w_i[:, n, :], xc[:, m, :], start=True, stop=True),
                                        after=[td, tw, fi]))
                    free["xpad"] = td
                    sig = []
                    for m in range(2):
                        n = n0 + m
                        s1 = act.do(lambda e, m=m, n=n: e.activation(rr[:, m, :], psum[:, br + m, :], ACT.Sigmoid, bias=v("lru_b_r", n)),
                                    after=[tr[m], free.get("rr")])
                        s2 = act.do(lambda e, m=m, n=n: e.activation(ii[:, m, :], psum[:, bi + m, :], ACT.Sigmoid, bias=v("lru_b_i", n)),
                                    after=[ts[m], free.get("ii")])
                        sig.append((s1, s2))
                    free_pair(br, [s1])
                    free_pair(bi, [s2])
                    e2 = []
                    for m in range(2):
                        n = n0 + m
                        a1 = act.do(lambda e, m=m, n=n: e.activation(aa[:, m, :], rr[:, m, :], ACT.Exp, scale=v("decay", n)),
                                    after=[sig[m][0], state["decay"], free.get("aa")])
                        a2 = act.do(lambda e, m=m, n=n: e.activation(th[:, m, :], rr[:, m, :], ACT.Tanh, scale=v("decay", n)),
                                    after=[sig[m][0], free.get("th")])
                        e2.append((a1, a2))
                    d1 = dve.do(lambda e: e.tensor_tensor(rr, aa, aa, ALU.mult), after=[e2[0][0], e2[1][0], e2[1][1]])
                    d2 = dve.do(lambda e: e.scalar_tensor_tensor(th, rr, 1.0, th, ALU.add, ALU.mult), after=[d1, e2[1][1]])
                    a3 = act.do(lambda e: e.activation(th, th, ACT.Sqrt, scale=-1.0), after=[d2])
                    p1 = pool.do(lambda e: e.tensor_tensor(ii, ii, xc, ALU.mult), after=[sig[1][1], td])
                    free["xc"] = [p1, ts[1]]
                    d3 = dve.do(lambda e: e.tensor_tensor(ii, ii, th, ALU.mult), after=[p1, a3])
                    for m in range(2):
                        d4 = dve.do(lambda e, m=m: e.tensor_tensor_scan(rr[:, m, :], aa[:, m, :], ii[:, m, :], 0.0, ALU.mult, ALU.add), after=[d3])
                    free["aa"] = d4
                    free["th"] = d3
                    free["ii"] = d4
                    d5 = dve.do(lambda e: e.tensor_tensor(rr, rr, gel, ALU.mult), after=[d4, tg])
                    free["gel"] = d5
                    for m in range(2):
                        both = split_into(Y, n0 - part0 + m, rr[:, m, :], d5, y_reads)
                        yr.append(both)
                    free["rr"] = both
                y_reads = [project_back(Y, yr, w_out, part0 * P, nk, gate, x_ready)]

        IN = {}
        off = 0
        for name, n in (("a_q", 384), ("a_k", 384), ("a_v", 384), ("a_g", 384), ("b_q", 384), ("b_k", 64), ("b_v", 64), ("b_g", 384),
                        ("i_q", 256), ("i_k", 64), ("i_w", 4), ("c_q", 768), ("c_k", 768), ("c_v", 768), ("c_g", 256), ("m_g", 3 * D)):
            IN[name] = off
            off += n

        def hybrid(layer, x_ready):
            hr = norm(x_ready, H, lambda j: v("norm_g_2", layer * KD + j), old_reads=fence())
            w_in = t["w_in_2"][layer]
            c = Carver()
            rope_x, rope_y = c.new(2, S), c.new(2, S)
            SS = [c.new(TRI) for _ in range(2)]
            PT = c.new(TRI)
            maskc = c.new(7 * P)
            stat = c.new(32)
            keep = c.at

            rope_free = {"x": fence(), "y": fence()}

            def columns(name, c0, n, widths):
                o = IN[name] + c0
                return product(H, hr, [piece(w_in[:, o:o + n], KD)], range(KD), n, None, widths)

            def rope(base, tok, dst, parts=P, n=2, after=(), dil=1):
                ta = act.do(lambda e: e.copy(rope_x[0:parts, 0:n, :], psum[0:parts, base:base + n, :]), after=[tok, rope_free["x"]])
                for r in range(0, parts, 64):
                    for a, b in ((r, r + 32), (r + 32, r)):
                        tswap = sp.load(rope_y[a:a + 32, 0:n, :], rope_x[b:b + 32, 0:n, :], s_swap, counts, after=[ta, rope_free["y"]])

                def split_tokens(ap):
                    return ap if dil == 1 else ap.rearrange("p (j r) -> p j r", r=dil)

                def to(m):
                    a = dst[0:parts, m, :]
                    return a if dil == 1 else a.rearrange("p (r j) -> p j r", r=dil)
                for m in range(n):
                    eng = pool if m == 0 else dve
                    t1 = eng.do(lambda e, m=m: e.tensor_tensor(to(m), split_tokens(rope_x[0:parts, m, :]), split_tokens(rope_c[0:parts, :]), ALU.mult),
                                after=[ta, tswap, after])
                    t2 = dve.do(lambda e, m=m: e.tensor_tensor(rope_y[0:parts, m, :], rope_y[0:parts, m, :], rope_s[0:parts, :], ALU.mult),
                                after=[tswap])
                    t3 = dve.do(lambda e, m=m: e.tensor_tensor(to(m), to(m), split_tokens(rope_y[0:parts, m, :]), ALU.add),
                                after=[t1, t2])
                rope_free["x"] = [t1, t3, tswap]
                rope_free["y"] = t3
                return [ta, t3]

            def roped(name, c0, n, widths, dst, after, dil=1):
                base, tok = columns(name, c0, n, widths)
                r = rope(base, tok, dst, n=len(widths), after=after, dil=dil)
                free_pair(base, [r[0]])
                return r[1]

            def token_major(name, c0, n, dst, after):
                o = IN[name] + c0
                base, view, tok = product_tok(H, hr, [piece(w_in[:, o:o + n], KD)], n)
                ta = act.do(lambda e: e.copy(dst, view), after=[tok, after])
                free_pair(base, [ta])
                return ta

            def gate_tiles(name, c0, n, dst, after):
                widths = (P,) * (n // P)
                base, tok = columns(name, c0, n, widths)
                m = len(widths)
                ta = act.do(lambda e: e.activation(dst[:, 0:m, :], psum[:, base:base + m, :], ACT.Sigmoid), after=[tok, after])
                td = dve.do(lambda e: e.tensor_tensor(dst[:, 0:m, :], dst[:, 0:m, :], psum[:, base:base + m, :], ALU.mult), after=[ta])
                free_pair(base, [td])
                return td

            def softmax_heads(heads):
                begin = fence()
                banks = [list(x) for x in bank_free]
                s_free = [begin, begin]
                read_scores = [begin]
                pt_free = [begin]
                st = {}

                def first(h):
                    scores, lo, hi, mask, rows, turns, outs, finish = heads[h]
                    s = h % 2
                    buf = SS[s]
                    tp = scores([read_scores[0], banks])
                    d = dve.do(lambda e: e.scalar_tensor_tensor(buf[:, lo:hi], flat[:, lo:hi], SCALE, mask[0], ALU.mult, ALU.add),
                               after=[tp, s_free[s], mask[1]])
                    read_scores[0] = d
                    m0 = 16 * s
                    for i, (a, b, n) in enumerate(rows):
                        dm = dve.do(lambda e, a=a, b=b, n=n, i=i: e.tensor_reduce(stat[:, m0 + i:m0 + i + n], buf[:, a:b].rearrange("p (n c) -> p n c", n=n),
                                                                                AX.X, ALU.max), after=[d, s_free[s]])
                    i_n = sum(n for _, _, n in rows)
                    nr = 0
                    dn = dve.do(lambda e: e.tensor_scalar(stat[:, m0 + 4:m0 + 4 + 4], stat[:, m0:m0 + 4], -1.0, None, ALU.mult), after=[dm, s_free[s]])
                    w = 0
                    for (a, b, n) in rows:
                        step = (b - a) // n
                        for u in range(n):
                            ta = act.do(lambda e, a=a, u=u, step=step, w=w: e.activation(
                                buf[:, a + u * step:a + (u + 1) * step], buf[:, a + u * step:a + (u + 1) * step], ACT.Exp,
                                bias=stat[:, m0 + 4 + w:m0 + 5 + w], accum_out=stat[:, m0 + 8 + w:m0 + 9 + w]), after=[dn])
                            w += 1
                    dr = dve.do(lambda e: e.reciprocal(stat[:, m0 + 12:m0 + 16], stat[:, m0 + 8:m0 + 12]), after=[ta, s_free[s]])
                    w = 0
                    for (a, b, n) in rows:
                        step = (b - a) // n
                        for u in range(n):
                            dn = dve.do(lambda e, a=a, u=u, step=step, w=w: e.tensor_scalar(
                                buf[:, a + u * step:a + (u + 1) * step], buf[:, a + u * step:a + (u + 1) * step],
                                stat[:, m0 + 12 + w:m0 + 13 + w], None, ALU.mult), after=[dr])
                            w += 1
                    st[h] = dn

                def second(h):
                    scores, lo, hi, mask, rows, turns, outs, finish = heads[h]
                    s = h % 2
                    buf = SS[s]
                    dn = st[h]
                    for i, (src, dst) in enumerate(turns):
                        tt = pe.do(lambda e, src=src, dst=dst: e.transpose(flat[:, 1536 + dst:1536 + dst + P], buf[:, src:src + P], ident[:, :]),
                                   after=[dn, pt_free[0]], signal=i == len(turns) - 1)
                    top = max(d for _, d in turns) + P
                    ta = act.do(lambda e: e.copy(PT[:, 0:top], flat[:, 1536:1536 + top]), after=[tt, pt_free[0]])
                    to = outs(ta)
                    pt_free[0] = to
                    s_free[s] = [tt, finish(s, to)]

                first(0)
                for h in range(len(heads)):
                    if h + 1 < len(heads):
                        first(h + 1)
                    second(h)
                end = fence()
                for b in range(8):
                    bank_free[b] = end

            yr = [None] * KD
            y_old = fence()
            RNG = {n: (ROW_AT[n], ROW_AT[n] + P * (n + 1)) for n in range(NT)}
            ROWS = [(ROW_AT[n], ROW_AT[n] + P * (n + 1), 1) for n in (0, 1, 2, 3)]
            TURNS = [(ROW_AT[n] + P * kt, COL_AT[kt] + P * (n - kt)) for kt in (0, 1, 3, 2) for n in range(kt, NT)]

            def causal_heads(y0, q, k_of, v_of, n_heads, mask, ready, gates):
                heads = []
                o_free = {6: [], 7: []}
                for h in range(n_heads):
                    ti, r0 = h // 2, (h % 2) * HD
                    ob = 6 + ti % 2

                    def scores(after, ti=ti, r0=r0, h=h):
                        for n in range(NT):
                            tok = pe.do(lambda e, n=n: e.matmul(flat[:, ROW_AT[n]:ROW_AT[n] + P * (n + 1)], q[r0:r0 + HD, ti, n * P:(n + 1) * P],
                                                                k_of(h)[:, 0:P * (n + 1)], start=True, stop=True),
                                        after=[after, ready], signal=n == NT - 1)
                        return tok

                    def outs(ta, ti=ti, r0=r0, h=h, ob=ob):
                        for kt in range(NT):
                            tok = pe.do(lambda e, kt=kt: e.matmul(psum[r0:r0 + HD, ob, kt * P:S], v_of(h, kt),
                                                                  PT[:, COL_AT[kt]:COL_AT[kt] + S - P * kt], start=kt == 0, stop=kt == NT - 1,
                                                                  skip_group_check=True),
                                        after=[ta, ready, o_free[ob]], signal=kt == NT - 1)
                        return tok

                    def finish(s, to, ti=ti, h=h, ob=ob):
                        if h % 2 == 0:
                            return None
                        d = dve.do(lambda e: e.tensor_tensor(gates[:, ti, :], gates[:, ti, :], psum[:, ob, :], ALU.mult), after=[to, ready])
                        o_free[ob] = [d]
                        yr[y0 + ti] = split_into(Y, y0 + ti, gates[:, ti, :], d, y_old)
                        return None

                    heads.append((scores, 0, TRI, mask, ROWS, TURNS, outs, finish))
                softmax_heads(heads)

            c.at = keep
            bg, bq, bk, bv = c.new(3, S), c.new(3, S), c.new(1, S), c.new(NT, HD)
            iq, ik = bg[:, 0:2, :], bg[:, 2:3, :]
            score, iwT, relu = c.new(TRI), c.new(NT, 4), SS[0]
            f = fence()
            t_iq = roped("i_q", 0, 256, (P, P), iq, f)
            base, tok = columns("i_k", 0, 68, (68,))
            r = rope(base, tok, ik, parts=64, n=1, after=f)
            t_iw = act.do(lambda e: e.mul(relu[64:68, 0:S], psum[64:68, base, :], 1.0 / 16.0), after=[tok, f])
            free_pair(base, [r[0], t_iw])
            t_ik = sp.load(ik[64:P, :, :], ik[0:64, :, :], s_dup, counts, after=[r[1], f])
            b0, fr = take_pair()
            for n in range(NT):
                tt = pe.do(lambda e, n=n: e.transpose(psum[:, b0, 4 * n:4 * n + 4], relu[64:68, n * P:(n + 1) * P], ident[64:68, 64:68]),
                           after=[t_iw, fr], signal=n == NT - 1)
            t_iw = act.do(lambda e: e.copy(iwT, psum[:, b0, 0:16].rearrange("p (n h) -> p n h", n=NT)), after=[tt, f])
            free_pair(b0, [t_iw])
            f2 = fence()
            for h in range(4):
                for n in range(NT):
                    r0 = (h % 2) * HD
                    tp = pe.do(lambda e, n=n, h=h, r0=r0: e.matmul(
                        flat[:, ROW_AT[n]:ROW_AT[n] + P * (n + 1)], iq[r0:r0 + HD, h // 2, n * P:(n + 1) * P], ik[r0:r0 + HD, 0, 0:P * (n + 1)],
                        start=True, stop=True), after=[t_iq, t_ik, r[1], f2, state.get("relu")], signal=n == NT - 1)
                ta = act.do(lambda e: e.activation(relu, flat[:, 0:TRI], ACT.Relu), after=[tp, dve.last()])
                state["relu"] = ta
                for n in range(NT):
                    a, b = RNG[n]
                    if h == 0:
                        td = dve.do(lambda e, a=a, b=b, n=n, h=h: e.tensor_scalar(score[:, a:b], relu[:, a:b], iwT[:, n, h:h + 1], None, ALU.mult),
                                    after=[ta, t_iw, f])
                    else:
                        td = dve.do(lambda e, a=a, b=b, n=n, h=h: e.scalar_tensor_tensor(
                            score[:, a:b], relu[:, a:b], iwT[:, n, h:h + 1], score[:, a:b], ALU.mult, ALU.add), after=[ta, td])
            for b in range(3):
                bank_free[b] = [ta]
            for n in range(1, NT):
                a, b = RNG[n]
                blk = score[:, b - P:b]
                tm = pool.do(lambda e, blk=blk: e.affine_select(out=blk, in_=blk, pattern=[[-1, P]], compare_op=ALU.is_ge, fill=NOT_CAUSAL,
                                                                base=0, channel_multiplier=1), after=[td])
            steps = []
            pos = {}

            def top8(n, i):
                a, b = RNG[n]
                m8 = stat[:, 8 * n:8 * n + 8]
                d1 = dve.do(lambda e: e.max(m8, score[:, a:b]), after=[pos.get(n), tm, td])
                pos[n] = dve.do(lambda e: e.match_replace(score[:, a:b], m8, score[:, a:b], PICKED), after=[d1])

            for i in range(P // 8):
                for n in range(1, NT):
                    steps.append((n, i))

            def some(n):
                for _ in range(min(n, len(steps))):
                    top8(*steps.pop(0))

            t_bq = roped("b_q", 0, 256, (P, P), bq, f)
            some(12)
            base, tok = columns("b_q", 256, 192, (P, 64))
            r1 = rope(base, tok, bq[:, 2:3, :], n=1, after=f)
            r2 = rope(base + 1, tok, bk, parts=64, n=1, after=f)
            free_pair(base, [r2[0]])
            t_bk = sp.load(bk[64:P, :, :], bk[0:64, :, :], s_dup, counts, after=[r2[1], f])
            some(12)
            t_bv = token_major("b_v", 0, 64, bv, f)
            t_g1 = gate_tiles("b_g", 0, 256, bg, [f, tp])
            some(12)
            t_g2 = gate_tiles("b_g", 256, 128, bg[:, 2:3, :], [f, tp])
            some(len(steps))
            for n in range(1, NT):
                a, b = RNG[n]
                tsel = dve.do(lambda e, a=a, b=b: e.tensor_scalar(score[:, a:b], score[:, a:b], PICKED_BELOW, MASKED, ALU.is_ge, ALU.mult),
                              after=[pos[n]])
            a, b = RNG[0]
            tsel = dve.do(lambda e: e.tensor_copy(score[:, a:b], causal[:, a:b]), after=[tsel, state["masks"]])
            causal_heads(3, bq, lambda h: bk[(h % 2) * HD:(h % 2) * HD + HD, 0, :], lambda h, kt: bv[:, kt, :], 6,
                         (score, [tsel]), [t_bq, r1[1], r2[1], t_bk, t_bv, t_g1, t_g2], bg)

            c.at = keep
            aq, ak, av, ag = c.new(3, S), c.new(3, S), c.new(NT, 3 * P), c.new(3, S)
            f = fence()
            r = [roped("a_q", 0, 256, (P, P), aq, f)]
            base, tok = columns("a_q", 256, 256, (P, P))
            r1 = rope(base, tok, aq[:, 2:3, :], n=1, after=f)
            r2 = rope(base + 1, tok, ak[:, 0:1, :], n=1, after=f)
            free_pair(base, [r2[0]])
            r += [r1[1], r2[1], roped("a_k", 128, 256, (P, P), ak[:, 1:3, :], f)]
            r.append(token_major("a_v", 0, 256, av[:, :, 0:256], f))
            r.append(token_major("a_v", 256, 128, av[:, :, 256:384], f))
            r.append(gate_tiles("a_g", 0, 256, ag, f))
            r.append(gate_tiles("a_g", 256, 128, ag[:, 2:3, :], f))
            causal_heads(0, aq, lambda h: ak[(h % 2) * HD:(h % 2) * HD + HD, h // 2, :], lambda h, kt: av[:, kt, h * HD:(h + 1) * HD], 6,
                         (causal[:, :], [state["masks"]]), r, ag)

            c.at = keep
            og = [c.new(2, S) for _ in range(3)]
            lse = [c.new(NT, 4) for _ in range(3)]
            rows_at = c.at
            for g, dil in enumerate((1, 4, 16)):
                c.at = rows_at
                cq, ck, cv = c.new(2, S), c.new(2, S), c.new(NT, PANEL)
                f = fence()
                vt = []
                tq = roped("c_q", g * PANEL, PANEL, (P, P), cq, f, dil)
                tk = roped("c_k", g * PANEL, PANEL, (P, P), ck, f, dil)
                if g == 0:
                    tv = token_major("c_v", 0, PANEL, cv, f)
                else:
                    base, tok = columns("c_v", g * PANEL, PANEL, (P, P))
                    for m in range(2):
                        ta = act.do(lambda e, base=base, m=m: e.copy(rope_x[:, m, :].rearrange("p (r j) -> p r j", r=dil),
                                                                     psum[:, base + m, :].rearrange("p (j r) -> p r j", r=dil)),
                                    after=[tok, rope_free["x"]])
                    free_pair(base, [ta])
                    base, fr = take_pair()
                    for m in range(2):
                        for r_ in range(NT):
                            o = (base + r_ // 2) * 512 + (r_ % 2) * PANEL + m * P
                            tt = pe.do(lambda e, m=m, r_=r_, o=o: e.transpose(flat[:, o:o + P], rope_x[:, m, r_ * P:(r_ + 1) * P], ident[:, :]),
                                       after=[ta, fr], signal=(m, r_) == (1, NT - 1))
                    tv = act.do(lambda e, base=base: e.copy(cv, flat[:, base * 512:(base + 2) * 512].rearrange("p (t c) -> p t c", c=PANEL)),
                                after=[tt, f])
                    rope_free["x"] = tt
                    free_pair(base, [tv])
                if g == 0:
                    tm = pool.do(lambda e: e.memset(maskc[:, 0:7 * P], 0.0), after=[f])
                    for u in range(7):
                        blk = maskc[:, u * P:(u + 1) * P]
                        own = u % 2 == 0
                        tm = pool.do(lambda e, blk=blk, own=own: e.affine_select(
                            out=blk, in_=blk, pattern=[[-1 if own else 1, P]], compare_op=ALU.is_ge, fill=MASKED, base=0,
                            channel_multiplier=1 if own else -1), after=[tm])
                else:
                    tm = pool.do(lambda e: e.memset(maskc[:, 0:4 * P], 0.0), after=[f])
                    tm = pool.do(lambda e: e.affine_select(out=maskc[:, 0:4 * P], in_=maskc[:, 0:4 * P], pattern=[[0, 4], [-1, P]],
                                                           compare_op=ALU.is_ge, fill=MASKED, base=0, channel_multiplier=1), after=[tm])
                    if g == 2:
                        n_sub = S // dil
                        for u in range(1, P // n_sub):
                            blk = maskc[:, 0:4 * P].rearrange("p (n c) -> p n c", n=4)[:, :, (u - 1) * n_sub:u * n_sub]
                            tm = pool.do(lambda e, blk=blk, u=u: e.affine_select(out=blk, in_=blk, pattern=[[0, 4], [0, n_sub]], compare_op=ALU.is_gt,
                                                                                 fill=MASKED, base=u * n_sub, channel_multiplier=-1), after=[tm])
                ready = [tq, tk, tv]
                heads = []
                o_free = {6: [], 7: []}
                for sl in range(4):
                    ti, r0 = sl // 2, (sl % 2) * HD
                    ob = 6 + ti

                    def scores(after, ti=ti, r0=r0, g=g, qq=cq, kk=ck):
                        for n in range(NT):
                            if g == 0:
                                lo = 0 if n == 0 else P * (2 * n - 1)
                                k0 = P * max(n - 1, 0)
                                for u in range(1 if n == 0 else 2):
                                    tok = pe.do(lambda e, n=n, lo=lo, k0=k0, u=u: e.matmul(
                                        flat[:, lo + u * P:lo + u * P + P], qq[r0:r0 + HD, ti, n * P:(n + 1) * P],
                                        kk[r0:r0 + HD, ti, k0 + u * P:k0 + u * P + P], start=True, stop=True), after=[after, ready])
                            else:
                                tok = pe.do(lambda e, n=n: e.matmul(
                                    flat[:, n * P:(n + 1) * P], qq[r0:r0 + HD, ti, n * P:(n + 1) * P],
                                    kk[r0:r0 + HD, ti, n * P:(n + 1) * P], start=True, stop=True), after=[after, ready])
                        return tok

                    def outs(ta, ti=ti, r0=r0, g=g, ob=ob, sl=sl, cv=cv):
                        for n in range(NT):
                            if g == 0:
                                terms = [(n, 2 * n * P)] + ([(n - 1, (2 * n - 1) * P)] if n else [])
                            else:
                                terms = [(n, n * P)]
                            for i, (kt, o) in enumerate(terms):
                                tok = pe.do(lambda e, n=n, kt=kt, o=o, i=i, last=len(terms) - 1: e.matmul(
                                    psum[r0:r0 + HD, ob, n * P:(n + 1) * P], cv[:, kt, sl * HD:(sl + 1) * HD], PT[:, o:o + P],
                                    start=i == 0, stop=i == last, skip_group_check=True), after=[ta, ready, o_free[ob]])
                        return tok

                    def finish(s, to, ti=ti, g=g, ob=ob, sl=sl, dil=dil):
                        m0 = 16 * s
                        ta = act.do(lambda e: e.activation(lse[g][:, :, sl], stat[:, m0 + 8:m0 + 12], ACT.Ln), after=[act.last()])
                        td = dve.do(lambda e: e.tensor_tensor(lse[g][:, :, sl], lse[g][:, :, sl], stat[:, m0:m0 + 4], ALU.add), after=[ta])
                        if sl % 2:
                            dst = og[g][:, ti, :]
                            src = psum[:, ob, :]
                            if dil > 1:
                                dst = dst.rearrange("p (j r) -> p r j", r=dil)
                                src = src.rearrange("p (r j) -> p r j", r=dil)
                            tc = act.do(lambda e: e.copy(dst, src), after=[to, f])
                            o_free[ob] = [tc]
                        return td

                    if g == 0:
                        rows = [(0, P, 1), (P, 7 * P, 3)]
                        turns = [(i * P, i * P) for i in range(7)]
                        heads.append((scores, 0, 7 * P, (maskc, [tm]), rows, turns, outs, finish))
                    else:
                        turns = [(i * P, i * P) for i in range(4)]
                        heads.append((scores, 0, 4 * P, (maskc[:, 0:4 * P], [tm]), [(0, 4 * P, 4)], turns, outs, finish))
                softmax_heads(heads)

            f = fence()
            c.at = rows_at
            cg = c.new(2, S)
            L = [c.new(S) for _ in range(3)]
            M = c.new(S)
            sel = c.new(2, P)
            t_cg = gate_tiles("c_g", 0, 256, cg, f)
            tm = pool.do(lambda e: e.memset(sel[0:4, :, :], 1.0), after=[f])
            tm = pool.do(lambda e: e.affine_select(out=sel[0:4, :, :], in_=sel[0:4, :, :], pattern=[[P, 2], [1, P]], compare_op=ALU.is_ge,
                                                   fill=0.0, base=0, channel_multiplier=-HD), after=[tm])
            tm = pool.do(lambda e: e.affine_select(out=sel[0:4, :, :], in_=sel[0:4, :, :], pattern=[[-P, 2], [-1, P]], compare_op=ALU.is_gt,
                                                   fill=0.0, base=HD, channel_multiplier=HD), after=[tm])
            lt = []
            for g, dil in enumerate((1, 4, 16)):
                b = g
                for n in range(NT):
                    tt = pe.do(lambda e, g=g, n=n, b=b: e.transpose(psum[0:4, b, n * P:(n + 1) * P], lse[g][:, n, :], ident[:, :]),
                               after=[f, bank_free[b]], signal=n == NT - 1)
                src, dst = psum[0:4, b, :], L[g][0:4, :]
                if dil > 1:
                    src = src.rearrange("p (r j) -> p r j", r=dil)
                    dst = dst.rearrange("p (j r) -> p r j", r=dil)
                ta = act.do(lambda e, src=src, dst=dst: e.copy(dst, src), after=[tt, f])
                bank_free[b] = [ta]
                lt.append(ta)
            l3 = [x[0:4, :] for x in L]
            mm = M[0:4, :]
            d = dve.do(lambda e: e.tensor_tensor(mm, l3[0], l3[1], ALU.max), after=[lt, f])
            d = dve.do(lambda e: e.tensor_tensor(mm, mm, l3[2], ALU.max), after=[d])
            es = []
            for g in range(3):
                dd = dve.do(lambda e, g=g: e.tensor_tensor(l3[g], l3[g], mm, ALU.subtract), after=[d])
                es.append(act.do(lambda e, g=g: e.activation(l3[g], l3[g], ACT.Exp), after=[dd]))
            d = dve.do(lambda e: e.tensor_tensor(mm, l3[0], l3[1], ALU.add), after=[es, dd])
            d = dve.do(lambda e: e.tensor_tensor(mm, mm, l3[2], ALU.add), after=[d])
            d = dve.do(lambda e: e.reciprocal(mm, mm), after=[d])
            for g in range(3):
                dd = dve.do(lambda e, g=g: e.tensor_tensor(l3[g], l3[g], mm, ALU.mult), after=[d])
            for m in range(2):
                base, fr = take_pair()
                prev = None
                for g in range(3):
                    b = base + g % 2
                    tp = pe.do(lambda e, g=g, m=m, b=b: e.matmul(psum[:, b, :], sel[0:4, m, :], l3[g], start=True, stop=True),
                               after=[dd, tm, fr, prev])
                    prev = dve.do(lambda e, g=g, m=m, b=b: e.tensor_tensor(og[g][:, m, :], og[g][:, m, :], psum[:, b, :], ALU.mult), after=[tp, f])
                free_pair(base, [prev])
                d1 = dve.do(lambda e, m=m: e.tensor_tensor(og[0][:, m, :], og[0][:, m, :], og[1][:, m, :], ALU.add), after=[prev])
                d1 = dve.do(lambda e, m=m: e.tensor_tensor(og[0][:, m, :], og[0][:, m, :], og[2][:, m, :], ALU.add), after=[d1])
                d1 = dve.do(lambda e, m=m: e.tensor_tensor(cg[:, m, :], cg[:, m, :], og[0][:, m, :], ALU.mult), after=[d1, t_cg])
                yr[6 + m] = split_into(Y, 6 + m, cg[:, m, :], d1, y_old)

            f = fence()
            c.at = 0
            merged = c.new(KD, S)
            sg = [c.new(2, S) for _ in range(3)]
            sg_free = [f, f, f]
            mt = []
            br_w = (t["w_br_a_2"][layer], t["w_br_b_2"][layer], t["w_br_c_2"][layer])
            chunks = (range(0, 3), range(3, 6), range(6, 8))
            for jj in range(KD // 2):
                st = []
                for b in range(3):
                    base, tok = columns("m_g", b * D + jj * PANEL, PANEL, (P, P))
                    ta = act.do(lambda e, b=b, base=base: e.activation(sg[b], psum[:, base:base + 2, :], ACT.Sigmoid), after=[tok, sg_free[b], f])
                    free_pair(base, [ta])
                    st.append(ta)
                (wh, wl), wt, done = stream.take([piece(w[:, jj * PANEL:(jj + 1) * PANEL], len(ch), off=ch[0] * PANEL) for w, ch in zip(br_w, chunks)])
                wv = [w[:, :RAW].rearrange("p (k n) -> p k n", n=PANEL) for w in (wh, wl)]
                dst = merged[:, 2 * jj:2 * jj + 2, :]
                for b in range(3):
                    base, free = take_pair()
                    for m in range(2):
                        for i, k in enumerate(chunks[b]):
                            for x, y in ((0, 0), (0, 1), (1, 0)):
                                end = (x, y) == (1, 0) and i == len(chunks[b]) - 1
                                tok = pe.do(lambda e, m=m, i=i, k=k, x=x, y=y, end=end, base=base: e.matmul(
                                    psum[:, base + m, :], wv[x][:, k, m * P:(m + 1) * P], Y[y][:, k, :], start=(i == 0 and (x, y) == (0, 0)), stop=end),
                                    after=[wt, yr[k], free], signal=end)
                    td = dve.do(lambda e, b=b, base=base: e.tensor_tensor(sg[b], sg[b], psum[:, base:base + 2, :], ALU.mult), after=[tok, st[b]])
                    free_pair(base, [td])
                    if b == 1:
                        td = dve.do(lambda e: e.tensor_tensor(dst, sg[0], sg[1], ALU.add), after=[td, f])
                    if b == 2:
                        td = dve.do(lambda e: e.tensor_tensor(dst, dst, sg[2], ALU.add), after=[td])
                done(tok)
                sg_free = [td, td, td]
                mt.append(td)
            old = fence()
            mr = []
            for j in range(KD):
                mr.append(split_into(H, j, merged[:, j, :], mt[j // 2], old))
            project_back(H, mr, t["w_out_2"][layer], 0, KD, None, x_ready)

        def program():
            tc = [pool.do(lambda e: e.memset(ones[:, :], 1.0)), pool.do(lambda e: e.memset(neg_ones[:, :], -1.0)),
                  pool.do(lambda e: e.memset(small[:, 0:1], EPS)), pool.do(lambda e: e.memset(causal[:, :], 0.0))]
            ti = pool.do(lambda e: e.affine_select(out=ident[:, :], in_=ones[:, :], pattern=[[1, P]], compare_op=ALU.is_equal, fill=0.0,
                                                   base=0, channel_multiplier=-1), after=tc)
            pool.do(lambda e: e.affine_select(out=neg_tri[:, :], in_=neg_ones[:, :], pattern=[[-1, P]], compare_op=ALU.is_ge, fill=0.0,
                                              base=0, channel_multiplier=1), after=[ti])
            for n in range(NT):
                blk = causal[:, ROW_AT[n] + n * P:ROW_AT[n] + (n + 1) * P]
                tm = pool.do(lambda e, blk=blk: e.affine_select(out=blk, in_=blk, pattern=[[-1, P]], compare_op=ALU.is_ge, fill=MASKED,
                                                                base=0, channel_multiplier=1), after=[ti])
            state["consts"] = state["masks"] = tm
            c = Carver()
            xin = c.new(NT, D)
            rows = c.new(len(groups), P)
            at = 0
            for g, names in enumerate(groups):
                r = 0
                for name, n in names:
                    src = t[name]
                    if name == "mod_b":
                        src = src[g - 1:g, :]
                    nd = len(src.shape)
                    src = (src.rearrange("(n p) -> n p", p=P) if nd == 1 else src.rearrange("a (n p) -> (a n) p", p=P) if nd == 2
                           else src.rearrange("a b (n p) -> (a b n) p", p=P))
                    tl = sp.load(rows[r:r + n, g, :], src, s_tab, counts)
                    r += n
            sp.load(rope_c[:, :], t["rope_cos"], s_tab, counts)
            tl = sp.load(rope_s[:, :], t["rope_sin"], s_tab, counts)
            xl = sp.load(xin, t["x"][0].rearrange("(n p) d -> p n d", p=P), s_in, counts)
            b, fr = take_pair()
            for g, names in enumerate(groups):
                n = sum(k for _, k in names)
                tt = pe.do(lambda e, g=g, n=n, at=at: e.transpose(psum[:, b, at:at + n], rows[0:n, g, :], ident[0:n, 0:n]), after=[tl, tm])
                at += n
            tv = act.do(lambda e: e.copy(vec[:, 0:at], psum[:, b, 0:at]), after=[tt])
            free_pair(b, [tv])
            state["vec"] = tv
            state["c_act"] = act.do(lambda e: e.activation(v("c_act", 0, KD), v("c", 0, KD), ACT.Silu), after=[tv])
            x_ready = []
            for j in range(KD):
                if j % 2 == 0:
                    b, fr = take_pair()
                for n in range(NT):
                    tt = pe.do(lambda e, j=j, n=n, b=b: e.transpose(psum[:, b + j % 2, n * P:(n + 1) * P], xin[:, n, j * P:(j + 1) * P], ident[:, :]),
                               after=[xl, fr, tm], signal=n == NT - 1)
                tx = act.do(lambda e, j=j, b=b: e.copy(xT[:, j, :], psum[:, b + j % 2, :]), after=[tt])
                if j % 2:
                    free_pair(b, [tx])
                x_ready.append([tx])
            n = RNN // P
            lam, dec = v("lru_lambda", 0, n), v("decay", 0, n)
            e0, s0, s2, p0 = (small[:, 16 + 16 * i:16 + 16 * i + n] for i in range(4))
            a = act.do(lambda e: e.activation(e0, lam, ACT.Abs), after=[tv])
            a = act.do(lambda e: e.activation(e0, e0, ACT.Exp, scale=-1.0), after=[a])
            d = dve.do(lambda e: e.tensor_scalar(s0, e0, 2.0, None, ALU.add), after=[a])
            d = dve.do(lambda e: e.reciprocal(s0, s0), after=[d])
            d = dve.do(lambda e: e.tensor_tensor(s0, s0, e0, ALU.mult), after=[d])
            d = dve.do(lambda e: e.tensor_tensor(s2, s0, s0, ALU.mult), after=[d])
            TERMS = 9
            d = dve.do(lambda e: e.tensor_scalar(p0, s2, 1.0 / (2 * TERMS - 1), 1.0 / (2 * TERMS - 3), ALU.mult, ALU.add), after=[d])
            for i in range(TERMS - 3, -1, -1):
                d = dve.do(lambda e: e.tensor_tensor(p0, p0, s2, ALU.mult), after=[d])
                d = dve.do(lambda e, i=i: e.tensor_scalar(p0, p0, 1.0 / (2 * i + 1), None, ALU.add), after=[d])
            d = dve.do(lambda e: e.tensor_tensor(p0, p0, s0, ALU.mult), after=[d])
            d = dve.do(lambda e: e.tensor_scalar(s2, lam, -1.0, 0.0, ALU.mult, ALU.max), after=[d])
            d = dve.do(lambda e: e.scalar_tensor_tensor(p0, p0, 2.0, s2, ALU.mult, ALU.add), after=[d])
            state["decay"] = dve.do(lambda e: e.tensor_scalar(dec, p0, -8.0, None, ALU.mult), after=[d])

            ffn_order = ((0, 0, 0), (0, 1, 2), (1, 0, 0), (1, 1, 2))
            if stream.plan is not None:
                while stream.n_split < 1:
                    stream.split_next()
            ffn(*ffn_order[0], x_ready)
            stick_breaking(x_ready)
            ffn(*ffn_order[1], x_ready)
            ffn(*ffn_order[2], x_ready)
            rglru(x_ready)
            ffn(*ffn_order[3], x_ready)
            x_ready = norm(x_ready, xT, lambda j: v("final_norm_g", j), split=False)
            for layer in range(2):
                hybrid(layer, x_ready)
            norm_out = norm(x_ready, xT, lambda j: v("final_norm_g_2", j), split=False)
            c = Carver()
            c.at = 5 * S
            y = c.new(NT, D)
            for n in range(NT):
                b, fr = take_pair()
                for j in range(KD):
                    tt = pe.do(lambda e, j=j, n=n, b=b: e.transpose(flat[:, b * 512 + j * P:b * 512 + (j + 1) * P], xT[:, j, n * P:(n + 1) * P], ident[:, :]),
                               after=[norm_out[j], fr], signal=j == KD - 1)
                ty = act.do(lambda e, n=n, b=b: e.copy(y[:, n, :], flat[:, b * 512:(b + 2) * 512]), after=[tt])
                free_pair(b, [ty])
                to = sp.load(out[0, n * P:(n + 1) * P, :], y[:, n, :], s_out, counts, after=[ty])
            sp.wait([to])

        stream = Stream(None, None, 0)
        program()
        asked = stream.asked
        for q in (pe, act, dve, pool, sp):
            q.value, q.items, q.waited = 0, [], {}
        counts.clear()
        state.clear()
        pairs[0] = 0
        bank_free[:] = [[] for _ in range(8)]
        stream = Stream(asked, mod_panels(), 3 * KD // 2)
        program()

        block = ctx.enter_context(nc.Block())

        @block.sync
        def _(e):
            sp.play(e)

        @block.tensor
        def _(e):
            pe.play(e)

        @block.scalar
        def _(e):
            act.play(e)

        @block.vector
        def _(e):
            dve.play(e)

        @block.gpsimd
        def _(e):
            pool.play(e)


_INS = ["x", "c", "mod_w", "mod_b", "norm_g", "ffn_w_gu", "ffn_w_down", "sb_w_qkv", "sb_w_o", "lru_w_in", "lru_conv_w",
        "lru_conv_b", "lru_w_r", "lru_b_r", "lru_w_i", "lru_b_i", "lru_lambda", "lru_w_out", "final_norm_g",
        "norm_g_2", "w_in_2", "w_br_a_2", "w_br_b_2", "w_br_c_2", "w_out_2", "final_norm_g_2"]


def rope_constants(seq, head_dim=64, theta=10000.0):
    half = head_dim // 2
    inv_freq = (np.float32(1.0) / (np.float32(theta) ** (np.arange(0, head_dim, 2, dtype=np.float32) / np.float32(head_dim)))).astype(np.float32)
    ang = (inv_freq[:, None] * np.arange(seq, dtype=np.float32)[None, :]).astype(np.float32)
    c, s = np.cos(ang), np.sin(ang)
    return np.tile(c, (4, 1)).astype(np.float32), np.concatenate([-s, s, -s, s]).astype(np.float32)


def kernel(**inputs):
    import numpy as _np
    import concourse.bacc as _bacc
    from concourse import mybir as _mybir
    from concourse.bass_utils import run_bass_kernel_spmd as _run

    nc = _bacc.Bacc("TRN2", target_bir_lowering=False, num_devices=1)
    arrays, aps = {}, {}
    for name in _INS:
        a = _np.ascontiguousarray(inputs[name])
        arrays[f"in_{name}"] = a
        aps[name] = nc.dram_tensor(f"in_{name}", a.shape, _mybir.dt.from_np(a.dtype), kind="ExternalInput").ap()
    shape = inputs["x"].shape
    for name, a in zip(("rope_cos", "rope_sin"), rope_constants(shape[1])):
        arrays[name] = a
        aps[name] = nc.dram_tensor(name, a.shape, _mybir.dt.from_np(a.dtype), kind="ExternalInput").ap()
    out = nc.dram_tensor("out_0", shape, _mybir.dt.from_np(_np.dtype("float32")), kind="ExternalOutput").ap()
    build(nc, aps, out)
    r = _run(nc, [arrays], core_ids=[0])
    return r.results[0]["out_0"]
```

```python
from contextlib import ExitStack

import numpy as np

import concourse.bass as bass
from concourse import mybir

F32 = mybir.dt.float32
F32R = mybir.dt.float32r
ALU = mybir.AluOpType
ACT = mybir.ActivationFunctionType
AX = mybir.AxisListType

P = 128
MASKED = -1.0e30
NOT_CAUSAL = -3.0e38
PICKED = -3.4e38
PICKED_BELOW = -3.2e38


class Operands:

    def matmul(self, *a, **k):
        return lambda e: e.matmul(*a, **k)

    def transpose(self, *a, **k):
        return lambda e: e.transpose(*a, **k)

    def activation(self, *a, **k):
        return lambda e: e.activation(*a, **k)

    def copy(self, *a, **k):
        return lambda e: e.copy(*a, **k)

    def mul(self, *a, **k):
        return lambda e: e.mul(*a, **k)

    def tensor_tensor(self, *a, **k):
        return lambda e: e.tensor_tensor(*a, **k)

    def tensor_scalar(self, *a, **k):
        return lambda e: e.tensor_scalar(*a, **k)

    def scalar_tensor_tensor(self, *a, **k):
        return lambda e: e.scalar_tensor_tensor(*a, **k)

    def tensor_tensor_scan(self, *a, **k):
        return lambda e: e.tensor_tensor_scan(*a, **k)

    def tensor_copy(self, *a, **k):
        return lambda e: e.tensor_copy(*a, **k)

    def tensor_reduce(self, *a, **k):
        return lambda e: e.tensor_reduce(*a, **k)

    def reciprocal(self, *a, **k):
        return lambda e: e.reciprocal(*a, **k)

    def max(self, *a, **k):
        return lambda e: e.max(*a, **k)

    def match_replace(self, *a, **k):
        return lambda e: e.match_replace(*a, **k)

    def memset(self, *a, **k):
        return lambda e: e.memset(*a, **k)

    def preload_act_table_set(self, *a, **k):
        return lambda e: e.preload_act_table_set(*a, **k)

    def affine_select(self, *a, **k):
        return lambda e: e.affine_select(*a, **k)


class Queue:

    def __init__(self, semaphore):
        self.semaphore, self.value, self.items, self.waited = semaphore, 0, [], {}

    def wait(self, after):
        for producer in after:
            if isinstance(producer, list):
                self.wait(producer)
            elif producer is not None:
                sem, value = producer
                if value > self.waited.get(id(sem), 0):
                    self.waited[id(sem)] = value
                    self.items.append(lambda e, sem=sem, value=value: e.wait_ge(sem, value))

    def do(self, make, after=(), signal=True):
        self.wait(after)
        step = make(Operands())
        if not signal:
            self.items.append(step)
            return None
        self.value += 1
        self.items.append(lambda e: step(e).then_inc(self.semaphore, 1))
        return (self.semaphore, self.value)

    def load(self, out, in_, sem, counts, after=()):
        self.wait(after)
        counts[id(sem)] = counts.get(id(sem), 0) + 16
        self.items.append(lambda e: e.dma_start(out, in_).then_inc(sem, 16))
        return (sem, counts[id(sem)])

    def last(self):
        return (self.semaphore, self.value) if self.value else None

    def play(self, engine):
        for item in self.items:
            item(engine)


def build(nc, t, out):
    S, D = t["x"].shape[1:]
    KD = D // P
    NT = S // P
    FF = t["ffn_w_down"].shape[2]
    RNN = t["lru_w_out"].shape[1]
    HD = 64
    PANEL = 2 * P
    RAW = KD * PANEL
    SCALE = HD ** -0.5
    EPS = 1e-6
    TRI = S * (NT + 1) // 2
    ROW_AT = {3: 0, 2: 512, 0: 896, 1: 1024}
    COL_AT = {0: 0, 1: 512, 3: 896, 2: 1024}

    with ExitStack() as ctx:
        def sb(name, shape, dt=F32):
            return ctx.enter_context(nc.sbuf_tensor(name, shape, dt))

        def sem(name):
            return ctx.enter_context(nc.semaphore(name))

        xT = sb("xT", [P, KD, S])
        H = (sb("h_high", [P, KD, S], F32R), sb("h_low", [P, KD, S], F32R))
        Y = (sb("y_high", [P, KD, S], F32R), sb("y_low", [P, KD, S], F32R))
        NRAW, NW = 3, 2
        raw = [sb(f"raw{i}", [P, RAW]) for i in range(NRAW)]
        W = [(sb(f"w_high{i}", [P, RAW], F32R), sb(f"w_low{i}", [P, RAW], F32R)) for i in range(NW)]
        ident = sb("ident", [P, P])
        ones = sb("ones", [P, P])
        neg_tri = sb("neg_tri", [P, P])
        neg_ones = sb("neg_ones", [P, P])
        causal = sb("causal", [P, TRI])
        rope_c = sb("rope_c", [P, S])
        rope_s = sb("rope_s", [P, S])
        mod_acc = sb("mod_acc", [P, D])
        inv = sb("inv", [P, S])
        vec = sb("vec", [P, 336])
        small = sb("small", [P, 96])
        AREA = 13312
        area = sb("area", [P, AREA])
        psum = ctx.enter_context(nc.psum_tensor("psum", [P, 8, 512], F32))
        flat = psum[:, :, :].rearrange("p b c -> p (b c)")

        pe, act, dve, pool, sp = (Queue(sem(f"{n}_done")) for n in ("pe", "act", "dve", "pool", "sp"))
        s_raw = [sem(f"raw_loaded{i}") for i in range(NRAW)]
        s_in, s_tab, s_swap, s_out, s_gate_w = sem("x_loaded"), sem("tables_loaded"), sem("swapped"), sem("stored"), sem("gate_w_loaded")
        s_dup = sem("copied_half")
        counts = {}
        state = {}

        def fence():
            return [q.last() for q in (pe, act, dve, pool)]

        class Carver:

            def __init__(self):
                self.at = 0

            def new(self, *shape):
                n = int(np.prod(shape))
                assert self.at + n <= AREA, (self.at, n)
                a = area[:, self.at:self.at + n]
                self.at += n
                if len(shape) == 2:
                    a = a.rearrange("p (a b) -> p a b", a=shape[0])
                if len(shape) == 3:
                    a = a.rearrange("p (a b c) -> p a b c", a=shape[0], b=shape[1])
                return a

        groups = [
            [("c", KD), ("norm_g", 6 * KD), ("final_norm_g", KD), ("norm_g_2", 2 * KD), ("final_norm_g_2", KD)],
            [("mod_b", 9 * KD)],
            [("mod_b", 9 * KD)],
            [("lru_conv_w", 4 * RNN // P), ("lru_conv_b", RNN // P), ("lru_b_r", RNN // P),
             ("lru_b_i", RNN // P), ("lru_lambda", RNN // P)],
        ]
        col = {}
        at = 0
        for g, names in enumerate(groups):
            for name, n in names:
                col[f"{name}{g - 1 if name == 'mod_b' else ''}"] = at
                at += n
        col["c_act"] = at
        col["decay"] = at + KD
        assert col["decay"] + RNN // P <= 336
        mods = [sb(f"mod{i}", [P, 9 * KD]) for i in range(2)]

        def v(name, i=0, n=1):
            return vec[:, col[name] + i:col[name] + i + n]

        bank_free = [[] for _ in range(8)]
        pairs = [0]

        def take_pair():
            b = 2 * (pairs[0] % 4)
            pairs[0] += 1
            return b, [bank_free[b], bank_free[b + 1]]

        class Stream:

            def __init__(self, plan, mod_plan, lead):
                self.asked = []
                self.plan = None
                if plan is not None:
                    merged, rest = list(mod_plan[:lead]), list(mod_plan[lead:])
                    for k in plan:
                        merged.append(("w", k))
                        if rest:
                            merged.append(rest.pop(0))
                    self.plan = merged
                self.loaded = self.split = 0
                self.raw_free = [None] * NRAW
                self.w_free = [None] * NW
                self.n_split = 0
                self.n_taken = 0
                self.ready = {}
                self.raw_ready = {}
                self.late = None
                self.low_by = dve

            def turn(self):
                if self.late:
                    late, self.late = self.late, None
                    late()

            def load_next(self):
                if self.loaded >= len(self.plan):
                    return
                kind, pieces = self.plan[self.loaded]
                s = self.loaded % NRAW
                for off, n, k, src in pieces:
                    dst = raw[s][:, off:off + n].rearrange("p (k n) -> p k n", k=k)
                    tok = sp.load(dst, src, s_raw[s], counts, after=[self.raw_free[s]])
                self.raw_ready[self.loaded] = tok
                self.loaded += 1

            def split_next(self):
                while self.split < len(self.plan):
                    i = self.split
                    while self.loaded <= i:
                        self.load_next()
                    kind, pieces = self.plan[i]
                    s = i % NRAW
                    self.split += 1
                    got = self.raw_ready.pop(i)
                    if kind == "w":
                        n = sum(p[1] for p in pieces)
                        w = self.n_split % NW
                        high, low = W[w]
                        th = act.do(lambda e: e.copy(high[:, :n], raw[s][:, :n]), after=[got, self.w_free[w]])
                        tl = self.low_by.do(lambda e: e.tensor_tensor(low[:, :n], raw[s][:, :n], high[:, :n].bitcast(F32), ALU.subtract),
                                            after=[th, self.w_free[w]])
                        self.raw_free[s] = tl
                        self.ready[self.n_split] = (w, [th, tl])
                        self.n_split += 1
                        self.load_next()
                        return
                    self.mod_step(kind, s, got)
                    self.load_next()

            def mod_step(self, kind, s, got):
                _, layer, sub, part, kp = kind
                if kp == 0:
                    self.turn()
                for k in range(2):
                    w = raw[s][:, k * D:(k + 1) * D]
                    c = v("c_act", 2 * kp + k)
                    if kp == 0 and k == 0:
                        tok = dve.do(lambda e: e.tensor_scalar(mod_acc[:, :], w, c, None, ALU.mult),
                                     after=[got, state["c_act"], state.get("mod_read")])
                    else:
                        tok = dve.do(lambda e: e.scalar_tensor_tensor(mod_acc[:, :], w, c, mod_acc[:, :], ALU.mult, ALU.add),
                                     after=[got, dve.last()])
                self.raw_free[s] = tok
                if kp < KD // 2 - 1:
                    return

                def turn():
                    b, free = take_pair()
                    for j in range(KD):
                        tp = pe.do(lambda e, j=j: e.matmul(psum[:, b, j:j + 1], mod_acc[:, j * P:(j + 1) * P], ones[:, 0:1],
                                                           start=True, stop=True), after=[tok, free, state["consts"]], signal=j == KD - 1)
                    state["mod_read"] = tp
                    o = (3 * sub + part) * KD
                    td = dve.do(lambda e: e.tensor_tensor(mods[layer][:, o:o + KD], psum[:, b, 0:KD], v(f"mod_b{layer}", o, KD), ALU.add),
                                after=[tp, state["vec"]])
                    bank_free[b] = [td]
                    state[("mod", layer, sub, part)] = td
                self.late = turn

            def take(self, pieces):
                if self.plan is None:
                    self.asked.append(pieces)
                    i = self.n_taken
                    self.n_taken += 1
                    return W[0], [], lambda tok: None
                i = self.n_taken
                self.n_taken += 1
                self.turn()
                while self.n_split <= i:
                    self.split_next()
                if self.n_split == i + 1 and i > 0:
                    self.split_next()
                w, toks = self.ready.pop(i)

                def done(tok):
                    self.w_free[w] = tok
                return W[w], toks, done

        def piece(src, k, off=0):
            n = src.shape[1] * k
            return (off, n, k, src.rearrange("(k p) n -> p k n", p=P))

        def mod_panels():
            plan = []
            for layer in range(2):
                for sub in range(3):
                    for part in range(3):
                        for kp in range(KD // 2):
                            c0 = (3 * sub + part) * D
                            src = t["mod_w"][layer, 2 * kp * P:(2 * kp + 2) * P, c0:c0 + D]
                            plan.append((("m", layer, sub, part, kp), [piece(src, 2)]))
            return plan

        def product(X, ready, src_pieces, ks, n, free, widths=(P, P), base=None, first=True, last=True):
            (wh, wl), wt, done = stream.take(src_pieces)
            if base is None:
                base, free = take_pair()
            wv = [w[:, :len(ks) * n].rearrange("p (k n) -> p k n", n=n) for w in (wh, wl)]
            combos = ((0, 0), (0, 1), (1, 0))
            for i, k in enumerate(ks):
                c0 = 0
                for m, width in enumerate(widths):
                    for a, b in combos:
                        end = i == len(ks) - 1 and m == len(widths) - 1 and (a, b) == combos[-1]
                        tok = pe.do(lambda e, i=i, k=k, m=m, a=a, b=b, c0=c0, width=width: e.matmul(
                            psum[0:width, base + m, :], wv[a][:, i, c0:c0 + width], X[b][:, k, :],
                            start=(i == 0 and (a, b) == (0, 0)), stop=(i == len(ks) - 1 and (a, b) == combos[-1])),
                            after=[wt, ready[k], free], signal=end)
                    c0 += width
            done(tok)
            return base, tok

        def product_tok(X, ready, src_pieces, n):
            (wh, wl), wt, done = stream.take(src_pieces)
            base, free = take_pair()
            wv = [w[:, :KD * n].rearrange("p (k n) -> p k n", n=n) for w in (wh, wl)]
            for tt in range(NT):
                for k in range(KD):
                    for a, b in ((0, 0), (0, 1), (1, 0)):
                        end = tt == NT - 1 and k == KD - 1 and (a, b) == (1, 0)
                        o = (base + tt // 2) * 512 + (tt % 2) * PANEL
                        tok = pe.do(lambda e, tt=tt, k=k, a=a, b=b, o=o: e.matmul(
                            flat[:, o:o + n], X[b][:, k, tt * P:(tt + 1) * P], wv[a][:, k, :],
                            start=(k == 0 and (a, b) == (0, 0)), stop=(k == KD - 1 and (a, b) == (1, 0))),
                            after=[wt, ready[k], free], signal=end)
            done(tok)
            view = flat[:, base * 512:(base + 2) * 512].rearrange("p (t c) -> p t c", c=PANEL)[:, :, :n]
            return base, view, tok

        def free_pair(base, toks):
            bank_free[base] = bank_free[base + 1] = list(toks)

        def norm(x_ready, dst, gain, shift=None, old_reads=(), split=True):
            f = state["area_free"]
            c = Carver()
            ssum = c.new(S)
            sq = c.new(2, S)
            tmp = c.new(2, S)
            stats = small[:, 80:96]
            mean, root, y2 = stats[:, 0:4], stats[:, 4:8], stats[:, 8:12]
            act.do(lambda e: e.activation(small[:, 1:2], small[:, 0:1], ACT.Sqrt), after=[state["consts"], act.last()])
            used = [None, None]
            tsum = None
            for j in range(KD):
                if j == 0:
                    tsum = act.do(lambda e: e.activation(ssum, xT[:, 0, :], ACT.Square), after=[x_ready[0], f])
                    continue
                ts = act.do(lambda e: e.activation(sq[:, j % 2, :], xT[:, j, :], ACT.Square), after=[x_ready[j], f, used[j % 2]])
                tsum = dve.do(lambda e: e.tensor_tensor(ssum, ssum, sq[:, j % 2, :], ALU.add), after=[ts, tsum])
                used[j % 2] = tsum
            b, free = take_pair()
            for n in range(NT):
                tp = pe.do(lambda e: e.matmul(psum[:, b, n:n + 1], ssum[:, n * P:(n + 1) * P], ones[:, 0:1], start=True, stop=True),
                           after=[tsum, free], signal=n == NT - 1)
            tv = dve.do(lambda e: e.tensor_scalar(mean, psum[:, b, 0:NT], 1.0 / D, EPS, ALU.mult, ALU.add), after=[tp])
            tr = act.do(lambda e: e.activation(root, mean, ACT.Sqrt), after=[tv])
            ti = dve.do(lambda e: e.reciprocal(root, root), after=[tr])
            ti = dve.do(lambda e: e.tensor_tensor(y2, root, root, ALU.mult), after=[ti])
            ti = dve.do(lambda e: e.scalar_tensor_tensor(y2, y2, -0.5, mean, ALU.mult, ALU.mult), after=[ti])
            ti = dve.do(lambda e: e.scalar_tensor_tensor(root, y2, 1.5, root, ALU.add, ALU.mult), after=[ti])
            for n in range(NT):
                td = dve.do(lambda e: e.tensor_scalar(inv[:, n * P:(n + 1) * P], ident[:, :], root[:, n:n + 1], None, ALU.mult),
                            after=[ti, state["consts"], state.get("inv_read")])
            ti = pe.do(lambda e: e.matmul(psum[:, b + 1, :], ones[:, :], inv[:, :], start=True, stop=True), after=[td, tv])
            state["inv_read"] = ti
            invp = psum[:, b + 1, :]
            toks = []
            used = [None, None]
            for j in range(KD):
                if not split:
                    toks.append([dve.do(lambda e, j=j: e.scalar_tensor_tensor(dst[:, j, :], xT[:, j, :], gain(j), invp, ALU.mult, ALU.mult),
                                        after=[ti, x_ready[j], tsum, f])])
                    continue
                s = j % 2
                td = dve.do(lambda e, j=j, s=s: e.scalar_tensor_tensor(tmp[:, s, :], xT[:, j, :], gain(j), invp, ALU.mult, ALU.mult),
                            after=[ti, used[s], f, state.get("gain")])
                high, low = dst
                if shift is None:
                    th = act.do(lambda e, j=j, s=s: e.copy(high[:, j, :], tmp[:, s, :]), after=[td, old_reads])
                    tl = dve.do(lambda e, j=j, s=s: e.tensor_tensor(low[:, j, :], tmp[:, s, :], high[:, j, :].bitcast(F32), ALU.subtract),
                                after=[th, td, old_reads])
                else:
                    th = act.do(lambda e, j=j, s=s: e.activation(high[:, j, :], tmp[:, s, :], ACT.Identity, bias=shift(j)), after=[td, old_reads])
                    tl = dve.do(lambda e, j=j, s=s: e.scalar_tensor_tensor(low[:, j, :], tmp[:, s, :], shift(j), high[:, j, :].bitcast(F32),
                                                                           ALU.add, ALU.subtract), after=[th, td, old_reads])
                used[s] = tl
                toks.append([th, tl])
            free_pair(b, [td if split else toks[-1][0]])
            return toks

        def split_into(X, j, src, after, old_reads, parts=slice(0, P)):
            th = act.do(lambda e: e.copy(X[0][parts, j, :], src), after=[after, old_reads])
            tl = dve.do(lambda e: e.tensor_tensor(X[1][parts, j, :], src, X[0][parts, j, :].bitcast(F32), ALU.subtract),
                        after=[th, after, old_reads])
            return [th, tl]

        gs = sb("gain_in", [P, KD])
        gg = sb("gain_out", [P, KD])

        def gains(layer, sub, weight):
            m = mods[layer]
            o = 3 * sub * KD
            need = [state.get(("mod", layer, sub, part)) for part in range(2)]
            state["gain"] = dve.do(lambda e: e.scalar_tensor_tensor(gs[:, :], m[:, o + KD:o + 2 * KD], 1.0, v("norm_g", (3 * layer + sub) * KD, KD),
                                                                    ALU.add, ALU.mult), after=[need, state["vec"], dve.last()])

            def gate():
                assert stream.plan is None or ("mod", layer, sub, 2) in state
                state["gate"] = dve.do(lambda e: e.tensor_scalar(gg[:, :], m[:, o + 2 * KD:o + 3 * KD], 1.0, weight, ALU.add, ALU.mult),
                                       after=[state.get(("mod", layer, sub, 2)), dve.last()])
                return lambda j: gg[:, j:j + 1]
            return (lambda j: gs[:, j:j + 1]), (lambda j: m[:, o + j:o + j + 1]), gate

        def add_to_x(base, tok, j0, gate, x_ready):
            toks = []
            for m in range(2):
                j = j0 + m
                if gate is None:
                    td = dve.do(lambda e, m=m, j=j: e.tensor_tensor(xT[:, j, :], xT[:, j, :], psum[:, base + m, :], ALU.add),
                                after=[tok, x_ready[j]])
                else:
                    td = dve.do(lambda e, m=m, j=j: e.scalar_tensor_tensor(xT[:, j, :], psum[:, base + m, :], gate(j), xT[:, j, :],
                                                                           ALU.mult, ALU.add), after=[tok, x_ready[j], state["gate"]])
                x_ready[j] = [td]
                toks.append(td)
            free_pair(base, toks)

        def project_back(X, ready, w, row0, nk, gate, x_ready):
            for c in range(D // PANEL):
                src = w[row0:row0 + nk * P, c * PANEL:(c + 1) * PANEL]
                base, tok = product(X, ready, [piece(src, nk)], range(nk), PANEL, None)
                add_to_x(base, tok, 2 * c, gate, x_ready)
            return tok

        def ffn(layer, which, sub, x_ready):
            gain, shift, out_gain = gains(layer, sub, 0.5)
            hr = norm(x_ready, H, gain, shift, old_reads=fence())
            state["area_free"] = fence()
            gate = None
            w_gu, w_down = t["ffn_w_gu"][layer, which], t["ffn_w_down"][layer, which]
            f = fence()
            c = Carver()
            c.at = 5 * S
            sil = [c.new(S) for _ in range(4)]
            prod = [c.new(S) for _ in range(4)]
            sil_free, prod_free = [None] * 4, [None] * 4
            n = 0
            y_reads = f
            for row in range(0, FF // P, KD):
                nk = min(KD, FF // P - row)
                yr = []
                for c0 in range(row, row + nk, 2):
                    bg, tg = product(H, hr, [piece(w_gu[:, c0 * P:c0 * P + PANEL], KD)], range(KD), PANEL, None)
                    bu, tu = product(H, hr, [piece(w_gu[:, FF + c0 * P:FF + c0 * P + PANEL], KD)], range(KD), PANEL, None)
                    gt, ut = [], []
                    for m in range(2):
                        s = n % 4
                        n += 1
                        a1 = act.do(lambda e, m=m, s=s: e.activation(sil[s], psum[:, bg + m, :], ACT.Silu), after=[tg, sil_free[s], f])
                        d1 = dve.do(lambda e, m=m, s=s: e.tensor_tensor(prod[s], sil[s], psum[:, bu + m, :], ALU.mult),
                                    after=[a1, tu, prod_free[s], f])
                        sil_free[s] = d1
                        both = split_into(Y, c0 - row + m, prod[s], d1, y_reads)
                        prod_free[s] = both
                        gt.append(a1)
                        ut.append(d1)
                        yr.append(both)
                    free_pair(bg, gt)
                    free_pair(bu, ut)
                gate = gate or out_gain()
                y_reads = [project_back(Y, yr, w_down, row * P, nk, gate, x_ready)]

        def stick_breaking(x_ready):
            gain, shift, out_gain = gains(0, 1, 1.0)
            hr = norm(x_ready, H, gain, shift, old_reads=fence())
            w_qkv, w_o = t["sb_w_qkv"][0], t["sb_w_o"][0]
            G = 4
            f = fence()
            c = Carver()
            c.at = 0
            q, k, vv = c.new(G, S), c.new(G, S), c.new(NT, G * P)
            tmp = [c.new(TRI) for _ in range(3)]
            sp_ = [c.new(TRI) for _ in range(2)]
            yr = [None] * KD
            for g in range(KD // G):
                f = fence()
                ready = {}
                for part, dst in ((0, q), (1, k)):
                    for c0 in range(0, G, 2):
                        src = w_qkv[:, part * D + (g * G + c0) * P:part * D + (g * G + c0) * P + PANEL]
                        base, tok = product(H, hr, [piece(src, KD)], range(KD), PANEL, None)
                        ta = act.do(lambda e, dst=dst, c0=c0, base=base, part=part: e.mul(dst[:, c0:c0 + 2, :], psum[:, base:base + 2, :],
                                                                                      SCALE if part == 0 else 1.0), after=[tok, f])
                        free_pair(base, [ta])
                        ready[part, c0] = ready[part, c0 + 1] = ta
                for c0 in range(0, G, 2):
                    src = w_qkv[:, 2 * D + (g * G + c0) * P:2 * D + (g * G + c0) * P + PANEL]
                    base, view, tok = product_tok(H, hr, [piece(src, KD)], PANEL)
                    ta = act.do(lambda e, c0=c0, view=view: e.copy(vv[:, :, c0 * P:c0 * P + PANEL], view), after=[tok, f])
                    free_pair(base, [ta])
                    ready[2, c0] = ready[2, c0 + 1] = ta
                zfree = [f, f]
                tmp_free, sp_free = [f, f, f], [f, f]
                o_free = {6: bank_free[6], 7: bank_free[7]}
                act.do(lambda e: e.preload_act_table_set("natural_log_exp_and_others"), signal=False)
                banks_before = [bank_free[b] for b in range(8)]
                st = {}

                def scores(h):
                    s, ti, r0 = h % 2, h // 2, (h % 2) * HD
                    for i in range(NT):
                        tz = pe.do(lambda e, i=i: e.matmul(
                            flat[:, s * 1536 + COL_AT[i]:s * 1536 + COL_AT[i] + S - P * i],
                            k[r0:r0 + HD, ti, i * P:(i + 1) * P], q[r0:r0 + HD, ti, i * P:S],
                            start=(i != 3), stop=True, skip_group_check=True),
                            after=[zfree[s], banks_before, ready[0, ti], ready[1, ti]], signal=i == NT - 1)
                    z = flat[:, s * 1536:s * 1536 + TRI]
                    a0 = act.do(lambda e: e.activation(tmp[h % 3], z, ACT.Abs), after=[tz, tmp_free[h % 3]])
                    a1 = act.do(lambda e: e.activation(tmp[h % 3], tmp[h % 3], ACT.Exp, scale=-1.0), after=[a0])
                    a2 = act.do(lambda e: e.activation(tmp[h % 3], tmp[h % 3], ACT.Ln, bias=1.0), after=[a1])
                    d2 = dve.do(lambda e: e.scalar_tensor_tensor(sp_[s], z, 0.0, tmp[h % 3], ALU.max, ALU.add), after=[a2, tz, sp_free[s]])
                    for i in range(NT):
                        blk = sp_[s][:, COL_AT[i]:COL_AT[i] + P]
                        tm = pool.do(lambda e, blk=blk: e.affine_select(out=blk, in_=blk, pattern=[[1, P]], compare_op=ALU.is_gt, fill=0.0,
                                                                        base=0, channel_multiplier=-1), after=[d2])
                    st[h] = (tm, d2)

                def weigh(h):
                    s, ti, r0 = h % 2, h // 2, (h % 2) * HD
                    tm, d2 = st[h]
                    for i in range(NT):
                        for j in range(i, NT):
                            o = s * 1536 + COL_AT[i] + P * (j - i)
                            tc = pe.do(lambda e, i=i, j=j, o=o: e.matmul(
                                flat[:, o:o + S - P * j], neg_tri[:, :] if i == j else neg_ones[:, :],
                                sp_[s][:, COL_AT[j]:COL_AT[j] + S - P * j], start=False, stop=True, skip_group_check=True),
                                after=[tm, d2], signal=(i, j) == (NT - 1, NT - 1))
                    sp_free[s] = tc
                    a1 = act.do(lambda e: e.activation(tmp[h % 3], flat[:, s * 1536:s * 1536 + TRI], ACT.Exp), after=[tc, d2])
                    zfree[s] = a1
                    for i in range(NT):
                        blk = tmp[h % 3][:, COL_AT[i]:COL_AT[i] + P]
                        tm = pool.do(lambda e, blk=blk: e.affine_select(out=blk, in_=blk, pattern=[[1, P]], compare_op=ALU.is_gt, fill=0.0,
                                                                        base=0, channel_multiplier=-1), after=[a1])
                    st[h] = (tm, a1)

                def values(h):
                    ti, r0 = h // 2, (h % 2) * HD
                    tm, a1 = st[h]
                    ob = 6 + ti % 2
                    for i in range(NT):
                        to = pe.do(lambda e, i=i: e.matmul(
                            psum[r0:r0 + HD, ob, i * P:S], vv[:, i, ti * P + r0:ti * P + r0 + HD], tmp[h % 3][:, COL_AT[i]:COL_AT[i] + S - P * i],
                            start=(i == 0), stop=(i == NT - 1), skip_group_check=True), after=[tm, a1, ready[2, ti], o_free[ob]], signal=i == NT - 1)
                    tmp_free[h % 3] = to
                    if h % 2:
                        yr[g * G + ti] = split_into(Y, g * G + ti, psum[:, ob, :], to, f)
                        o_free[ob] = yr[g * G + ti]

                scores(0)
                for h in range(2 * G + 2):
                    if h >= 2:
                        values(h - 2)
                    if h + 1 < 2 * G:
                        scores(h + 1)
                    if h < 2 * G:
                        weigh(h)
                end = fence()
                for b in range(8):
                    bank_free[b] = end
            state["area_free"] = fence()
            project_back(Y, yr, w_o, 0, KD, out_gain(), x_ready)

        def rglru(x_ready):
            gain, shift, out_gain = gains(1, 1, 1.0)
            hr = norm(x_ready, H, gain, shift, old_reads=fence())
            state["area_free"] = fence()
            gate = out_gain()
            w_in, w_out = t["lru_w_in"][0], t["lru_w_out"][0]
            stream.low_by = pool
            NB = RNN // P
            f = fence()
            c = Carver()
            c.at = 2 * S
            w_r, w_i = c.new(NB, P), c.new(NB, P)
            gel, xcs = [c.new(2, S) for _ in range(2)], [c.new(2, S) for _ in range(2)]
            rr, ii, aa, th = (c.new(2, S) for _ in range(4))
            xpad = c.new(2, S + 3)
            sp.load(w_r, t["lru_w_r"][0].rearrange("n k j -> k n j"), s_gate_w, counts, after=[f])
            tw = sp.load(w_i, t["lru_w_i"][0].rearrange("n k j -> k n j"), s_gate_w, counts, after=[f])
            tz = dve.do(lambda e: e.memset(xpad[:, :, 0:3], 0.0), after=[f])
            y_reads = f
            free = {}
            front = {}

            def project_in(n0):
                base, tok = product(H, hr, [piece(w_in[:, n0 * P:n0 * P + PANEL], KD)], range(KD), PANEL, None)
                tg = act.do(lambda e: e.activation(gel[n0 // 2 % 2], psum[:, base:base + 2, :], ACT.Gelu_apprx_tanh),
                            after=[tok, f, free.get(("gel", n0 // 2 % 2))])
                free_pair(base, [tg])
                base, tok = product(H, hr, [piece(w_in[:, RNN + n0 * P:RNN + n0 * P + PANEL], KD)], range(KD), PANEL, None)
                tx = act.do(lambda e: e.copy(xpad[:, :, 3:S + 3], psum[:, base:base + 2, :]), after=[tok, f, free.get("xpad")])
                free_pair(base, [tx])
                xc = xcs[n0 // 2 % 2]
                tds = []
                for m in range(2):
                    n = n0 + m
                    td = dve.do(lambda e: e.tensor_scalar(xc[:, m, :], xpad[:, m, 0:S], v("lru_conv_w", n), v("lru_conv_b", n), ALU.mult, ALU.add),
                                after=[tx, tz, free.get(("xc", n0 // 2 % 2))])
                    for tap in range(1, 4):
                        td = dve.do(lambda e: e.scalar_tensor_tensor(xc[:, m, :], xpad[:, m, tap:tap + S], v("lru_conv_w", tap * NB + n), xc[:, m, :],
                                                                     ALU.mult, ALU.add), after=[td])
                    tds.append(td)
                free["xpad"] = td
                front[n0] = (tg, tds)

            def recur(n0, part0, yr, y_reads):
                tg, tds = front[n0]
                xc, gl = xcs[n0 // 2 % 2], gel[n0 // 2 % 2]
                br, fr = take_pair()
                bi, fi = take_pair()
                sig = []
                for m in range(2):
                    n = n0 + m
                    tr = pe.do(lambda e: e.matmul(psum[:, br + m, :], w_r[:, n, :], xc[:, m, :], start=True, stop=True), after=[tds[m], tw, fr])
                    ts = pe.do(lambda e: e.matmul(psum[:, bi + m, :], w_i[:, n, :], xc[:, m, :], start=True, stop=True), after=[tds[m], tw, fi])
                    s1 = act.do(lambda e: e.activation(rr[:, m, :], psum[:, br + m, :], ACT.Sigmoid, bias=v("lru_b_r", n)), after=[tr, free.get("rr")])
                    s2 = act.do(lambda e: e.activation(ii[:, m, :], psum[:, bi + m, :], ACT.Sigmoid, bias=v("lru_b_i", n)), after=[ts, free.get("ii")])
                    sig.append((s1, s2))
                free_pair(br, [s1])
                free_pair(bi, [s2])
                e2 = []
                for m in range(2):
                    n = n0 + m
                    a1 = act.do(lambda e: e.activation(aa[:, m, :], rr[:, m, :], ACT.Exp, scale=v("decay", n)),
                                after=[sig[m][0], state["decay"], free.get("aa")])
                    a2 = act.do(lambda e: e.activation(th[:, m, :], rr[:, m, :], ACT.Tanh, scale=v("decay", n)), after=[sig[m][0], free.get("th")])
                    e2.append((a1, a2))
                d1 = act.do(lambda e: e.activation(rr, aa, ACT.Square), after=[e2[0][0], e2[1][0], e2[1][1]])
                d2 = dve.do(lambda e: e.scalar_tensor_tensor(th, rr, 1.0, th, ALU.add, ALU.mult), after=[d1, e2[1][1]])
                a3 = act.do(lambda e: e.activation(th, th, ACT.Sqrt, scale=-1.0), after=[d2])
                p1 = pool.do(lambda e: e.tensor_tensor(ii, ii, xc, ALU.mult), after=[sig[1][1], tds])
                free["xc", n0 // 2 % 2] = [p1, ts]
                d3 = dve.do(lambda e: e.tensor_tensor(ii, ii, th, ALU.mult), after=[p1, a3])
                for m in range(2):
                    d4 = dve.do(lambda e: e.tensor_tensor_scan(rr[:, m, :], aa[:, m, :], ii[:, m, :], 0.0, ALU.mult, ALU.add), after=[d3])
                free["aa"] = free["ii"] = d4
                free["th"] = d3
                d5 = pool.do(lambda e: e.tensor_tensor(rr, rr, gl, ALU.mult), after=[d4, tg])
                free["gel", n0 // 2 % 2] = d5
                for m in range(2):
                    both = split_into(Y, n0 - part0 + m, rr[:, m, :], d5, y_reads)
                    yr.append(both)
                free["rr"] = both

            project_in(0)
            for part0 in range(0, NB, KD):
                nk = min(KD, NB - part0)
                yr = []
                for n0 in range(part0, part0 + nk, 2):
                    if n0 + 2 < NB:
                        project_in(n0 + 2)
                    recur(n0, part0, yr, y_reads)
                state["area_free"] = fence()
                y_reads = [project_back(Y, yr, w_out, part0 * P, nk, gate, x_ready)]
            stream.low_by = dve

        IN = {}
        off = 0
        for name, n in (("a_q", 384), ("a_k", 384), ("a_v", 384), ("a_g", 384), ("b_q", 384), ("b_k", 64), ("b_v", 64), ("b_g", 384),
                        ("i_q", 256), ("i_k", 64), ("i_w", 4), ("c_q", 768), ("c_k", 768), ("c_v", 768), ("c_g", 256), ("m_g", 3 * D)):
            IN[name] = off
            off += n

        def hybrid(layer, x_ready):
            hr = norm(x_ready, H, lambda j: v("norm_g_2", layer * KD + j), old_reads=fence())
            w_in = t["w_in_2"][layer]
            stream.low_by = pool
            c = Carver()
            rope_x, rope_y = c.new(2, S), c.new(2, S)
            SS = [c.new(TRI) for _ in range(2)] + [area[:, 0:TRI]]
            PT = c.new(TRI)
            maskc, stat = mod_acc[:, 0:7 * P], mod_acc[:, 7 * P:7 * P + 48]
            keep = c.at

            rope_free = {"x": fence(), "y": fence()}

            def columns(name, c0, n, widths):
                o = IN[name] + c0
                return product(H, hr, [piece(w_in[:, o:o + n], KD)], range(KD), n, None, widths)

            def rope(base, tok, dst, parts=P, n=2, after=(), dil=1):
                ta = act.do(lambda e: e.copy(rope_x[0:parts, 0:n, :], psum[0:parts, base:base + n, :]), after=[tok, rope_free["x"]])
                for r in range(0, parts, 64):
                    for a, b in ((r, r + 32), (r + 32, r)):
                        tswap = sp.load(rope_y[a:a + 32, 0:n, :], rope_x[b:b + 32, 0:n, :], s_swap, counts, after=[ta, rope_free["y"]])

                def split_tokens(ap):
                    return ap if dil == 1 else ap.rearrange("p (j r) -> p j r", r=dil)

                def to(m):
                    a = dst[0:parts, m, :]
                    return a if dil == 1 else a.rearrange("p (r j) -> p j r", r=dil)
                for m in range(n):
                    eng = pool if m == 0 else dve
                    t1 = eng.do(lambda e, m=m: e.tensor_tensor(to(m), split_tokens(rope_x[0:parts, m, :]), split_tokens(rope_c[0:parts, :]), ALU.mult),
                                after=[ta, tswap, after])
                    t2 = dve.do(lambda e, m=m: e.tensor_tensor(rope_y[0:parts, m, :], rope_y[0:parts, m, :], rope_s[0:parts, :], ALU.mult),
                                after=[tswap])
                    t3 = dve.do(lambda e, m=m: e.tensor_tensor(to(m), to(m), split_tokens(rope_y[0:parts, m, :]), ALU.add),
                                after=[t1, t2])
                rope_free["x"] = [t1, t3, tswap]
                rope_free["y"] = t3
                return [ta, t3]

            def roped(name, c0, n, widths, dst, after, dil=1):
                base, tok = columns(name, c0, n, widths)
                r = rope(base, tok, dst, n=len(widths), after=after, dil=dil)
                free_pair(base, [r[0]])
                return r[1]

            def token_major(name, c0, n, dst, after):
                o = IN[name] + c0
                base, view, tok = product_tok(H, hr, [piece(w_in[:, o:o + n], KD)], n)
                ta = act.do(lambda e: e.copy(dst, view), after=[tok, after])
                free_pair(base, [ta])
                return ta

            def gate_tiles(name, c0, n, dst, after):
                widths = (P,) * (n // P)
                base, tok = columns(name, c0, n, widths)
                m = len(widths)
                ta = act.do(lambda e: e.activation(dst[:, 0:m, :], psum[:, base:base + m, :], ACT.Sigmoid), after=[tok, after])
                td = dve.do(lambda e: e.tensor_tensor(dst[:, 0:m, :], dst[:, 0:m, :], psum[:, base:base + m, :], ALU.mult), after=[ta])
                free_pair(base, [td])
                return td

            def softmax_heads(heads):
                act.do(lambda e: e.preload_act_table_set("natural_log_exp_and_others"), signal=False)
                begin = fence()
                banks = [list(x) for x in bank_free]
                s_free = [begin, begin, begin]
                scores_read = [begin]
                pt_free = [begin]
                got, peak, weights, turned = {}, {}, {}, {}

                def spans(rows):
                    out = []
                    for a, b, n in rows:
                        step = (b - a) // n
                        out += [(a + u * step, a + (u + 1) * step) for u in range(n)]
                    return list(enumerate(out))

                def do_scores(h):
                    got[h] = heads[h][0]([scores_read[0], banks])

                def do_max(h):
                    _, lo, hi, mask, rows, _, _, _ = heads[h]
                    s, buf, m0 = h % 3, SS[h % 3], 16 * (h % 3)
                    d = dve.do(lambda e: e.scalar_tensor_tensor(buf[:, lo:hi], flat[:, lo:hi], SCALE, mask[0], ALU.mult, ALU.add),
                               after=[got[h], s_free[s], mask[1]])
                    scores_read[0] = d
                    i = 0
                    for a, b, n in rows:
                        dm = dve.do(lambda e: e.tensor_reduce(stat[:, m0 + i:m0 + i + n], buf[:, a:b].rearrange("p (n c) -> p n c", n=n), AX.X, ALU.max),
                                    after=[d, s_free[s]])
                        i += n
                    peak[h] = dve.do(lambda e: e.tensor_scalar(stat[:, m0 + 4:m0 + 8], stat[:, m0:m0 + 4], -1.0, None, ALU.mult), after=[dm, s_free[s]])

                def do_weights(h):
                    rows = heads[h][4]
                    buf, m0 = SS[h % 3], 16 * (h % 3)
                    for w, (a, b) in spans(rows):
                        ta = act.do(lambda e: e.activation(buf[:, a:b], buf[:, a:b], ACT.Exp, bias=stat[:, m0 + 4 + w:m0 + 5 + w],
                                                           accum_out=stat[:, m0 + 8 + w:m0 + 9 + w]), after=[peak[h]])
                    dr = dve.do(lambda e: e.reciprocal(stat[:, m0 + 12:m0 + 16], stat[:, m0 + 8:m0 + 12]), after=[ta])
                    for w, (a, b) in spans(rows):
                        dn = dve.do(lambda e: e.tensor_scalar(buf[:, a:b], buf[:, a:b], stat[:, m0 + 12 + w:m0 + 13 + w], None, ALU.mult), after=[dr])
                    weights[h] = dn

                def do_turns(h):
                    turns = heads[h][5]
                    buf = SS[h % 3]
                    for src, dst in turns:
                        tt = pe.do(lambda e: e.transpose(flat[:, 1536 + dst:1536 + dst + P], buf[:, src:src + P], ident[:, :]),
                                   after=[weights[h], pt_free[0]], signal=(src, dst) == turns[-1])
                    turned[h] = tt

                def do_values(h):
                    turns, outs, finish = heads[h][5:]
                    top = max(d for _, d in turns) + P
                    ta = act.do(lambda e: e.copy(PT[:, 0:top], flat[:, 1536:1536 + top]), after=[turned[h], pt_free[0]])
                    to = outs(ta)
                    pt_free[0] = to
                    s_free[h % 3] = [turned[h], finish(h % 3, to)]

                n_heads = len(heads)
                do_scores(0)
                for i in range(n_heads + 2):
                    if i >= 2:
                        do_turns(i - 2)
                    if i < n_heads:
                        do_max(i)
                    if i + 1 < n_heads:
                        do_scores(i + 1)
                    if 1 <= i <= n_heads:
                        do_weights(i - 1)
                    if i >= 2:
                        do_values(i - 2)
                end = fence()
                for b in range(8):
                    bank_free[b] = end
                rope_free["x"] = rope_free["y"] = end

            yr = [None] * KD
            y_old = fence()
            ROWS = [(ROW_AT[n], ROW_AT[n] + P * (n + 1), 1) for n in (0, 1, 2, 3)]
            TURNS = [(ROW_AT[n] + P * kt, COL_AT[kt] + P * (n - kt)) for kt in (0, 1, 3, 2) for n in range(kt, NT)]

            def causal_heads(y0, q, k_of, v_of, n_heads, mask, ready, gates):
                heads = []
                o_free = {6: [], 7: []}
                for h in range(n_heads):
                    ti, r0 = h // 2, (h % 2) * HD
                    ob = 6 + ti % 2

                    def scores(after, ti=ti, r0=r0, h=h):
                        for n in range(NT):
                            tok = pe.do(lambda e, n=n: e.matmul(flat[:, ROW_AT[n]:ROW_AT[n] + P * (n + 1)], q[r0:r0 + HD, ti, n * P:(n + 1) * P],
                                                                k_of(h)[:, 0:P * (n + 1)], start=True, stop=True),
                                        after=[after, ready], signal=n == NT - 1)
                        return tok

                    def outs(ta, ti=ti, r0=r0, h=h, ob=ob):
                        for kt in range(NT):
                            tok = pe.do(lambda e, kt=kt: e.matmul(psum[r0:r0 + HD, ob, kt * P:S], v_of(h, kt),
                                                                  PT[:, COL_AT[kt]:COL_AT[kt] + S - P * kt], start=kt == 0, stop=kt == NT - 1,
                                                                  skip_group_check=True),
                                        after=[ta, ready, o_free[ob]], signal=kt == NT - 1)
                        return tok

                    def finish(s, to, ti=ti, h=h, ob=ob):
                        if h % 2 == 0:
                            return None
                        d = dve.do(lambda e: e.tensor_tensor(gates[:, ti, :], gates[:, ti, :], psum[:, ob, :], ALU.mult), after=[to, ready])
                        o_free[ob] = [d]
                        yr[y0 + ti] = split_into(Y, y0 + ti, gates[:, ti, :], d, y_old)
                        return None

                    heads.append((scores, 0, TRI, mask, ROWS, TURNS, outs, finish))
                softmax_heads(heads)

            c.at = keep
            score = c.new(TRI)
            shared = c.at
            ag, aq, ak, av = c.new(3, S), c.new(3, S), c.new(3, S), c.new(NT, 3 * P)
            iq, ik = ag[:, 0:2, :], ag[:, 2:3, :]
            iwT, best = small[:, 2:2 + 4 * NT].rearrange("p (n h) -> p n h", n=NT), small[:, 24:56]
            f = fence()
            t_iq = roped("i_q", 0, 256, (P, P), iq, f)
            base, tok = columns("i_k", 0, 68, (68,))
            r = rope(base, tok, ik, parts=64, n=1, after=f)
            t_iw = act.do(lambda e: e.mul(SS[0][64:68, 0:S], psum[64:68, base, :], 1.0 / 16.0), after=[tok, f])
            free_pair(base, [r[0], t_iw])
            t_ik = sp.load(ik[64:P, :, :], ik[0:64, :, :], s_dup, counts, after=[r[1], f])
            ra = [roped("a_q", 0, 256, (P, P), aq, f)]
            b0, fr = take_pair()
            for n in range(NT):
                tt = pe.do(lambda e: e.transpose(psum[:, b0, 4 * n:4 * n + 4], SS[0][64:68, n * P:(n + 1) * P], ident[64:68, 64:68]),
                           after=[t_iw, fr], signal=n == NT - 1)
            t_iw = act.do(lambda e: e.copy(iwT, psum[:, b0, 0:16].rearrange("p (n h) -> p n h", n=NT)), after=[tt, f])
            free_pair(b0, [t_iw])
            f2 = fence()
            relu_read = [f2, f2]
            relu_done = [f2, f2]
            for h in range(4):
                g, r0 = h % 2, (h % 2) * HD
                relu = SS[g]
                for n in range(NT):
                    tp = pe.do(lambda e: e.matmul(
                        flat[:, 1536 * g + ROW_AT[n]:1536 * g + ROW_AT[n] + P * (n + 1)], iq[r0:r0 + HD, h // 2, n * P:(n + 1) * P],
                        ik[r0:r0 + HD, 0, 0:P * (n + 1)], start=True, stop=True),
                        after=[t_iq, t_ik, r[1], relu_done[g]], signal=n == NT - 1)
                ta = act.do(lambda e: e.activation(relu, flat[:, 1536 * g:1536 * g + TRI], ACT.Relu), after=[tp, relu_read[g]])
                relu_done[g] = ta
                for n in range(NT):
                    a, b = ROW_AT[n], ROW_AT[n] + P * (n + 1)
                    if h == 0:
                        td = dve.do(lambda e: e.tensor_scalar(score[:, a:b], relu[:, a:b], iwT[:, n, h:h + 1], None, ALU.mult), after=[ta, t_iw, f])
                    else:
                        td = dve.do(lambda e: e.scalar_tensor_tensor(score[:, a:b], relu[:, a:b], iwT[:, n, h:h + 1], score[:, a:b],
                                                                     ALU.mult, ALU.add), after=[ta, td])
                relu_read[g] = td
            index_read = tp
            for b in range(6):
                bank_free[b] = [relu_done[b // 3]]
            for n in range(1, NT):
                b = ROW_AT[n] + P * (n + 1)
                blk = score[:, b - P:b]
                tm = pool.do(lambda e: e.affine_select(out=blk, in_=blk, pattern=[[-1, P]], compare_op=ALU.is_ge, fill=NOT_CAUSAL,
                                                       base=0, channel_multiplier=1), after=[td])
            picked = {}

            def top8(n):
                a, b = ROW_AT[n], ROW_AT[n] + P * (n + 1)
                m8 = best[:, 8 * n:8 * n + 8]
                d1 = dve.do(lambda e: e.max(m8, score[:, a:b]), after=[picked.get(n), tm, td])
                picked[n] = dve.do(lambda e: e.match_replace(score[:, a:b], m8, score[:, a:b], PICKED), after=[d1])

            rounds = [n for _ in range(P // 8) for n in range(1, NT)]

            def some(n):
                for _ in range(min(n, len(rounds))):
                    top8(rounds.pop(0))

            some(6)
            base, tok = columns("a_q", 256, 256, (P, P))
            r1 = rope(base, tok, aq[:, 2:3, :], n=1, after=f)
            r2 = rope(base + 1, tok, ak[:, 0:1, :], n=1, after=f)
            free_pair(base, [r2[0]])
            some(7)
            ra += [r1[1], r2[1], roped("a_k", 128, 256, (P, P), ak[:, 1:3, :], f)]
            some(7)
            ra.append(token_major("a_v", 0, 256, av[:, :, 0:256], f))
            some(8)
            ra.append(token_major("a_v", 256, 128, av[:, :, 256:384], f))
            some(6)
            ra.append(gate_tiles("a_g", 0, 256, ag, [f, index_read]))
            some(8)
            ra.append(gate_tiles("a_g", 256, 128, ag[:, 2:3, :], [f, index_read]))
            some(len(rounds))
            for n in range(1, NT):
                a, b = ROW_AT[n], ROW_AT[n] + P * (n + 1)
                tsel = dve.do(lambda e: e.tensor_scalar(score[:, a:b], score[:, a:b], PICKED_BELOW, MASKED, ALU.is_ge, ALU.mult), after=[picked[n]])
            a, b = ROW_AT[0], ROW_AT[0] + P
            tsel = dve.do(lambda e: e.tensor_copy(score[:, a:b], causal[:, a:b]), after=[tsel, state["masks"]])
            causal_heads(0, aq, lambda h: ak[(h % 2) * HD:(h % 2) * HD + HD, h // 2, :], lambda h, kt: av[:, kt, h * HD:(h + 1) * HD], 6,
                         (causal[:, :], [state["masks"]]), ra, ag)

            c.at = shared
            bg, bq, bk, bv = c.new(3, S), c.new(3, S), c.new(1, S), c.new(NT, HD)
            f = fence()
            t_bq = roped("b_q", 0, 256, (P, P), bq, f)
            base, tok = columns("b_q", 256, 192, (P, 64))
            r1 = rope(base, tok, bq[:, 2:3, :], n=1, after=f)
            r2 = rope(base + 1, tok, bk, parts=64, n=1, after=f)
            free_pair(base, [r2[0]])
            t_bk = sp.load(bk[64:P, :, :], bk[0:64, :, :], s_dup, counts, after=[r2[1], f])
            t_bv = token_major("b_v", 0, 64, bv, f)
            t_g1 = gate_tiles("b_g", 0, 256, bg, f)
            t_g2 = gate_tiles("b_g", 256, 128, bg[:, 2:3, :], f)
            causal_heads(3, bq, lambda h: bk[(h % 2) * HD:(h % 2) * HD + HD, 0, :], lambda h, kt: bv[:, kt, :], 6,
                         (score, [tsel]), [t_bq, r1[1], r2[1], t_bk, t_bv, t_g1, t_g2], bg)

            c.at = keep
            og = [c.new(2, S) for _ in range(3)]
            lse = [c.new(NT, 4) for _ in range(3)]
            rows_at = c.at
            for g, dil in enumerate((1, 4, 16)):
                c.at = rows_at
                cq, ck, cv = c.new(2, S), c.new(2, S), c.new(NT, PANEL)
                f = fence()
                vt = []
                tq = roped("c_q", g * PANEL, PANEL, (P, P), cq, f, dil)
                tk = roped("c_k", g * PANEL, PANEL, (P, P), ck, f, dil)
                if g == 0:
                    tv = token_major("c_v", 0, PANEL, cv, f)
                else:
                    base, tok = columns("c_v", g * PANEL, PANEL, (P, P))
                    for m in range(2):
                        ta = act.do(lambda e, base=base, m=m: e.copy(rope_x[:, m, :].rearrange("p (r j) -> p r j", r=dil),
                                                                     psum[:, base + m, :].rearrange("p (j r) -> p r j", r=dil)),
                                    after=[tok, rope_free["x"]])
                    free_pair(base, [ta])
                    base, fr = take_pair()
                    for m in range(2):
                        for r_ in range(NT):
                            o = (base + r_ // 2) * 512 + (r_ % 2) * PANEL + m * P
                            tt = pe.do(lambda e, m=m, r_=r_, o=o: e.transpose(flat[:, o:o + P], rope_x[:, m, r_ * P:(r_ + 1) * P], ident[:, :]),
                                       after=[ta, fr], signal=(m, r_) == (1, NT - 1))
                    tv = act.do(lambda e, base=base: e.copy(cv, flat[:, base * 512:(base + 2) * 512].rearrange("p (t c) -> p t c", c=PANEL)),
                                after=[tt, f])
                    rope_free["x"] = tt
                    free_pair(base, [tv])
                if g == 0:
                    tm = pool.do(lambda e: e.memset(maskc[:, 0:7 * P], 0.0), after=[f])
                    for u in range(7):
                        blk = maskc[:, u * P:(u + 1) * P]
                        own = u % 2 == 0
                        tm = pool.do(lambda e, blk=blk, own=own: e.affine_select(
                            out=blk, in_=blk, pattern=[[-1 if own else 1, P]], compare_op=ALU.is_ge, fill=MASKED, base=0,
                            channel_multiplier=1 if own else -1), after=[tm])
                else:
                    tm = pool.do(lambda e: e.memset(maskc[:, 0:4 * P], 0.0), after=[f])
                    tm = pool.do(lambda e: e.affine_select(out=maskc[:, 0:4 * P], in_=maskc[:, 0:4 * P], pattern=[[0, 4], [-1, P]],
                                                           compare_op=ALU.is_ge, fill=MASKED, base=0, channel_multiplier=1), after=[tm])
                    if g == 2:
                        n_sub = S // dil
                        for u in range(1, P // n_sub):
                            blk = maskc[:, 0:4 * P].rearrange("p (n c) -> p n c", n=4)[:, :, (u - 1) * n_sub:u * n_sub]
                            tm = pool.do(lambda e, blk=blk, u=u: e.affine_select(out=blk, in_=blk, pattern=[[0, 4], [0, n_sub]], compare_op=ALU.is_gt,
                                                                                 fill=MASKED, base=u * n_sub, channel_multiplier=-1), after=[tm])
                ready = [tq, tk, tv]
                heads = []
                o_free = {6: [], 7: []}
                for sl in range(4):
                    ti, r0 = sl // 2, (sl % 2) * HD
                    ob = 6 + ti

                    def scores(after, ti=ti, r0=r0, g=g, qq=cq, kk=ck):
                        for n in range(NT):
                            if g == 0:
                                lo = 0 if n == 0 else P * (2 * n - 1)
                                k0 = P * max(n - 1, 0)
                                for u in range(1 if n == 0 else 2):
                                    tok = pe.do(lambda e, n=n, lo=lo, k0=k0, u=u: e.matmul(
                                        flat[:, lo + u * P:lo + u * P + P], qq[r0:r0 + HD, ti, n * P:(n + 1) * P],
                                        kk[r0:r0 + HD, ti, k0 + u * P:k0 + u * P + P], start=True, stop=True), after=[after, ready])
                            else:
                                tok = pe.do(lambda e, n=n: e.matmul(
                                    flat[:, n * P:(n + 1) * P], qq[r0:r0 + HD, ti, n * P:(n + 1) * P],
                                    kk[r0:r0 + HD, ti, n * P:(n + 1) * P], start=True, stop=True), after=[after, ready])
                        return tok

                    def outs(ta, ti=ti, r0=r0, g=g, ob=ob, sl=sl, cv=cv):
                        for n in range(NT):
                            if g == 0:
                                terms = [(n, 2 * n * P)] + ([(n - 1, (2 * n - 1) * P)] if n else [])
                            else:
                                terms = [(n, n * P)]
                            for i, (kt, o) in enumerate(terms):
                                tok = pe.do(lambda e, n=n, kt=kt, o=o, i=i, last=len(terms) - 1: e.matmul(
                                    psum[r0:r0 + HD, ob, n * P:(n + 1) * P], cv[:, kt, sl * HD:(sl + 1) * HD], PT[:, o:o + P],
                                    start=i == 0, stop=i == last, skip_group_check=True), after=[ta, ready, o_free[ob]])
                        return tok

                    def finish(s, to, ti=ti, g=g, ob=ob, sl=sl, dil=dil):
                        m0 = 16 * s
                        ta = act.do(lambda e: e.activation(lse[g][:, :, sl], stat[:, m0 + 8:m0 + 12], ACT.Ln), after=[act.last()])
                        td = dve.do(lambda e: e.tensor_tensor(lse[g][:, :, sl], lse[g][:, :, sl], stat[:, m0:m0 + 4], ALU.add), after=[ta])
                        if sl % 2:
                            dst = og[g][:, ti, :]
                            src = psum[:, ob, :]
                            if dil > 1:
                                dst = dst.rearrange("p (j r) -> p r j", r=dil)
                                src = src.rearrange("p (r j) -> p r j", r=dil)
                            tc = act.do(lambda e: e.copy(dst, src), after=[to, f])
                            o_free[ob] = [tc]
                        return td

                    if g == 0:
                        rows = [(0, P, 1), (P, 7 * P, 3)]
                        turns = [(i * P, i * P) for i in range(7)]
                        heads.append((scores, 0, 7 * P, (maskc, [tm]), rows, turns, outs, finish))
                    else:
                        turns = [(i * P, i * P) for i in range(4)]
                        heads.append((scores, 0, 4 * P, (maskc[:, 0:4 * P], [tm]), [(0, 4 * P, 4)], turns, outs, finish))
                softmax_heads(heads)

            f = fence()
            c.at = rows_at
            cg = c.new(2, S)
            L = [c.new(S) for _ in range(3)]
            M = c.new(S)
            sel = c.new(2, P)
            t_cg = gate_tiles("c_g", 0, 256, cg, f)
            tm = pool.do(lambda e: e.memset(sel[0:4, :, :], 1.0), after=[f])
            tm = pool.do(lambda e: e.affine_select(out=sel[0:4, :, :], in_=sel[0:4, :, :], pattern=[[P, 2], [1, P]], compare_op=ALU.is_ge,
                                                   fill=0.0, base=0, channel_multiplier=-HD), after=[tm])
            tm = pool.do(lambda e: e.affine_select(out=sel[0:4, :, :], in_=sel[0:4, :, :], pattern=[[-P, 2], [-1, P]], compare_op=ALU.is_gt,
                                                   fill=0.0, base=HD, channel_multiplier=HD), after=[tm])
            lt = []
            for g, dil in enumerate((1, 4, 16)):
                b = g
                for n in range(NT):
                    tt = pe.do(lambda e, g=g, n=n, b=b: e.transpose(psum[0:4, b, n * P:(n + 1) * P], lse[g][:, n, :], ident[:, :]),
                               after=[f, bank_free[b]], signal=n == NT - 1)
                src, dst = psum[0:4, b, :], L[g][0:4, :]
                if dil > 1:
                    src = src.rearrange("p (r j) -> p r j", r=dil)
                    dst = dst.rearrange("p (j r) -> p r j", r=dil)
                ta = act.do(lambda e, src=src, dst=dst: e.copy(dst, src), after=[tt, f])
                bank_free[b] = [ta]
                lt.append(ta)
            l3 = [x[0:4, :] for x in L]
            mm = M[0:4, :]
            d = dve.do(lambda e: e.tensor_tensor(mm, l3[0], l3[1], ALU.max), after=[lt, f])
            d = dve.do(lambda e: e.tensor_tensor(mm, mm, l3[2], ALU.max), after=[d])
            es = []
            for g in range(3):
                dd = dve.do(lambda e, g=g: e.tensor_tensor(l3[g], l3[g], mm, ALU.subtract), after=[d])
                es.append(act.do(lambda e, g=g: e.activation(l3[g], l3[g], ACT.Exp), after=[dd]))
            d = dve.do(lambda e: e.tensor_tensor(mm, l3[0], l3[1], ALU.add), after=[es, dd])
            d = dve.do(lambda e: e.tensor_tensor(mm, mm, l3[2], ALU.add), after=[d])
            d = dve.do(lambda e: e.reciprocal(mm, mm), after=[d])
            for g in range(3):
                dd = dve.do(lambda e, g=g: e.tensor_tensor(l3[g], l3[g], mm, ALU.mult), after=[d])
            for m in range(2):
                base, fr = take_pair()
                prev = None
                for g in range(3):
                    b = base + g % 2
                    tp = pe.do(lambda e, g=g, m=m, b=b: e.matmul(psum[:, b, :], sel[0:4, m, :], l3[g], start=True, stop=True),
                               after=[dd, tm, fr, prev])
                    prev = dve.do(lambda e, g=g, m=m, b=b: e.tensor_tensor(og[g][:, m, :], og[g][:, m, :], psum[:, b, :], ALU.mult), after=[tp, f])
                free_pair(base, [prev])
                d1 = dve.do(lambda e, m=m: e.tensor_tensor(og[0][:, m, :], og[0][:, m, :], og[1][:, m, :], ALU.add), after=[prev])
                d1 = dve.do(lambda e, m=m: e.tensor_tensor(og[0][:, m, :], og[0][:, m, :], og[2][:, m, :], ALU.add), after=[d1])
                d1 = dve.do(lambda e, m=m: e.tensor_tensor(cg[:, m, :], cg[:, m, :], og[0][:, m, :], ALU.mult), after=[d1, t_cg])
                yr[6 + m] = split_into(Y, 6 + m, cg[:, m, :], d1, y_old)

            f = fence()
            c.at = 0
            merged = c.new(KD, S)
            sg = [c.new(2, S) for _ in range(3)]
            sg_free = [f, f, f]
            mt = []
            br_w = (t["w_br_a_2"][layer], t["w_br_b_2"][layer], t["w_br_c_2"][layer])
            chunks = (range(0, 3), range(3, 6), range(6, 8))
            for jj in range(KD // 2):
                st = []
                for b in range(3):
                    base, tok = columns("m_g", b * D + jj * PANEL, PANEL, (P, P))
                    ta = act.do(lambda e, b=b, base=base: e.activation(sg[b], psum[:, base:base + 2, :], ACT.Sigmoid), after=[tok, sg_free[b], f])
                    free_pair(base, [ta])
                    st.append(ta)
                (wh, wl), wt, done = stream.take([piece(w[:, jj * PANEL:(jj + 1) * PANEL], len(ch), off=ch[0] * PANEL) for w, ch in zip(br_w, chunks)])
                wv = [w[:, :RAW].rearrange("p (k n) -> p k n", n=PANEL) for w in (wh, wl)]
                dst = merged[:, 2 * jj:2 * jj + 2, :]
                for b in range(3):
                    base, free = take_pair()
                    for m in range(2):
                        for i, k in enumerate(chunks[b]):
                            for x, y in ((0, 0), (0, 1), (1, 0)):
                                end = (x, y) == (1, 0) and i == len(chunks[b]) - 1
                                tok = pe.do(lambda e, m=m, i=i, k=k, x=x, y=y, end=end, base=base: e.matmul(
                                    psum[:, base + m, :], wv[x][:, k, m * P:(m + 1) * P], Y[y][:, k, :], start=(i == 0 and (x, y) == (0, 0)), stop=end),
                                    after=[wt, yr[k], free], signal=end)
                    td = dve.do(lambda e, b=b, base=base: e.tensor_tensor(sg[b], sg[b], psum[:, base:base + 2, :], ALU.mult), after=[tok, st[b]])
                    free_pair(base, [td])
                    if b == 1:
                        td = dve.do(lambda e: e.tensor_tensor(dst, sg[0], sg[1], ALU.add), after=[td, f])
                    if b == 2:
                        td = dve.do(lambda e: e.tensor_tensor(dst, dst, sg[2], ALU.add), after=[td])
                done(tok)
                sg_free = [td, td, td]
                mt.append(td)
            old = fence()
            state["area_free"] = old
            mr = []
            for j in range(KD):
                mr.append(split_into(H, j, merged[:, j, :], mt[j // 2], old))
            project_back(H, mr, t["w_out_2"][layer], 0, KD, None, x_ready)

        def program():
            tc = [pool.do(lambda e: e.memset(ones[:, :], 1.0)), pool.do(lambda e: e.memset(neg_ones[:, :], -1.0)),
                  pool.do(lambda e: e.memset(small[:, 0:1], EPS)), pool.do(lambda e: e.memset(causal[:, :], 0.0))]
            ti = pool.do(lambda e: e.affine_select(out=ident[:, :], in_=ones[:, :], pattern=[[1, P]], compare_op=ALU.is_equal, fill=0.0,
                                                   base=0, channel_multiplier=-1), after=tc)
            pool.do(lambda e: e.affine_select(out=neg_tri[:, :], in_=neg_ones[:, :], pattern=[[-1, P]], compare_op=ALU.is_ge, fill=0.0,
                                              base=0, channel_multiplier=1), after=[ti])
            for n in range(NT):
                blk = causal[:, ROW_AT[n] + n * P:ROW_AT[n] + (n + 1) * P]
                tm = pool.do(lambda e, blk=blk: e.affine_select(out=blk, in_=blk, pattern=[[-1, P]], compare_op=ALU.is_ge, fill=MASKED,
                                                                base=0, channel_multiplier=1), after=[ti])
            state["consts"] = state["masks"] = tm
            c = Carver()
            xin = c.new(NT, D)
            rows = c.new(len(groups), P)
            at = 0
            for g, names in enumerate(groups):
                r = 0
                for name, n in names:
                    src = t[name]
                    if name == "mod_b":
                        src = src[g - 1:g, :]
                    nd = len(src.shape)
                    src = (src.rearrange("(n p) -> n p", p=P) if nd == 1 else src.rearrange("a (n p) -> (a n) p", p=P) if nd == 2
                           else src.rearrange("a b (n p) -> (a b n) p", p=P))
                    tl = sp.load(rows[r:r + n, g, :], src, s_tab, counts)
                    r += n
            sp.load(rope_c[:, :], t["rope_cos"], s_tab, counts)
            tl = sp.load(rope_s[:, :], t["rope_sin"], s_tab, counts)
            xl = sp.load(xin, t["x"][0].rearrange("(n p) d -> p n d", p=P), s_in, counts)
            b, fr = take_pair()
            for g, names in enumerate(groups):
                n = sum(k for _, k in names)
                tt = pe.do(lambda e, g=g, n=n, at=at: e.transpose(psum[:, b, at:at + n], rows[0:n, g, :], ident[0:n, 0:n]), after=[tl, tm])
                at += n
            tv = act.do(lambda e: e.copy(vec[:, 0:at], psum[:, b, 0:at]), after=[tt])
            free_pair(b, [tv])
            state["vec"] = tv
            state["c_act"] = act.do(lambda e: e.activation(v("c_act", 0, KD), v("c", 0, KD), ACT.Silu), after=[tv])
            x_ready = []
            for j in range(KD):
                if j % 2 == 0:
                    b, fr = take_pair()
                for n in range(NT):
                    tt = pe.do(lambda e, j=j, n=n, b=b: e.transpose(psum[:, b + j % 2, n * P:(n + 1) * P], xin[:, n, j * P:(j + 1) * P], ident[:, :]),
                               after=[xl, fr, tm], signal=n == NT - 1)
                tx = act.do(lambda e, j=j, b=b: e.copy(xT[:, j, :], psum[:, b + j % 2, :]), after=[tt])
                if j % 2:
                    free_pair(b, [tx])
                x_ready.append([tx])
            n = RNN // P
            lam, dec = v("lru_lambda", 0, n), v("decay", 0, n)
            e0, s0, s2, p0 = (small[:, 16 + 16 * i:16 + 16 * i + n] for i in range(4))
            a = act.do(lambda e: e.activation(e0, lam, ACT.Abs), after=[tv])
            a = act.do(lambda e: e.activation(e0, e0, ACT.Exp, scale=-1.0), after=[a])
            d = dve.do(lambda e: e.tensor_scalar(s0, e0, 2.0, None, ALU.add), after=[a])
            d = dve.do(lambda e: e.reciprocal(s0, s0), after=[d])
            d = dve.do(lambda e: e.tensor_tensor(s0, s0, e0, ALU.mult), after=[d])
            d = dve.do(lambda e: e.tensor_tensor(s2, s0, s0, ALU.mult), after=[d])
            TERMS = 9
            d = dve.do(lambda e: e.tensor_scalar(p0, s2, 1.0 / (2 * TERMS - 1), 1.0 / (2 * TERMS - 3), ALU.mult, ALU.add), after=[d])
            for i in range(TERMS - 3, -1, -1):
                d = dve.do(lambda e: e.tensor_tensor(p0, p0, s2, ALU.mult), after=[d])
                d = dve.do(lambda e, i=i: e.tensor_scalar(p0, p0, 1.0 / (2 * i + 1), None, ALU.add), after=[d])
            d = dve.do(lambda e: e.tensor_tensor(p0, p0, s0, ALU.mult), after=[d])
            d = dve.do(lambda e: e.tensor_scalar(s2, lam, -1.0, 0.0, ALU.mult, ALU.max), after=[d])
            d = dve.do(lambda e: e.scalar_tensor_tensor(p0, p0, 2.0, s2, ALU.mult, ALU.add), after=[d])
            state["decay"] = dve.do(lambda e: e.tensor_scalar(dec, p0, -8.0, None, ALU.mult), after=[d])

            state["area_free"] = fence()
            ffn_order = ((0, 0, 0), (0, 1, 2), (1, 0, 0), (1, 1, 2))
            if stream.plan is not None:
                while stream.n_split < 1:
                    stream.split_next()
                stream.turn()
            ffn(*ffn_order[0], x_ready)
            stick_breaking(x_ready)
            ffn(*ffn_order[1], x_ready)
            ffn(*ffn_order[2], x_ready)
            rglru(x_ready)
            ffn(*ffn_order[3], x_ready)
            x_ready = norm(x_ready, xT, lambda j: v("final_norm_g", j), split=False)
            for layer in range(2):
                hybrid(layer, x_ready)
            norm_out = norm(x_ready, xT, lambda j: v("final_norm_g_2", j), split=False)
            c = Carver()
            c.at = 5 * S
            y = c.new(NT, D)
            for n in range(NT):
                b, fr = take_pair()
                for j in range(KD):
                    tt = pe.do(lambda e, j=j, n=n, b=b: e.transpose(flat[:, b * 512 + j * P:b * 512 + (j + 1) * P], xT[:, j, n * P:(n + 1) * P], ident[:, :]),
                               after=[norm_out[j], fr], signal=j == KD - 1)
                ty = act.do(lambda e, n=n, b=b: e.copy(y[:, n, :], flat[:, b * 512:(b + 2) * 512]), after=[tt])
                free_pair(b, [ty])
                to = sp.load(out[0, n * P:(n + 1) * P, :], y[:, n, :], s_out, counts, after=[ty])
            sp.wait([to])

        stream = Stream(None, None, 0)
        program()
        asked = stream.asked
        for q in (pe, act, dve, pool, sp):
            q.value, q.items, q.waited = 0, [], {}
        counts.clear()
        state.clear()
        pairs[0] = 0
        bank_free[:] = [[] for _ in range(8)]
        stream = Stream(asked, mod_panels(), KD)
        program()

        block = ctx.enter_context(nc.Block())

        @block.sync
        def _(e):
            sp.play(e)

        @block.tensor
        def _(e):
            pe.play(e)

        @block.scalar
        def _(e):
            act.play(e)

        @block.vector
        def _(e):
            dve.play(e)

        @block.gpsimd
        def _(e):
            pool.play(e)


_INS = ["x", "c", "mod_w", "mod_b", "norm_g", "ffn_w_gu", "ffn_w_down", "sb_w_qkv", "sb_w_o", "lru_w_in", "lru_conv_w",
        "lru_conv_b", "lru_w_r", "lru_b_r", "lru_w_i", "lru_b_i", "lru_lambda", "lru_w_out", "final_norm_g",
        "norm_g_2", "w_in_2", "w_br_a_2", "w_br_b_2", "w_br_c_2", "w_out_2", "final_norm_g_2"]


def rope_constants(seq, head_dim=64, theta=10000.0):
    half = head_dim // 2
    inv_freq = (np.float32(1.0) / (np.float32(theta) ** (np.arange(0, head_dim, 2, dtype=np.float32) / np.float32(head_dim)))).astype(np.float32)
    ang = (inv_freq[:, None] * np.arange(seq, dtype=np.float32)[None, :]).astype(np.float32)
    c, s = np.cos(ang), np.sin(ang)
    return np.tile(c, (4, 1)).astype(np.float32), np.concatenate([-s, s, -s, s]).astype(np.float32)


def kernel(**inputs):
    import numpy as _np
    import concourse.bacc as _bacc
    from concourse import mybir as _mybir
    from concourse.bass_utils import run_bass_kernel_spmd as _run

    nc = _bacc.Bacc("TRN2", target_bir_lowering=False, num_devices=1)
    arrays, aps = {}, {}
    for name in _INS:
        a = _np.ascontiguousarray(inputs[name])
        arrays[f"in_{name}"] = a
        aps[name] = nc.dram_tensor(f"in_{name}", a.shape, _mybir.dt.from_np(a.dtype), kind="ExternalInput").ap()
    shape = inputs["x"].shape
    for name, a in zip(("rope_cos", "rope_sin"), rope_constants(shape[1])):
        arrays[name] = a
        aps[name] = nc.dram_tensor(name, a.shape, _mybir.dt.from_np(a.dtype), kind="ExternalInput").ap()
    out = nc.dram_tensor("out_0", shape, _mybir.dt.from_np(_np.dtype("float32")), kind="ExternalOutput").ap()
    build(nc, aps, out)
    r = _run(nc, [arrays], core_ids=[0])
    return r.results[0]["out_0"]
```

```python
from contextlib import ExitStack

import numpy as np

import concourse.bass as bass
from concourse import mybir

F32 = mybir.dt.float32
F32R = mybir.dt.float32r
ALU = mybir.AluOpType
ACT = mybir.ActivationFunctionType
AX = mybir.AxisListType

P = 128
MASKED = -1.0e30
NOT_CAUSAL = -3.0e38
PICKED = -3.4e38
PICKED_BELOW = -3.2e38


class Operands:

    def matmul(self, *a, **k):
        return lambda e: e.matmul(*a, **k)

    def transpose(self, *a, **k):
        return lambda e: e.transpose(*a, **k)

    def activation(self, *a, **k):
        return lambda e: e.activation(*a, **k)

    def copy(self, *a, **k):
        return lambda e: e.copy(*a, **k)

    def mul(self, *a, **k):
        return lambda e: e.mul(*a, **k)

    def tensor_tensor(self, *a, **k):
        return lambda e: e.tensor_tensor(*a, **k)

    def tensor_scalar(self, *a, **k):
        return lambda e: e.tensor_scalar(*a, **k)

    def scalar_tensor_tensor(self, *a, **k):
        return lambda e: e.scalar_tensor_tensor(*a, **k)

    def tensor_tensor_scan(self, *a, **k):
        return lambda e: e.tensor_tensor_scan(*a, **k)

    def tensor_copy(self, *a, **k):
        return lambda e: e.tensor_copy(*a, **k)

    def tensor_reduce(self, *a, **k):
        return lambda e: e.tensor_reduce(*a, **k)

    def reciprocal(self, *a, **k):
        return lambda e: e.reciprocal(*a, **k)

    def max(self, *a, **k):
        return lambda e: e.max(*a, **k)

    def match_replace(self, *a, **k):
        return lambda e: e.match_replace(*a, **k)

    def memset(self, *a, **k):
        return lambda e: e.memset(*a, **k)

    def preload_act_table_set(self, *a, **k):
        return lambda e: e.preload_act_table_set(*a, **k)

    def affine_select(self, *a, **k):
        return lambda e: e.affine_select(*a, **k)


class Queue:

    def __init__(self, semaphore):
        self.semaphore, self.value, self.items, self.waited = semaphore, 0, [], {}

    def wait(self, after):
        for producer in after:
            if isinstance(producer, list):
                self.wait(producer)
            elif producer is not None:
                sem, value = producer
                if value > self.waited.get(id(sem), 0):
                    self.waited[id(sem)] = value
                    self.items.append(lambda e, sem=sem, value=value: e.wait_ge(sem, value))

    def do(self, make, after=(), signal=True):
        self.wait(after)
        step = make(Operands())
        if not signal:
            self.items.append(step)
            return None
        self.value += 1
        self.items.append(lambda e: step(e).then_inc(self.semaphore, 1))
        return (self.semaphore, self.value)

    def load(self, out, in_, sem, counts, after=()):
        self.wait(after)
        counts[id(sem)] = counts.get(id(sem), 0) + 16
        self.items.append(lambda e: e.dma_start(out, in_).then_inc(sem, 16))
        return (sem, counts[id(sem)])

    def last(self):
        return (self.semaphore, self.value) if self.value else None

    def play(self, engine):
        for item in self.items:
            item(engine)


def build(nc, t, out):
    S, D = t["x"].shape[1:]
    KD = D // P
    NT = S // P
    FF = t["ffn_w_down"].shape[2]
    RNN = t["lru_w_out"].shape[1]
    HD = 64
    PANEL = 2 * P
    RAW = KD * PANEL
    SCALE = HD ** -0.5
    EPS = 1e-6
    TRI = S * (NT + 1) // 2
    ROW_AT = {3: 0, 2: 512, 0: 896, 1: 1024}
    COL_AT = {0: 0, 1: 512, 3: 896, 2: 1024}
    HALF = (slice(0, S // 2), slice(S // 2, S))
    HT = NT // 2

    with ExitStack() as ctx:
        def sb(name, shape, dt=F32):
            return ctx.enter_context(nc.sbuf_tensor(name, shape, dt))

        def sem(name):
            return ctx.enter_context(nc.semaphore(name))

        xT = sb("xT", [P, KD, S])
        H = (sb("h_high", [P, KD, S], F32R), sb("h_low", [P, KD, S], F32R))
        with nc.sbuf_tensor("y_plain", [P, 2, KD, S], F32) as y_plain:
            pass
        Y = (sb("y_high", [P, KD, S], F32R), sb("y_low", [P, KD, S], F32R))
        NRAW, NW = 3, 2
        raw = [sb(f"raw{i}", [P, RAW]) for i in range(NRAW)]
        W = [(sb(f"w_high{i}", [P, RAW], F32R), sb(f"w_low{i}", [P, RAW], F32R)) for i in range(NW)]
        ident = sb("ident", [P, P])
        ones = sb("ones", [P, P])
        neg_tri = sb("neg_tri", [P, P])
        neg_ones = sb("neg_ones", [P, P])
        causal = sb("causal", [P, TRI])
        rope_c = sb("rope_c", [P, S])
        rope_s = sb("rope_s", [P, S])
        mod_acc = sb("mod_acc", [P, D])
        inv = sb("inv", [P, S])
        vec = sb("vec", [P, 336])
        small = sb("small", [P, 96])
        AREA = 13312
        area = sb("area", [P, AREA])
        psum = ctx.enter_context(nc.psum_tensor("psum", [P, 8, 512], F32))
        flat = psum[:, :, :].rearrange("p b c -> p (b c)")

        pe, act, dve, pool, sp = (Queue(sem(f"{n}_done")) for n in ("pe", "act", "dve", "pool", "sp"))
        s_raw = [sem(f"raw_loaded{i}") for i in range(NRAW)]
        s_in, s_tab, s_swap, s_out, s_gate_w = sem("x_loaded"), sem("tables_loaded"), sem("swapped"), sem("stored"), sem("gate_w_loaded")
        s_dup = sem("copied_half")
        counts = {}
        state = {}

        def fence():
            return [q.last() for q in (pe, act, dve, pool)]

        class Carver:

            def __init__(self):
                self.at = 0

            def new(self, *shape):
                n = int(np.prod(shape))
                assert self.at + n <= AREA, (self.at, n)
                a = area[:, self.at:self.at + n]
                self.at += n
                if len(shape) == 2:
                    a = a.rearrange("p (a b) -> p a b", a=shape[0])
                if len(shape) == 3:
                    a = a.rearrange("p (a b c) -> p a b c", a=shape[0], b=shape[1])
                return a

        groups = [
            [("c", KD), ("norm_g", 6 * KD), ("final_norm_g", KD), ("norm_g_2", 2 * KD), ("final_norm_g_2", KD)],
            [("mod_b", 9 * KD)],
            [("mod_b", 9 * KD)],
            [("lru_conv_w", 4 * RNN // P), ("lru_conv_b", RNN // P), ("lru_b_r", RNN // P),
             ("lru_b_i", RNN // P), ("lru_lambda", RNN // P)],
        ]
        col = {}
        at = 0
        for g, names in enumerate(groups):
            for name, n in names:
                col[f"{name}{g - 1 if name == 'mod_b' else ''}"] = at
                at += n
        col["c_act"] = at
        col["decay"] = at + KD
        assert col["decay"] + RNN // P <= 336
        mods = [sb(f"mod{i}", [P, 9 * KD]) for i in range(2)]

        def v(name, i=0, n=1):
            return vec[:, col[name] + i:col[name] + i + n]

        bank_free = [[] for _ in range(8)]
        pairs = [0]

        only_pair = [None]

        def take_pair():
            if only_pair[0] is not None:
                b = only_pair[0]
                return b, [bank_free[b], bank_free[b + 1]]
            b = 2 * (pairs[0] % 4)
            pairs[0] += 1
            return b, [bank_free[b], bank_free[b + 1]]

        class Stream:

            def __init__(self, plan, mod_plan, lead):
                self.asked = []
                self.plan = None
                if plan is not None:
                    merged, rest = list(mod_plan[:lead]), list(mod_plan[lead:])
                    for k in plan:
                        merged.append(("w", k))
                        if rest:
                            merged.append(rest.pop(0))
                    self.plan = merged
                self.loaded = self.split = 0
                self.raw_free = [None] * NRAW
                self.w_free = [None] * NW
                self.n_split = 0
                self.n_taken = 0
                self.ready = {}
                self.raw_ready = {}
                self.late = None
                self.low_by = dve

            def turn(self):
                if self.late:
                    late, self.late = self.late, None
                    late()

            def load_next(self):
                if self.loaded >= len(self.plan):
                    return
                kind, pieces = self.plan[self.loaded]
                s = self.loaded % NRAW
                for off, n, k, src in pieces:
                    dst = raw[s][:, off:off + n].rearrange("p (k n) -> p k n", k=k)
                    tok = sp.load(dst, src, s_raw[s], counts, after=[self.raw_free[s]])
                self.raw_ready[self.loaded] = tok
                self.loaded += 1

            def split_next(self):
                while self.split < len(self.plan):
                    i = self.split
                    while self.loaded <= i:
                        self.load_next()
                    kind, pieces = self.plan[i]
                    s = i % NRAW
                    self.split += 1
                    got = self.raw_ready.pop(i)
                    if kind == "w":
                        n = sum(p[1] for p in pieces)
                        w = self.n_split % NW
                        high, low = W[w]
                        th = act.do(lambda e: e.copy(high[:, :n], raw[s][:, :n]), after=[got, self.w_free[w]])
                        tl = self.low_by.do(lambda e: e.tensor_tensor(low[:, :n], raw[s][:, :n], high[:, :n].bitcast(F32), ALU.subtract),
                                            after=[th, self.w_free[w]])
                        self.raw_free[s] = tl
                        self.ready[self.n_split] = (w, [th, tl])
                        self.n_split += 1
                        self.load_next()
                        return
                    self.mod_step(kind, s, got)
                    self.load_next()

            def mod_step(self, kind, s, got):
                _, layer, sub, part, kp = kind
                if kp == 0:
                    self.turn()
                for k in range(2):
                    w = raw[s][:, k * D:(k + 1) * D]
                    c = v("c_act", 2 * kp + k)
                    if kp == 0 and k == 0:
                        tok = dve.do(lambda e: e.tensor_scalar(mod_acc[:, :], w, c, None, ALU.mult),
                                     after=[got, state["c_act"], state.get("mod_read")])
                    else:
                        tok = dve.do(lambda e: e.scalar_tensor_tensor(mod_acc[:, :], w, c, mod_acc[:, :], ALU.mult, ALU.add),
                                     after=[got, dve.last()])
                self.raw_free[s] = tok
                if kp < KD // 2 - 1:
                    return

                def turn():
                    b, free = take_pair()
                    for j in range(KD):
                        tp = pe.do(lambda e, j=j: e.matmul(psum[:, b, j:j + 1], mod_acc[:, j * P:(j + 1) * P], ones[:, 0:1],
                                                           start=True, stop=True), after=[tok, free, state["consts"]], signal=j == KD - 1)
                    state["mod_read"] = tp
                    o = (3 * sub + part) * KD
                    td = dve.do(lambda e: e.tensor_tensor(mods[layer][:, o:o + KD], psum[:, b, 0:KD], v(f"mod_b{layer}", o, KD), ALU.add),
                                after=[tp, state["vec"]])
                    bank_free[b] = [td]
                    state[("mod", layer, sub, part)] = td
                self.late = turn

            def ahead(self, low_by):
                if self.plan is not None and self.n_split == self.n_taken:
                    mine, self.low_by = self.low_by, low_by
                    self.split_next()
                    self.low_by = mine

            def take(self, pieces, ahead=True):
                if self.plan is None:
                    self.asked.append(pieces)
                    i = self.n_taken
                    self.n_taken += 1
                    return W[0], [], lambda tok: None
                i = self.n_taken
                self.n_taken += 1
                self.turn()
                while self.n_split <= i:
                    self.split_next()
                if self.n_split == i + 1 and i > 0 and ahead:
                    self.split_next()
                w, toks = self.ready.pop(i)

                def done(tok):
                    self.w_free[w] = tok
                return W[w], toks, done

        def piece(src, k, off=0):
            n = src.shape[1] * k
            return (off, n, k, src.rearrange("(k p) n -> p k n", p=P))

        def mod_panels():
            plan = []
            for layer in range(2):
                for sub in range(3):
                    for part in range(3):
                        for kp in range(KD // 2):
                            c0 = (3 * sub + part) * D
                            src = t["mod_w"][layer, 2 * kp * P:(2 * kp + 2) * P, c0:c0 + D]
                            plan.append((("m", layer, sub, part, kp), [piece(src, 2)]))
            return plan

        def product(X, ready, src_pieces, ks, n, free, widths=(P, P), base=None, mid=None):
            (wh, wl), wt, done = stream.take(src_pieces, ahead=mid is None)
            if base is None:
                base, free = take_pair()
            wv = [w[:, :len(ks) * n].rearrange("p (k n) -> p k n", n=n) for w in (wh, wl)]
            combos = ((0, 0), (0, 1), (1, 0))
            if mid:
                for h in range(2):
                    for i, k in enumerate(ks):
                        for m, width in enumerate(widths):
                            for a, b in combos:
                                end = i == len(ks) - 1 and m == len(widths) - 1 and (a, b) == combos[-1]
                                tok = pe.do(lambda e: e.matmul(
                                    psum[0:width, base + m, HALF[h]], wv[a][:, i, m * P:m * P + width], X[b][:, k, HALF[h]],
                                    start=(i == 0 and (a, b) == (0, 0)), stop=(i == len(ks) - 1 and (a, b) == combos[-1])),
                                    after=[wt, ready[k][h], free], signal=end)
                        if h == 0:
                            mid(i)
                        if h == 0 and i == 2:
                            stream.ahead(pool)
                done(tok)
                return base, tok
            for i, k in enumerate(ks):
                c0 = 0
                for m, width in enumerate(widths):
                    for a, b in combos:
                        end = i == len(ks) - 1 and m == len(widths) - 1 and (a, b) == combos[-1]
                        tok = pe.do(lambda e, i=i, k=k, m=m, a=a, b=b, c0=c0, width=width: e.matmul(
                            psum[0:width, base + m, :], wv[a][:, i, c0:c0 + width], X[b][:, k, :],
                            start=(i == 0 and (a, b) == (0, 0)), stop=(i == len(ks) - 1 and (a, b) == combos[-1])),
                            after=[wt, ready[k], free], signal=end)
                    c0 += width
            done(tok)
            return base, tok

        def product_tok(X, ready, src_pieces, n):
            (wh, wl), wt, done = stream.take(src_pieces)
            base, free = take_pair()
            wv = [w[:, :KD * n].rearrange("p (k n) -> p k n", n=n) for w in (wh, wl)]
            for tt in range(NT):
                for k in range(KD):
                    for a, b in ((0, 0), (0, 1), (1, 0)):
                        end = tt == NT - 1 and k == KD - 1 and (a, b) == (1, 0)
                        o = (base + tt // 2) * 512 + (tt % 2) * PANEL
                        tok = pe.do(lambda e, tt=tt, k=k, a=a, b=b, o=o: e.matmul(
                            flat[:, o:o + n], X[b][:, k, tt * P:(tt + 1) * P], wv[a][:, k, :],
                            start=(k == 0 and (a, b) == (0, 0)), stop=(k == KD - 1 and (a, b) == (1, 0))),
                            after=[wt, ready[k], free], signal=end)
            done(tok)
            view = flat[:, base * 512:(base + 2) * 512].rearrange("p (t c) -> p t c", c=PANEL)[:, :, :n]
            return base, view, tok

        def free_pair(base, toks):
            bank_free[base] = bank_free[base + 1] = list(toks)

        class Norm:

            def __init__(self, x_ready, dst, gain, shift=None, split=True):
                self.x_ready, self.dst, self.gain, self.shift, self.split = x_ready, dst, gain, shift, split
                self.f = state["area_free"]
                self.reads = [[fence()], [fence()]]
                c = Carver()
                self.ssum, self.sq, self.tmp = c.new(S), c.new(2, S), c.new(2, S)
                self.used, self.tmp_used = [[None, None], [None, None]], [[None, None], [None, None]]
                self.tsum, self.bank, self.summed, self.spread_ = [None, None], [None, None], [None, None], [None, None]
                self.out = [[None, None] for _ in range(KD)]
                act.do(lambda e: e.activation(small[:, 1:2], small[:, 0:1], ACT.Sqrt), after=[state["consts"], act.last()])

            def squares(self, h, j0=0, j1=KD):
                ssum, sq, f, hs = self.ssum, self.sq, self.f, HALF[h]
                for j in range(j0, j1):
                    if j == 0:
                        self.tsum[h] = act.do(lambda e: e.activation(ssum[:, hs], xT[:, 0, hs], ACT.Square), after=[self.x_ready[0][h], f])
                        continue
                    ts = act.do(lambda e: e.activation(sq[:, j % 2, hs], xT[:, j, hs], ACT.Square),
                                after=[self.x_ready[j][h], f, self.used[h][j % 2]])
                    self.tsum[h] = self.used[h][j % 2] = dve.do(lambda e: e.tensor_tensor(ssum[:, hs], ssum[:, hs], sq[:, j % 2, hs], ALU.add),
                                                                after=[ts, self.tsum[h]])

            def gather(self, h):
                ssum = self.ssum
                b, free = take_pair()
                self.bank[h] = b
                for n in range(HT):
                    o = (HT * h + n) * P
                    self.summed[h] = pe.do(lambda e: e.matmul(psum[:, b, n:n + 1], ssum[:, o:o + P], ones[:, 0:1], start=True, stop=True),
                                           after=[self.tsum[h], free], signal=n == HT - 1)

            def spread(self, h):
                b = self.bank[h]
                stats = small[:, 80:96]
                mean, root, y2 = (stats[:, 4 * i + HT * h:4 * i + HT * (h + 1)] for i in range(3))
                tv = dve.do(lambda e: e.tensor_scalar(mean, psum[:, b, 0:HT], 1.0 / D, EPS, ALU.mult, ALU.add), after=[self.summed[h]])
                tr = act.do(lambda e: e.activation(root, mean, ACT.Sqrt), after=[tv])
                ti = dve.do(lambda e: e.reciprocal(root, root), after=[tr])
                ti = dve.do(lambda e: e.tensor_tensor(y2, root, root, ALU.mult), after=[ti])
                ti = dve.do(lambda e: e.scalar_tensor_tensor(y2, y2, -0.5, mean, ALU.mult, ALU.mult), after=[ti])
                ti = dve.do(lambda e: e.scalar_tensor_tensor(root, y2, 1.5, root, ALU.add, ALU.mult), after=[ti])
                for n in range(HT):
                    o = (HT * h + n) * P
                    td = dve.do(lambda e: e.tensor_scalar(inv[:, o:o + P], ident[:, :], root[:, n:n + 1], None, ALU.mult),
                                after=[ti, state["consts"], state.get(("inv_read", h))])
                self.diag, self.tv = td, tv

            def broadcast(self, h):
                b = self.bank[h]
                self.spread_[h] = state["inv_read", h] = pe.do(lambda e: e.matmul(psum[:, b + 1, 0:S // 2], ones[:, :], inv[:, HALF[h]],
                                                                                 start=True, stop=True), after=[self.diag, self.tv])

            def apply(self, h, j0=0, j1=KD):
                hs, f, reads = HALF[h], self.f, self.reads[h]
                invp = psum[:, self.bank[h] + 1, 0:S // 2]
                if not self.split:
                    for j in range(j0, j1):
                        td = dve.do(lambda e: e.scalar_tensor_tensor(self.dst[:, j, hs], xT[:, j, hs], self.gain(j), invp, ALU.mult, ALU.mult),
                                    after=[self.spread_[h], self.x_ready[j][h], self.tsum[h]])
                        self.out[j][h] = [td]
                    if j1 == KD:
                        free_pair(self.bank[h], [td])
                    return
                high, low = self.dst

                def scaled(j):
                    p = j % 2
                    td = dve.do(lambda e: e.scalar_tensor_tensor(self.tmp[:, p, hs], xT[:, j, hs], self.gain(j), invp, ALU.mult, ALU.mult),
                                after=[self.spread_[h], self.tmp_used[h][p], self.x_ready[j][h], f, state.get("gain")])
                    th = act.do((lambda e: e.copy(high[:, j, hs], self.tmp[:, p, hs])) if self.shift is None else
                                (lambda e: e.activation(high[:, j, hs], self.tmp[:, p, hs], ACT.Identity, bias=self.shift(j))), after=[td, reads])
                    return td, th

                def rest(j, td, th):
                    p = j % 2
                    if self.shift is None:
                        tl = dve.do(lambda e: e.tensor_tensor(low[:, j, hs], self.tmp[:, p, hs], high[:, j, hs].bitcast(F32), ALU.subtract),
                                    after=[th, td, reads])
                    else:
                        tl = dve.do(lambda e: e.scalar_tensor_tensor(low[:, j, hs], self.tmp[:, p, hs], self.shift(j), high[:, j, hs].bitcast(F32),
                                                                     ALU.add, ALU.subtract), after=[th, td, reads])
                    self.tmp_used[h][p] = tl
                    self.out[j][h] = [th, tl]

                before = scaled(j0)
                for j in range(j0, j1):
                    this = before
                    if j + 1 < j1:
                        before = scaled(j + 1)
                    rest(j, *this)
                if j1 == KD:
                    free_pair(self.bank[h], [this[0]])

            def begin(self, j0):
                self.apply(0, 0, 3)
                self.squares(1, j0)
                self.apply(0, 3, 5)

            def during(self, i):
                if i == 2:
                    self.gather(1)
                    self.spread(1)
                    self.apply(0, 5)
                if i == 5:
                    self.broadcast(1)
                    self.apply(1)

            def finish(self):
                for i in (2, 5):
                    self.during(i)

        def split_into(X, j, src, after, old_reads, parts=slice(0, P)):
            th = act.do(lambda e: e.copy(X[0][parts, j, :], src), after=[after, old_reads])
            tl = dve.do(lambda e: e.tensor_tensor(X[1][parts, j, :], src, X[0][parts, j, :].bitcast(F32), ALU.subtract),
                        after=[th, after, old_reads])
            return [th, tl]

        gs = sb("gain_in", [P, KD])
        gg = sb("gain_out", [P, KD])

        def gains(layer, sub, weight):
            m = mods[layer]
            o = 3 * sub * KD
            need = [state.get(("mod", layer, sub, part)) for part in range(2)]
            assert stream.plan is None or None not in need
            state["gain"] = dve.do(lambda e: e.scalar_tensor_tensor(gs[:, :], m[:, o + KD:o + 2 * KD], 1.0, v("norm_g", (3 * layer + sub) * KD, KD),
                                                                    ALU.add, ALU.mult), after=[need, state["vec"], dve.last()])

            def gate():
                assert stream.plan is None or ("mod", layer, sub, 2) in state
                state["gate"] = dve.do(lambda e: e.tensor_scalar(gg[:, :], m[:, o + 2 * KD:o + 3 * KD], 1.0, weight, ALU.add, ALU.mult),
                                       after=[state.get(("mod", layer, sub, 2)), dve.last()])
                return lambda j: gg[:, j:j + 1]
            return (lambda j: gs[:, j:j + 1]), (lambda j: m[:, o + j:o + j + 1]), gate

        def add_to_x(base, tok, j0, gate, x_ready):
            toks = []
            for m in range(2):
                j = j0 + m
                if gate is None:
                    td = dve.do(lambda e, m=m, j=j: e.tensor_tensor(xT[:, j, :], xT[:, j, :], psum[:, base + m, :], ALU.add),
                                after=[tok, x_ready[j]])
                else:
                    td = dve.do(lambda e, m=m, j=j: e.scalar_tensor_tensor(xT[:, j, :], psum[:, base + m, :], gate(j), xT[:, j, :],
                                                                           ALU.mult, ALU.add), after=[tok, x_ready[j], state["gate"]])
                x_ready[j] = [td, td]
                toks.append(td)
            free_pair(base, toks)

        def project_back(X, ready, w, row0, nk, gate, x_ready, next_norm=None, first=0):
            def src(c):
                return [piece(w[row0:row0 + nk * P, c * PANEL:(c + 1) * PANEL], nk)]

            ks = [(first + i) % KD for i in range(nk)]
            whole = D // PANEL - (2 if next_norm else 0)
            for c in range(whole):
                base, tok = product(X, ready, src(c), ks, PANEL, None)
                add_to_x(base, tok, 2 * c, gate, x_ready)
            if not next_norm:
                return tok, None
            norm = next_norm()
            taken, bases = [], []
            for c in (whole, whole + 1):
                taken.append(stream.take(src(c), ahead=c == whole))
                bases.append(take_pair())

            def half(i, h):
                (wh, wl), wt, _ = taken[i]
                base, free = bases[i]
                wv = [x[:, :nk * PANEL].rearrange("p (k n) -> p k n", n=PANEL) for x in (wh, wl)]
                for m in range(2):
                    for i, k in enumerate(ks):
                        for a, b in ((0, 0), (0, 1), (1, 0)):
                            end = m == 1 and i == nk - 1 and (a, b) == (1, 0)
                            tok = pe.do(lambda e: e.matmul(
                                psum[:, base + h, m * S // 2:(m + 1) * S // 2], wv[a][:, i, m * P:(m + 1) * P], X[b][:, k, HALF[h]],
                                start=(i == 0 and (a, b) == (0, 0)), stop=(i == nk - 1 and (a, b) == (1, 0))),
                                after=[wt, ready[k], free], signal=end)
                return tok

            def add(i, h, tok):
                toks = []
                for m in range(2):
                    j = 2 * (whole + i) + m
                    src, dst = psum[:, bases[i][0] + h, m * S // 2:(m + 1) * S // 2], xT[:, j, HALF[h]]
                    if gate is None:
                        td = dve.do(lambda e: e.tensor_tensor(dst, dst, src, ALU.add), after=[tok, x_ready[j][h]])
                    else:
                        td = dve.do(lambda e: e.scalar_tensor_tensor(dst, src, gate(j), dst, ALU.mult, ALU.add),
                                    after=[tok, x_ready[j][h], state["gate"]])
                    x_ready[j] = [td, x_ready[j][1]] if h == 0 else [x_ready[j][0], td]
                    toks.append(td)
                if h:
                    free_pair(bases[i][0], toks)

            t00 = half(0, 0)
            t10 = half(1, 0)
            norm.reads[0].append(t10)
            add(0, 0, t00)
            norm.squares(0, 0, 2 * whole + 2)
            add(1, 0, t10)
            t01 = half(0, 1)
            taken[0][2](t01)
            norm.squares(0, 2 * whole + 2)
            norm.gather(0)
            norm.spread(0)
            stream.ahead(pool)
            add(0, 1, t01)
            norm.squares(1, 0, 2 * whole + 2)
            t11 = half(1, 1)
            taken[1][2](t11)
            norm.reads[1].append(t11)
            norm.broadcast(0)
            add(1, 1, t11)
            norm.begin(2 * whole + 2)
            return t11, norm

        def modulated(layer, sub, weight, x_ready):
            gain, shift, out_gain = gains(layer, sub, weight)
            norm = Norm(x_ready, H, gain, shift)
            norm.out_gain = out_gain
            return norm

        def ffn(layer, which, norm, x_ready, next_norm):
            hr, out_gain, mid = norm.out, norm.out_gain, norm.during
            state["area_free"] = None
            gate = None
            w_gu, w_down = t["ffn_w_gu"][layer, which], t["ffn_w_down"][layer, which]
            f = fence()
            c = Carver()
            c.at = 5 * S
            sil = [c.new(S) for _ in range(4)]
            prod = [c.new(S) for _ in range(4)]
            sil_free, prod_free = [None] * 4, [None] * 4
            n = 0
            y_reads = f
            for row in range(0, FF // P, KD):
                nk = min(KD, FF // P - row)
                yr = []
                for c0 in range(row, row + nk, 2):
                    bg, tg = product(H, hr, [piece(w_gu[:, c0 * P:c0 * P + PANEL], KD)], range(KD), PANEL, None, mid=mid)
                    if mid:
                        state["area_free"], mid = fence(), None
                    bu, tu = product(H, hr, [piece(w_gu[:, FF + c0 * P:FF + c0 * P + PANEL], KD)], range(KD), PANEL, None)
                    gt, ut = [], []
                    for m in range(2):
                        s = n % 4
                        n += 1
                        a1 = act.do(lambda e, m=m, s=s: e.activation(sil[s], psum[:, bg + m, :], ACT.Silu), after=[tg, sil_free[s], f])
                        d1 = dve.do(lambda e, m=m, s=s: e.tensor_tensor(prod[s], sil[s], psum[:, bu + m, :], ALU.mult),
                                    after=[a1, tu, prod_free[s], f])
                        sil_free[s] = d1
                        both = split_into(Y, c0 - row + m, prod[s], d1, y_reads)
                        prod_free[s] = both
                        gt.append(a1)
                        ut.append(d1)
                        yr.append(both)
                    free_pair(bg, gt)
                    free_pair(bu, ut)
                gate = gate or out_gain()
                tok, norm = project_back(Y, yr, w_down, row * P, nk, gate, x_ready, next_norm if row + nk == FF // P else None)
                y_reads = [tok]
            return norm

        def stick_breaking(norm, x_ready, next_norm):
            hr, out_gain, mid = norm.out, norm.out_gain, norm.during
            w_qkv, w_o = t["sb_w_qkv"][0], t["sb_w_o"][0]
            G = 4
            f = fence()
            c = Carver()
            c.at = 0
            q, k, vv = c.new(G, S), c.new(G, S), c.new(NT, G * P)
            tmp = [c.new(TRI) for _ in range(3)]
            sp_ = [c.new(TRI) for _ in range(2)]
            yr = [None] * KD
            for g in range(KD // G):
                f = fence()
                ready = {}
                for part, dst in ((0, q), (1, k)):
                    for c0 in range(0, G, 2):
                        src = w_qkv[:, part * D + (g * G + c0) * P:part * D + (g * G + c0) * P + PANEL]
                        base, tok = product(H, hr, [piece(src, KD)], range(KD), PANEL, None, mid=mid)
                        if mid:
                            f, mid = fence(), None
                        ta = act.do(lambda e, dst=dst, c0=c0, base=base, part=part: e.mul(dst[:, c0:c0 + 2, :], psum[:, base:base + 2, :],
                                                                                      SCALE if part == 0 else 1.0), after=[tok, f])
                        free_pair(base, [ta])
                        ready[part, c0] = ready[part, c0 + 1] = ta
                for c0 in range(0, G, 2):
                    src = w_qkv[:, 2 * D + (g * G + c0) * P:2 * D + (g * G + c0) * P + PANEL]
                    base, view, tok = product_tok(H, hr, [piece(src, KD)], PANEL)
                    ta = act.do(lambda e, c0=c0, view=view: e.copy(vv[:, :, c0 * P:c0 * P + PANEL], view), after=[tok, f])
                    free_pair(base, [ta])
                    ready[2, c0] = ready[2, c0 + 1] = ta
                zfree = [f, f]
                tmp_free, sp_free = [f, f, f], [f, f]
                o_free = {6: bank_free[6], 7: bank_free[7]}
                act.do(lambda e: e.preload_act_table_set("natural_log_exp_and_others"), signal=False)
                banks_before = [bank_free[b] for b in range(8)]
                st = {}

                def scores(h):
                    s, ti, r0 = h % 2, h // 2, (h % 2) * HD
                    for i in range(NT):
                        tz = pe.do(lambda e, i=i: e.matmul(
                            flat[:, s * 1536 + COL_AT[i]:s * 1536 + COL_AT[i] + S - P * i],
                            k[r0:r0 + HD, ti, i * P:(i + 1) * P], q[r0:r0 + HD, ti, i * P:S],
                            start=(i != 3), stop=True, skip_group_check=True),
                            after=[zfree[s], banks_before, ready[0, ti], ready[1, ti]], signal=i == NT - 1)
                    z = flat[:, s * 1536:s * 1536 + TRI]
                    a0 = act.do(lambda e: e.activation(tmp[h % 3], z, ACT.Abs), after=[tz, tmp_free[h % 3]])
                    a1 = act.do(lambda e: e.activation(tmp[h % 3], tmp[h % 3], ACT.Exp, scale=-1.0), after=[a0])
                    a2 = act.do(lambda e: e.activation(tmp[h % 3], tmp[h % 3], ACT.Ln, bias=1.0), after=[a1])
                    d2 = dve.do(lambda e: e.scalar_tensor_tensor(sp_[s], z, 0.0, tmp[h % 3], ALU.max, ALU.add), after=[a2, tz, sp_free[s]])
                    for i in range(NT):
                        blk = sp_[s][:, COL_AT[i]:COL_AT[i] + P]
                        tm = pool.do(lambda e, blk=blk: e.affine_select(out=blk, in_=blk, pattern=[[1, P]], compare_op=ALU.is_gt, fill=0.0,
                                                                        base=0, channel_multiplier=-1), after=[d2])
                    st[h] = (tm, d2)

                def weigh(h):
                    s, ti, r0 = h % 2, h // 2, (h % 2) * HD
                    tm, d2 = st[h]
                    for i in range(NT):
                        for j in range(i, NT):
                            o = s * 1536 + COL_AT[i] + P * (j - i)
                            tc = pe.do(lambda e, i=i, j=j, o=o: e.matmul(
                                flat[:, o:o + S - P * j], neg_tri[:, :] if i == j else neg_ones[:, :],
                                sp_[s][:, COL_AT[j]:COL_AT[j] + S - P * j], start=False, stop=True, skip_group_check=True),
                                after=[tm, d2], signal=(i, j) == (NT - 1, NT - 1))
                    sp_free[s] = tc
                    a1 = act.do(lambda e: e.activation(tmp[h % 3], flat[:, s * 1536:s * 1536 + TRI], ACT.Exp), after=[tc, d2])
                    zfree[s] = a1
                    for i in range(NT):
                        blk = tmp[h % 3][:, COL_AT[i]:COL_AT[i] + P]
                        tm = pool.do(lambda e, blk=blk: e.affine_select(out=blk, in_=blk, pattern=[[1, P]], compare_op=ALU.is_gt, fill=0.0,
                                                                        base=0, channel_multiplier=-1), after=[a1])
                    st[h] = (tm, a1)

                def values(h):
                    ti, r0 = h // 2, (h % 2) * HD
                    tm, a1 = st[h]
                    ob = 6 + ti % 2
                    for i in range(NT):
                        to = pe.do(lambda e, i=i: e.matmul(
                            psum[r0:r0 + HD, ob, i * P:S], vv[:, i, ti * P + r0:ti * P + r0 + HD], tmp[h % 3][:, COL_AT[i]:COL_AT[i] + S - P * i],
                            start=(i == 0), stop=(i == NT - 1), skip_group_check=True), after=[tm, a1, ready[2, ti], o_free[ob]], signal=i == NT - 1)
                    tmp_free[h % 3] = to
                    if h % 2:
                        yr[g * G + ti] = split_into(Y, g * G + ti, psum[:, ob, :], to, f)
                        o_free[ob] = yr[g * G + ti]

                scores(0)
                for h in range(2 * G + 2):
                    if h >= 2:
                        values(h - 2)
                    if h + 1 < 2 * G:
                        scores(h + 1)
                    if h < 2 * G:
                        weigh(h)
                end = fence()
                for b in range(8):
                    bank_free[b] = end
            state["area_free"] = fence()
            return project_back(Y, yr, w_o, 0, KD, out_gain(), x_ready, next_norm)[1]

        def rglru(norm, x_ready, next_norm):
            hr = norm.out
            w0 = product(H, hr, [piece(t["lru_w_in"][0][:, 0:PANEL], KD)], range(KD), PANEL, None, mid=norm.during)
            state["area_free"] = fence()
            gate = norm.out_gain()
            w_in, w_out = t["lru_w_in"][0], t["lru_w_out"][0]
            stream.low_by = pool
            NB = RNN // P
            f = fence()
            c = Carver()
            c.at = 2 * S
            w_r, w_i = c.new(NB, P), c.new(NB, P)
            gel, xcs = [c.new(2, S) for _ in range(2)], [c.new(2, S) for _ in range(2)]
            rr, ii, aa, th = (c.new(2, S) for _ in range(4))
            xpad = c.new(2, S + 3)
            sp.load(w_r, t["lru_w_r"][0].rearrange("n k j -> k n j"), s_gate_w, counts, after=[f])
            tw = sp.load(w_i, t["lru_w_i"][0].rearrange("n k j -> k n j"), s_gate_w, counts, after=[f])
            tz = dve.do(lambda e: e.memset(xpad[:, :, 0:3], 0.0), after=[f])
            y_reads = f
            free = {}
            front = {}

            def project_in(n0, between=None):
                base, tok = w0 if n0 == 0 else product(H, hr, [piece(w_in[:, n0 * P:n0 * P + PANEL], KD)], range(KD), PANEL, None)
                if between:
                    between()
                tg = act.do(lambda e: e.activation(gel[n0 // 2 % 2], psum[:, base:base + 2, :], ACT.Gelu_apprx_tanh),
                            after=[tok, f, free.get(("gel", n0 // 2 % 2))])
                free_pair(base, [tg])
                base, tok = product(H, hr, [piece(w_in[:, RNN + n0 * P:RNN + n0 * P + PANEL], KD)], range(KD), PANEL, None)
                tx = act.do(lambda e: e.copy(xpad[:, :, 3:S + 3], psum[:, base:base + 2, :]), after=[tok, f, free.get("xpad")])
                free_pair(base, [tx])
                xc = xcs[n0 // 2 % 2]
                tds = []
                for m in range(2):
                    n = n0 + m
                    td = dve.do(lambda e: e.tensor_scalar(xc[:, m, :], xpad[:, m, 0:S], v("lru_conv_w", n), v("lru_conv_b", n), ALU.mult, ALU.add),
                                after=[tx, tz, free.get(("xc", n0 // 2 % 2))])
                    for tap in range(1, 4):
                        td = dve.do(lambda e: e.scalar_tensor_tensor(xc[:, m, :], xpad[:, m, tap:tap + S], v("lru_conv_w", tap * NB + n), xc[:, m, :],
                                                                     ALU.mult, ALU.add), after=[td])
                    tds.append(td)
                free["xpad"] = td
                front[n0] = (tg, tds)

            def recur(n0, yr, y_reads):
                tg, tds = front[n0]
                xc, gl = xcs[n0 // 2 % 2], gel[n0 // 2 % 2]
                br, fr = take_pair()
                bi, fi = take_pair()
                sig = []
                for m in range(2):
                    n = n0 + m
                    tr = pe.do(lambda e: e.matmul(psum[:, br + m, :], w_r[:, n, :], xc[:, m, :], start=True, stop=True), after=[tds[m], tw, fr])
                    ts = pe.do(lambda e: e.matmul(psum[:, bi + m, :], w_i[:, n, :], xc[:, m, :], start=True, stop=True), after=[tds[m], tw, fi])
                    s1 = act.do(lambda e: e.activation(rr[:, m, :], psum[:, br + m, :], ACT.Sigmoid, bias=v("lru_b_r", n)), after=[tr, free.get("rr")])
                    s2 = act.do(lambda e: e.activation(ii[:, m, :], psum[:, bi + m, :], ACT.Sigmoid, bias=v("lru_b_i", n)), after=[ts, free.get("ii")])
                    sig.append((s1, s2))
                free_pair(br, [s1])
                free_pair(bi, [s2])
                e2 = []
                for m in range(2):
                    n = n0 + m
                    a1 = act.do(lambda e: e.activation(aa[:, m, :], rr[:, m, :], ACT.Exp, scale=v("decay", n)),
                                after=[sig[m][0], state["decay"], free.get("aa")])
                    a2 = act.do(lambda e: e.activation(th[:, m, :], rr[:, m, :], ACT.Tanh, scale=v("decay", n)), after=[sig[m][0], free.get("th")])
                    e2.append((a1, a2))
                d1 = act.do(lambda e: e.activation(rr, aa, ACT.Square), after=[e2[0][0], e2[1][0], e2[1][1]])

                def second():
                    d2 = dve.do(lambda e: e.scalar_tensor_tensor(th, rr, 1.0, th, ALU.add, ALU.mult), after=[d1, e2[1][1]])
                    a3 = act.do(lambda e: e.activation(th, th, ACT.Sqrt, scale=-1.0), after=[d2])
                    p1 = pool.do(lambda e: e.tensor_tensor(ii, ii, xc, ALU.mult), after=[sig[1][1], tds])
                    free["xc", n0 // 2 % 2] = [p1, ts]
                    d3 = dve.do(lambda e: e.tensor_tensor(ii, ii, th, ALU.mult), after=[p1, a3])
                    for m in range(2):
                        d4 = dve.do(lambda e: e.tensor_tensor_scan(rr[:, m, :], aa[:, m, :], ii[:, m, :], 0.0, ALU.mult, ALU.add), after=[d3])
                    free["aa"] = free["ii"] = d4
                    free["th"] = d3
                    d5 = pool.do(lambda e: e.tensor_tensor(rr, rr, gl, ALU.mult), after=[d4, tg])
                    free["gel", n0 // 2 % 2] = d5
                    for m in range(2):
                        both = yr[(n0 + m) % KD] = split_into(Y, (n0 + m) % KD, rr[:, m, :], d5, y_reads)
                    free["rr"] = both
                return second

            project_in(0)
            early = NB - KD
            second = None
            yr = [None] * KD
            y_reads = f
            for n0 in range(0, NB, 2):
                if n0 + 2 < NB:
                    project_in(n0 + 2, second)
                elif second:
                    second()
                second = recur(n0, yr, y_reads if n0 >= KD else f)
                if n0 == early:
                    tok, _ = project_back(Y, yr, w_out, 0, early, gate, x_ready)
                    y_reads = [tok]
            second()
            state["area_free"] = fence()
            tok, norm = project_back(Y, yr, w_out, early * P, KD, gate, x_ready, next_norm, first=early)
            stream.low_by = dve
            return norm

        IN = {}
        off = 0
        for name, n in (("a_q", 384), ("a_k", 384), ("a_v", 384), ("a_g", 384), ("b_q", 384), ("b_k", 64), ("b_v", 64), ("b_g", 384),
                        ("i_q", 256), ("i_k", 64), ("i_w", 4), ("c_q", 768), ("c_k", 768), ("c_v", 768), ("c_g", 256), ("m_g", 3 * D)):
            IN[name] = off
            off += n

        def hybrid(layer, norm, x_ready, next_norm):
            hr = norm.out
            w0 = product(H, hr, [piece(t["w_in_2"][layer][:, IN["i_q"]:IN["i_q"] + 256], KD)], range(KD), PANEL, None, mid=norm.during)
            w_in = t["w_in_2"][layer]
            stream.low_by = pool
            c = Carver()
            rope_x, rope_y = c.new(2, S), c.new(2, S)
            SS_at = c.at
            SS = [c.new(TRI) for _ in range(3)]
            PT_at = c.at
            PT = c.new(TRI)
            score_at = c.at
            score = c.new(TRI)
            pool_at = c.at
            tiles = c.new(9, S)
            bv = c.new(NT, HD)

            def unused(i, j0, j1):
                return y_plain[:, i, j0:j1, :]

            ag, bg = unused(1, 0, 3), unused(1, 3, 6)
            iq, ik = unused(0, 3, 5), unused(0, 5, 6)
            aq, ak, av = tiles[:, 0:3, :], tiles[:, 3:6, :], area[:, pool_at + 6 * S:pool_at + 9 * S].rearrange("p (n c) -> p n c", n=NT)
            bq = [unused(0, 6, 7), unused(0, 7, 8), unused(1, 6, 7)]
            bk = unused(1, 7, 8)

            def token_tiles(at):
                return area[:, at:at + 2 * S].rearrange("p (n c) -> p n c", n=NT)

            cqs = [tiles[:, 0:2, :], tiles[:, 4:6, :], tiles[:, 0:2, :]]
            cks = [tiles[:, 2:4, :], area[:, score_at:score_at + 2 * S].rearrange("p (a b) -> p a b", a=2), tiles[:, 2:4, :]]
            cvs = [token_tiles(pool_at + 6 * S), unused(0, 6, 8).rearrange("p a b -> p (a b)").rearrange("p (n c) -> p n c", n=NT),
                   token_tiles(pool_at + 6 * S)]
            og = [unused(1, 6, 8), tiles[:, 4:6, :], area[:, score_at:score_at + 2 * S].rearrange("p (a b) -> p a b", a=2)]
            cg = tiles[:, 0:2, :]
            sg = [rope_x, rope_y, area[:, PT_at:PT_at + 2 * S].rearrange("p (a b) -> p a b", a=2)]
            masks = [mod_acc[:, 0:7 * P], inv[:, :], mod_acc[:, 0:4 * P]]
            stat = mod_acc[:, 7 * P:7 * P + 48]
            lse = [mod_acc[:, 7 * P + 48 + 16 * g:7 * P + 64 + 16 * g].rearrange("p (n h) -> p n h", n=NT) for g in range(3)]
            iwT, best = small[:, 2:2 + 4 * NT].rearrange("p (n h) -> p n h", n=NT), small[:, 24:56]

            f = fence()
            rope_free = {"x": f, "y": f}

            def columns(name, c0, n, widths):
                o = IN[name] + c0
                return product(H, hr, [piece(w_in[:, o:o + n], KD)], range(KD), n, None, widths)

            def rope(base, tok, dsts, parts=(P, P), after=None, dil=1):
                n = len(dsts)
                ta = act.do(lambda e: e.copy(rope_x[0:parts[0], 0:n, :], psum[0:parts[0], base:base + n, :]), after=[tok, rope_free["x"]])
                for r in range(0, parts[0], 64):
                    m = sum(1 for p in parts[:n] if p > r)
                    for a, b in ((r, r + 32), (r + 32, r)):
                        tswap = sp.load(rope_y[a:a + 32, 0:m, :], rope_x[b:b + 32, 0:m, :], s_swap, counts, after=[ta, rope_free["y"]])
                toks = []

                def split_tokens(ap):
                    return ap if dil == 1 else ap.rearrange("p (j r) -> p j r", r=dil)

                def to(m):
                    a = dsts[m][0:parts[m], :]
                    return a if dil == 1 else a.rearrange("p (r j) -> p j r", r=dil)

                def rest():
                    for m in range(n):
                        eng = pool if m == 0 else dve
                        p = parts[m]
                        t1 = eng.do(lambda e: e.tensor_tensor(to(m), split_tokens(rope_x[0:p, m, :]), split_tokens(rope_c[0:p, :]), ALU.mult),
                                    after=[ta, tswap, after])
                        t2 = dve.do(lambda e: e.tensor_tensor(rope_y[0:p, m, :], rope_y[0:p, m, :], rope_s[0:p, :], ALU.mult),
                                    after=[tswap])
                        t3 = dve.do(lambda e: e.tensor_tensor(to(m), to(m), split_tokens(rope_y[0:p, m, :]), ALU.add), after=[t1, t2])
                        toks.append(t3)
                        toks.append(t1)
                    rope_free["x"] = toks + [tswap]
                    rope_free["y"] = t3
                return ta, toks, rest

            def roped(name, c0, dsts, got, after=None, dil=1):
                base, tok = w0 if name == "i_q" else columns(name, c0, P * len(dsts), (P,) * len(dsts))
                ta, toks, rest = rope(base, tok, dsts, after=after, dil=dil)
                free_pair(base, [ta])

                def finish():
                    rest()
                    got.append(toks)
                return finish

            def token_major(name, c0, n, dst, got, after=None):
                o = IN[name] + c0
                base, view, tok = product_tok(H, hr, [piece(w_in[:, o:o + n], KD)], n)
                ta = act.do(lambda e: e.copy(dst, view), after=[tok, after])
                free_pair(base, [ta])
                got.append(ta)

            def gate_tiles(name, c0, n, dst, got, after=None):
                widths = (P,) * (n // P)
                base, tok = columns(name, c0, n, widths)
                m = len(widths)
                ta = act.do(lambda e: e.activation(dst, psum[:, base:base + m, :], ACT.Sigmoid), after=[tok, after])
                act.do(lambda e: e.preload_act_table_set("natural_log_exp_and_others"), signal=False)

                def rest():
                    td = dve.do(lambda e: e.tensor_tensor(dst, dst, psum[:, base:base + m, :], ALU.mult), after=[ta])
                    free_pair(base, [td])
                    got.append(td)
                return rest

            t_iq, t_ik, t_a, t_ag = [], [], [], []
            roped("i_q", 0, [iq[:, 0, :], iq[:, 1, :]], t_iq, f)()
            base, tok = columns("i_k", 0, 68, (68,))
            ta, toks, rest = rope(base, tok, [ik[:, 0, :]], parts=(64,), after=f)
            t_iw = act.do(lambda e: e.mul(SS[0][64:68, 0:S], psum[64:68, base, :], 1.0 / 16.0), after=[tok, f])
            free_pair(base, [ta, t_iw])
            token_major("a_v", 0, 256, av[:, :, 0:256], t_a, f)
            only_pair[0] = 6
            base_q, tok_q = columns("a_q", 0, 256, (P, P))
            only_pair[0] = None
            rest()
            t_ik = [toks, sp.load(ik[64:P, :, :], ik[0:64, :, :], s_dup, counts, after=[toks, f])]
            ta_q, toks_q, rest_q = rope(base_q, tok_q, [aq[:, 0, :], aq[:, 1, :]], after=f)
            free_pair(base_q, [ta_q])
            for n in range(NT):
                tt = pe.do(lambda e: e.transpose(psum[:, 5, 4 * n:4 * n + 4], SS[0][64:68, n * P:(n + 1) * P], ident[64:68, 64:68]),
                           after=[t_iw, bank_free[5]], signal=n == NT - 1)
            t_iw = act.do(lambda e: e.copy(iwT, psum[:, 5, 0:16].rearrange("p (n h) -> p n h", n=NT)), after=[tt, f])
            bank_free[5] = [t_iw]
            relu_read = [t_iw, t_iw]
            relu_done = [bank_free[0:3], bank_free[3:6]]
            for h in range(4):
                g, r0 = h % 2, (h % 2) * HD
                relu = SS[g]
                for n in range(NT):
                    tp = pe.do(lambda e: e.matmul(
                        flat[:, 1536 * g + ROW_AT[n]:1536 * g + ROW_AT[n] + P * (n + 1)], iq[r0:r0 + HD, h // 2, n * P:(n + 1) * P],
                        ik[r0:r0 + HD, 0, 0:P * (n + 1)], start=True, stop=True),
                        after=[t_iq, t_ik, relu_done[g]], signal=n == NT - 1)
                ta = act.do(lambda e: e.activation(relu, flat[:, 1536 * g:1536 * g + TRI], ACT.Relu), after=[tp, relu_read[g], f])
                relu_done[g] = ta
                for n in range(NT):
                    a, b = ROW_AT[n], ROW_AT[n] + P * (n + 1)
                    if h == 0:
                        td = dve.do(lambda e: e.tensor_scalar(score[:, a:b], relu[:, a:b], iwT[:, n, h:h + 1], None, ALU.mult), after=[ta, t_iw, f])
                    else:
                        td = dve.do(lambda e: e.scalar_tensor_tensor(score[:, a:b], relu[:, a:b], iwT[:, n, h:h + 1], score[:, a:b],
                                                                     ALU.mult, ALU.add), after=[ta, td])
                relu_read[g] = td
            for b in range(6):
                bank_free[b] = [relu_done[b // 3]]
            for n in range(1, NT):
                b = ROW_AT[n] + P * (n + 1)
                blk = score[:, b - P:b]
                tm = pool.do(lambda e: e.affine_select(out=blk, in_=blk, pattern=[[-1, P]], compare_op=ALU.is_ge, fill=NOT_CAUSAL,
                                                       base=0, channel_multiplier=1), after=[td])
            rest_q()
            t_a.append(toks_q)
            picked = {}

            def top8(n):
                a, b = ROW_AT[n], ROW_AT[n] + P * (n + 1)
                m8 = best[:, 8 * n:8 * n + 8]
                d1 = dve.do(lambda e: e.max(m8, score[:, a:b]), after=[picked.get(n), tm, td])
                picked[n] = dve.do(lambda e: e.match_replace(score[:, a:b], m8, score[:, a:b], PICKED), after=[d1])

            rounds = [n for _ in range(P // 8) for n in range(1, NT)]

            def some(n):
                for _ in range(min(n, len(rounds))):
                    top8(rounds.pop(0))

            t_sel = []

            def select():
                some(len(rounds))
                for n in range(1, NT):
                    a, b = ROW_AT[n], ROW_AT[n] + P * (n + 1)
                    d = dve.do(lambda e: e.tensor_scalar(score[:, a:b], score[:, a:b], PICKED_BELOW, MASKED, ALU.is_ge, ALU.mult), after=[picked[n]])
                a, b = ROW_AT[0], ROW_AT[0] + P
                t_sel.append(dve.do(lambda e: e.tensor_copy(score[:, a:b], causal[:, a:b]), after=[d, state["masks"]]))

            base, tok = columns("a_q", 256, 256, (P, P))
            ta, toks, rest = rope(base, tok, [aq[:, 2, :], ak[:, 0, :]], after=f)
            free_pair(base, [ta])
            some(4)
            rest()
            t_a.append(toks)
            rest = roped("a_k", 128, [ak[:, 1, :], ak[:, 2, :]], t_a, f)
            some(5)
            rest()
            base, tok = columns("a_v", 256, 256, (P, P))
            t_v = act.do(lambda e: e.copy(rope_x[:, 0, :], psum[:, base, :]), after=[tok, rope_free["x"]])
            ta = act.do(lambda e: e.activation(ag[:, 0, :], psum[:, base + 1, :], ACT.Sigmoid), after=[tok, f])
            some(6)
            td = dve.do(lambda e: e.tensor_tensor(ag[:, 0, :], ag[:, 0, :], psum[:, base + 1, :], ALU.mult), after=[ta])
            t_ag.append(td)
            free_pair(base, [t_v, td])
            rest = gate_tiles("a_g", 128, 256, ag[:, 1:3, :], t_ag, f)
            base, fr = take_pair()
            for n in range(NT):
                tt = pe.do(lambda e: e.transpose(psum[:, base, n * P:(n + 1) * P], rope_x[:, 0, n * P:(n + 1) * P], ident[:, :]),
                           after=[t_v, fr], signal=n == NT - 1)
            ta = act.do(lambda e: e.copy(av[:, :, 256:384], psum[:, base, :].rearrange("p (n c) -> p n c", n=NT)), after=[tt, f])
            rope_free["x"] = rope_free["x"] + [tt]
            free_pair(base, [ta])
            t_a.append(ta)
            some(6)
            rest()

            def dilated_mask(g, after):
                mk = masks[g]
                if g == 0:
                    tk = pool.do(lambda e: e.memset(mk, 0.0), after=[after])
                    for u in range(7):
                        blk = mk[:, u * P:(u + 1) * P]
                        own = u % 2 == 0
                        tk = pool.do(lambda e: e.affine_select(
                            out=blk, in_=blk, pattern=[[-1 if own else 1, P]], compare_op=ALU.is_ge, fill=MASKED, base=0,
                            channel_multiplier=1 if own else -1), after=[tk])
                    return tk
                tk = pool.do(lambda e: e.memset(mk, 0.0), after=[after])
                tk = pool.do(lambda e: e.affine_select(out=mk, in_=mk, pattern=[[0, 4], [-1, P]],
                                                       compare_op=ALU.is_ge, fill=MASKED, base=0, channel_multiplier=1), after=[tk])
                if g == 2:
                    n_sub = S // 16
                    for u in range(1, P // n_sub):
                        blk = mk.rearrange("p (n c) -> p n c", n=4)[:, :, (u - 1) * n_sub:u * n_sub]
                        tk = pool.do(lambda e: e.affine_select(out=blk, in_=blk, pattern=[[0, 4], [0, n_sub]], compare_op=ALU.is_gt,
                                                               fill=MASKED, base=u * n_sub, channel_multiplier=-1), after=[tk])
                return tk

            t_mask = [[], [], []]

            yr = [None] * KD
            ROWS = [(ROW_AT[n], ROW_AT[n] + P * (n + 1), 1) for n in (0, 1, 2, 3)]
            TURNS = [(ROW_AT[n] + P * kt, COL_AT[kt] + P * (n - kt)) for kt in (0, 1, 3, 2) for n in range(kt, NT)]
            OUT = 5
            o_read = [[]]
            heads = []

            def causal_heads(y0, q_of, k_of, v_of, n_heads, mask, ready, gates, gates_ready):
                for h in range(n_heads):
                    ti, r0 = h // 2, (h % 2) * HD

                    def scores(after, ti=ti, r0=r0, h=h):
                        for n in range(NT):
                            tok = pe.do(lambda e: e.matmul(flat[:, ROW_AT[n]:ROW_AT[n] + P * (n + 1)], q_of(ti)[r0:r0 + HD, n * P:(n + 1) * P],
                                                           k_of(h)[:, 0:P * (n + 1)], start=True, stop=True),
                                        after=[after, ready], signal=n == NT - 1)
                        return tok

                    def outs(ta, ti=ti, r0=r0, h=h):
                        for kt in range(NT):
                            tok = pe.do(lambda e: e.matmul(psum[r0:r0 + HD, OUT, kt * P:S], v_of(h, kt),
                                                           PT[:, COL_AT[kt]:COL_AT[kt] + S - P * kt], start=kt == 0, stop=kt == NT - 1,
                                                           skip_group_check=True),
                                        after=[ta, ready, o_read[0]], signal=kt == NT - 1)
                        return tok

                    def finish(s, to, ti=ti, h=h):
                        if h % 2 == 0:
                            return None
                        d = dve.do(lambda e: e.tensor_tensor(gates[:, ti, :], gates[:, ti, :], psum[:, OUT, :], ALU.mult), after=[to, gates_ready])
                        o_read[0] = [d]
                        yr[y0 + ti] = split_into(Y, y0 + ti, gates[:, ti, :], d, f)
                        return None

                    heads.append((scores, 0, TRI, mask, ROWS, TURNS, outs, finish))

            def dilated_heads(g, dil, ready):
                qq, kk, vv = cqs[g], cks[g], cvs[g]
                for sl in range(4):
                    ti, r0 = sl // 2, (sl % 2) * HD

                    def scores(after, ti=ti, r0=r0):
                        for n in range(NT):
                            if g == 0:
                                lo = 0 if n == 0 else P * (2 * n - 1)
                                k0 = P * max(n - 1, 0)
                                for u in range(1 if n == 0 else 2):
                                    tok = pe.do(lambda e: e.matmul(
                                        flat[:, lo + u * P:lo + u * P + P], qq[r0:r0 + HD, ti, n * P:(n + 1) * P],
                                        kk[r0:r0 + HD, ti, k0 + u * P:k0 + u * P + P], start=True, stop=True), after=[after, ready])
                            else:
                                tok = pe.do(lambda e: e.matmul(
                                    flat[:, n * P:(n + 1) * P], qq[r0:r0 + HD, ti, n * P:(n + 1) * P],
                                    kk[r0:r0 + HD, ti, n * P:(n + 1) * P], start=True, stop=True), after=[after, ready])
                        return tok

                    def outs(ta, ti=ti, r0=r0, sl=sl):
                        for n in range(NT):
                            if g == 0:
                                terms = [(n, 2 * n * P)] + ([(n - 1, (2 * n - 1) * P)] if n else [])
                            else:
                                terms = [(n, n * P)]
                            for i, (kt, o) in enumerate(terms):
                                tok = pe.do(lambda e: e.matmul(
                                    psum[r0:r0 + HD, OUT, n * P:(n + 1) * P], vv[:, kt, sl * HD:(sl + 1) * HD], PT[:, o:o + P],
                                    start=i == 0, stop=i == len(terms) - 1, skip_group_check=True), after=[ta, ready, o_read[0]])
                        return tok

                    def finish(s, to, ti=ti, sl=sl):
                        m0 = 16 * s
                        ta = act.do(lambda e: e.activation(lse[g][:, :, sl], stat[:, m0 + 8:m0 + 12], ACT.Ln), after=[act.last()])
                        td = dve.do(lambda e: e.tensor_tensor(lse[g][:, :, sl], lse[g][:, :, sl], stat[:, m0:m0 + 4], ALU.add), after=[ta])
                        if sl % 2:
                            dst = og[g][:, ti, :]
                            src = psum[:, OUT, :]
                            if dil > 1:
                                dst = dst.rearrange("p (j r) -> p r j", r=dil)
                                src = src.rearrange("p (r j) -> p r j", r=dil)
                            tc = act.do(lambda e: e.copy(dst, src), after=[to])
                            o_read[0] = [tc]
                        return td

                    width = 7 if g == 0 else 4
                    rows = [(0, P, 1), (P, 7 * P, 3)] if g == 0 else [(0, 4 * P, 4)]
                    turns = [(i * P, i * P) for i in range(width)]
                    heads.append((scores, 0, width * P, (masks[g], t_mask[g]), rows, turns, outs, finish))

            t_b, t_bg, t_c, t_cg, t_sg = [], [], [[], [], []], [], {}
            causal_heads(0, lambda ti: aq[:, ti, :], lambda h: ak[(h % 2) * HD:(h % 2) * HD + HD, h // 2, :],
                         lambda h, kt: av[:, kt, h * HD:(h + 1) * HD], 6, (causal[:, :], [state["masks"]]), t_a, ag, t_ag)
            causal_heads(3, lambda ti: bq[ti][:, 0, :], lambda h: bk[(h % 2) * HD:(h % 2) * HD + HD, 0, :],
                         lambda h, kt: bv[:, kt, :], 6, (score, t_sel), t_b, bg, t_bg)
            for g, dil in enumerate((1, 4, 16)):
                dilated_heads(g, dil, t_c[g])

            scores_read = [fence()]

            def queries_key_and_values():
                base, tok = columns("b_q", 256, 256, (P, P))
                ta, toks, rest = rope(base, tok, [bq[2][:, 0, :], bk[:, 0, :]], parts=(P, 64), after=f)
                free_pair(base, [ta])

                def finish():
                    rest()
                    t_b.append([toks, sp.load(bk[64:P, :, :], bk[0:64, :, :], s_dup, counts, after=[toks, f])])
                    base, fr = take_pair()
                    for n in range(NT):
                        tt = pe.do(lambda e: e.transpose(psum[:, base, n * HD:(n + 1) * HD], rope_x[64:P, 1, n * P:(n + 1) * P], ident[64:P, 64:P]),
                                   after=[ta, fr], signal=n == NT - 1)
                    tv = act.do(lambda e: e.copy(bv, psum[:, base, 0:NT * HD].rearrange("p (n c) -> p n c", n=NT)), after=[tt, f])
                    rope_free["x"] = rope_free["x"] + [tt]
                    free_pair(base, [tv])
                    t_b.append(tv)
                return finish

            def dilated_values(g, dil):
                base, tok = columns("c_v", g * PANEL, PANEL, (P, P))
                for m in range(2):
                    ta = act.do(lambda e: e.copy(rope_x[:, m, :].rearrange("p (r j) -> p r j", r=dil),
                                                 psum[:, base + m, :].rearrange("p (j r) -> p r j", r=dil)),
                                after=[tok, rope_free["x"]])
                free_pair(base, [ta])

                def rest():
                    base, fr = take_pair()
                    for m in range(2):
                        for r_ in range(NT):
                            o = (base + r_ // 2) * 512 + (r_ % 2) * PANEL + m * P
                            tt = pe.do(lambda e: e.transpose(flat[:, o:o + P], rope_x[:, m, r_ * P:(r_ + 1) * P], ident[:, :]),
                                       after=[ta, fr], signal=(m, r_) == (1, NT - 1))
                    tv = act.do(lambda e: e.copy(cvs[g], flat[:, base * 512:(base + 2) * 512].rearrange("p (t c) -> p t c", c=PANEL)),
                                after=[tt])
                    rope_free["x"] = tt
                    free_pair(base, [tv])
                    t_c[g].append(tv)
                return rest

            def merge_gate(b, jj):
                base, tok = columns("m_g", b * D + jj * PANEL, PANEL, (P, P))
                ta = act.do(lambda e: e.activation(sg[b], psum[:, base:base + 2, :], ACT.Sigmoid), after=[tok, sg_free[b]])
                free_pair(base, [ta])
                t_sg[b] = ta

            def merge_gate_early(b):
                sg_free[b] = rope_free["x"] if b == 0 else rope_free["y"]
                merge_gate(b, 0)
                act.do(lambda e: e.preload_act_table_set("natural_log_exp_and_others"), signal=False)

            sg_free = [None] * 3

            def c_tiles(name, g, dst):
                dil = (1, 4, 16)[g]
                return roped(name, g * PANEL, [dst[:, 0, :], dst[:, 1, :]], t_c[g], [scores_read[0]], dil)

            def make_mask(g, after):
                t_mask[g].append(dilated_mask(g, after))

            fills = {
                0: lambda: roped("b_q", 0, [bq[0][:, 0, :], bq[1][:, 0, :]], t_b, f),
                1: queries_key_and_values,
                2: lambda: gate_tiles("b_g", 0, 256, bg[:, 0:2, :], t_bg, f),
                4: lambda: gate_tiles("b_g", 256, 128, bg[:, 2:3, :], t_bg, f),
                5: lambda: c_tiles("c_q", 0, cqs[0]),
                6: lambda: c_tiles("c_k", 0, cks[0]),
                8: lambda: token_major("c_v", 0, PANEL, cvs[0], t_c[0]),
                9: lambda: c_tiles("c_q", 1, cqs[1]),
                12: lambda: c_tiles("c_k", 1, cks[1]),
                13: lambda: dilated_values(1, 4),
                15: lambda: c_tiles("c_q", 2, cqs[2]),
                16: lambda: c_tiles("c_k", 2, cks[2]),
                18: lambda: dilated_values(2, 16),
                20: lambda: merge_gate_early(0),
                21: lambda: merge_gate_early(1),
                23: lambda: gate_tiles("c_g", 0, 256, cg, t_cg),
            }
            beside = {0: lambda: some(6), 1: lambda: some(6), 2: lambda: some(6), 3: lambda: some(6), 5: select,
                      7: lambda: make_mask(0, f), 11: lambda: make_mask(1, [f, state.get(("inv_read", 0)), state.get(("inv_read", 1))]),
                      17: lambda: make_mask(2, scores_read[0])}

            TURNED = TRI
            banks = [list(x) for x in bank_free[0:6]]
            only_pair[0] = 6
            act.do(lambda e: e.preload_act_table_set("natural_log_exp_and_others"), signal=False)
            s_free = [scores_read[0]] * 3
            pt_free, pt_copied = [scores_read[0]], [None]
            got, peak, weights, turned, copied = {}, {}, {}, {}, {}

            def spans(rows):
                out = []
                for a, b, n in rows:
                    step = (b - a) // n
                    out += [(a + u * step, a + (u + 1) * step) for u in range(n)]
                return list(enumerate(out))

            def do_scores(h):
                got[h] = heads[h][0]([scores_read[0], banks])

            def do_max(h):
                _, lo, hi, mask, rows, _, _, _ = heads[h]
                s, buf, m0 = h % 3, SS[h % 3], 16 * (h % 3)
                d = dve.do(lambda e: e.scalar_tensor_tensor(buf[:, lo:hi], flat[:, lo:hi], SCALE, mask[0], ALU.mult, ALU.add),
                           after=[got[h], s_free[s], mask[1], turned.get(h - 2)])
                scores_read[0] = d
                i = 0
                for a, b, n in rows:
                    dm = dve.do(lambda e: e.tensor_reduce(stat[:, m0 + i:m0 + i + n], buf[:, a:b].rearrange("p (n c) -> p n c", n=n), AX.X, ALU.max),
                                after=[d, s_free[s]])
                    i += n
                peak[h] = dve.do(lambda e: e.tensor_scalar(stat[:, m0 + 4:m0 + 8], stat[:, m0:m0 + 4], -1.0, None, ALU.mult), after=[dm, s_free[s]])

            def do_weights(h):
                rows = heads[h][4]
                buf, m0 = SS[h % 3], 16 * (h % 3)
                for w, (a, b) in spans(rows):
                    ta = act.do(lambda e: e.activation(buf[:, a:b], buf[:, a:b], ACT.Exp, bias=stat[:, m0 + 4 + w:m0 + 5 + w],
                                                       accum_out=stat[:, m0 + 8 + w:m0 + 9 + w]), after=[peak[h]])
                dr = dve.do(lambda e: e.reciprocal(stat[:, m0 + 12:m0 + 16], stat[:, m0 + 8:m0 + 12]), after=[ta])
                for w, (a, b) in spans(rows):
                    dn = dve.do(lambda e: e.tensor_scalar(buf[:, a:b], buf[:, a:b], stat[:, m0 + 12 + w:m0 + 13 + w], None, ALU.mult), after=[dr])
                weights[h] = dn

            def do_turns(h):
                turns, buf = heads[h][5], SS[h % 3]
                for src, dst in turns:
                    turned[h] = pe.do(lambda e: e.transpose(flat[:, TURNED + dst:TURNED + dst + P], buf[:, src:src + P], ident[:, :]),
                                      after=[weights[h], pt_copied[0]], signal=(src, dst) == turns[-1])

            def do_copy(h):
                top = max(d for _, d in heads[h][5]) + P
                mine = 2 * P if heads[h][2] > 2 * 512 else 0
                ta = act.do(lambda e: e.copy(PT[:, mine:top], flat[:, TURNED + mine:TURNED + top]), after=[turned[h], pt_free[0]])
                td = dve.do(lambda e: e.tensor_copy(PT[:, 0:mine], flat[:, TURNED:TURNED + mine]), after=[turned[h], pt_free[0]]) if mine else None
                copied[h] = pt_copied[0] = [ta, td]

            def do_values(h):
                outs, finish = heads[h][6:]
                pt_free[0] = outs(copied[h])
                s_free[h % 3] = [turned[h], finish(h % 3, pt_free[0])]

            n_heads = len(heads)
            rest = None
            do_scores(0)
            for i in range(n_heads + 2):
                if i >= 2:
                    do_turns(i - 2)
                    do_copy(i - 2)
                if i < n_heads:
                    do_max(i)
                if 1 <= i <= n_heads:
                    do_weights(i - 1)
                if rest:
                    rest()
                rest = fills[i]() if i in fills else None
                if i in beside:
                    beside[i]()
                if i + 1 < n_heads:
                    do_scores(i + 1)
                if i >= 2:
                    do_values(i - 2)
            for b in range(5):
                bank_free[b] = [scores_read[0], pt_copied[0]]
            bank_free[OUT] = [o_read[0], state["masks"]]
            only_pair[0] = None

            f = fence()
            c.at = SS_at
            L = [c.new(S) for _ in range(3)]
            M = c.new(S)
            sel = c.new(2, P)
            t_cg = t_cg[0]
            tm = pool.do(lambda e: e.memset(sel[0:4, :, :], 1.0), after=[f])
            tm = pool.do(lambda e: e.affine_select(out=sel[0:4, :, :], in_=sel[0:4, :, :], pattern=[[P, 2], [1, P]], compare_op=ALU.is_ge,
                                                   fill=0.0, base=0, channel_multiplier=-HD), after=[tm])
            tm = pool.do(lambda e: e.affine_select(out=sel[0:4, :, :], in_=sel[0:4, :, :], pattern=[[-P, 2], [-1, P]], compare_op=ALU.is_gt,
                                                   fill=0.0, base=HD, channel_multiplier=HD), after=[tm])
            lt = []
            for g, dil in enumerate((1, 4, 16)):
                b, _ = take_pair()
                for n in range(NT):
                    tt = pe.do(lambda e, g=g, n=n, b=b: e.transpose(psum[0:4, b, n * P:(n + 1) * P], lse[g][:, n, :], ident[:, :]),
                               after=[f, bank_free[b]], signal=n == NT - 1)
                src, dst = psum[0:4, b, :], L[g][0:4, :]
                if dil > 1:
                    src = src.rearrange("p (r j) -> p r j", r=dil)
                    dst = dst.rearrange("p (j r) -> p r j", r=dil)
                ta = act.do(lambda e, src=src, dst=dst: e.copy(dst, src), after=[tt, f])
                free_pair(b, [ta])
                lt.append(ta)
            l3 = [x[0:4, :] for x in L]
            mm = M[0:4, :]
            d = dve.do(lambda e: e.tensor_tensor(mm, l3[0], l3[1], ALU.max), after=[lt, f])
            d = dve.do(lambda e: e.tensor_tensor(mm, mm, l3[2], ALU.max), after=[d])
            es = []
            for g in range(3):
                dd = dve.do(lambda e, g=g: e.tensor_tensor(l3[g], l3[g], mm, ALU.subtract), after=[d])
                es.append(act.do(lambda e, g=g: e.activation(l3[g], l3[g], ACT.Exp), after=[dd]))
            d = dve.do(lambda e: e.tensor_tensor(mm, l3[0], l3[1], ALU.add), after=[es, dd])
            d = dve.do(lambda e: e.tensor_tensor(mm, mm, l3[2], ALU.add), after=[d])
            d = dve.do(lambda e: e.reciprocal(mm, mm), after=[d])
            for g in range(3):
                dd = dve.do(lambda e, g=g: e.tensor_tensor(l3[g], l3[g], mm, ALU.mult), after=[d])
            sg_free[2] = f
            merge_gate(2, 0)
            for m in range(2):
                base, fr = take_pair()
                prev = None
                for g in range(3):
                    b = base + g % 2
                    tp = pe.do(lambda e, g=g, m=m, b=b: e.matmul(psum[:, b, :], sel[0:4, m, :], l3[g], start=True, stop=True),
                               after=[dd, tm, fr, prev])
                    prev = dve.do(lambda e, g=g, m=m, b=b: e.tensor_tensor(og[g][:, m, :], og[g][:, m, :], psum[:, b, :], ALU.mult), after=[tp, f])
                free_pair(base, [prev])
                d1 = dve.do(lambda e, m=m: e.tensor_tensor(og[0][:, m, :], og[0][:, m, :], og[1][:, m, :], ALU.add), after=[prev])
                d1 = dve.do(lambda e, m=m: e.tensor_tensor(og[0][:, m, :], og[0][:, m, :], og[2][:, m, :], ALU.add), after=[d1])
                d1 = dve.do(lambda e, m=m: e.tensor_tensor(cg[:, m, :], cg[:, m, :], og[0][:, m, :], ALU.mult), after=[d1, t_cg])
                yr[6 + m] = split_into(Y, 6 + m, cg[:, m, :], d1, f)

            f = fence()
            merged = area[:, score_at:score_at + KD * S].rearrange("p (a b) -> p a b", a=KD)
            mt = []
            br_w = (t["w_br_a_2"][layer], t["w_br_b_2"][layer], t["w_br_c_2"][layer])
            chunks = (range(0, 3), range(3, 6), range(6, 8))
            for jj in range(KD // 2):
                if jj:
                    for b in range(3):
                        merge_gate(b, jj)
                st = dict(t_sg)
                (wh, wl), wt, done = stream.take([piece(w[:, jj * PANEL:(jj + 1) * PANEL], len(ch), off=ch[0] * PANEL) for w, ch in zip(br_w, chunks)])
                wv = [w[:, :RAW].rearrange("p (k n) -> p k n", n=PANEL) for w in (wh, wl)]
                dst = merged[:, 2 * jj:2 * jj + 2, :]
                for b in range(3):
                    base, free = take_pair()
                    for m in range(2):
                        for i, k in enumerate(chunks[b]):
                            for x, y in ((0, 0), (0, 1), (1, 0)):
                                end = (x, y) == (1, 0) and i == len(chunks[b]) - 1
                                tok = pe.do(lambda e, m=m, i=i, k=k, x=x, y=y, end=end, base=base: e.matmul(
                                    psum[:, base + m, :], wv[x][:, k, m * P:(m + 1) * P], Y[y][:, k, :], start=(i == 0 and (x, y) == (0, 0)), stop=end),
                                    after=[wt, yr[k], free], signal=end)
                    td = dve.do(lambda e, b=b, base=base: e.tensor_tensor(sg[b], sg[b], psum[:, base:base + 2, :], ALU.mult), after=[tok, st[b]])
                    free_pair(base, [td])
                    if b == 1:
                        td = dve.do(lambda e: e.tensor_tensor(dst, sg[0], sg[1], ALU.add), after=[td, f])
                    if b == 2:
                        td = dve.do(lambda e: e.tensor_tensor(dst, dst, sg[2], ALU.add), after=[td])
                done(tok)
                sg_free[:] = [td, td, td]
                mt.append(td)
            old = fence()
            state["area_free"] = old
            mr = []
            for j in range(KD):
                mr.append(split_into(H, j, merged[:, j, :], mt[j // 2], old))
            return project_back(H, mr, t["w_out_2"][layer], 0, KD, None, x_ready, next_norm)[1]

        def program():
            tc = [pool.do(lambda e: e.memset(ones[:, :], 1.0)), pool.do(lambda e: e.memset(neg_ones[:, :], -1.0)),
                  pool.do(lambda e: e.memset(small[:, 0:1], EPS)), pool.do(lambda e: e.memset(causal[:, :], 0.0))]
            ti = pool.do(lambda e: e.affine_select(out=ident[:, :], in_=ones[:, :], pattern=[[1, P]], compare_op=ALU.is_equal, fill=0.0,
                                                   base=0, channel_multiplier=-1), after=tc)
            pool.do(lambda e: e.affine_select(out=neg_tri[:, :], in_=neg_ones[:, :], pattern=[[-1, P]], compare_op=ALU.is_ge, fill=0.0,
                                              base=0, channel_multiplier=1), after=[ti])
            for n in range(NT):
                blk = causal[:, ROW_AT[n] + n * P:ROW_AT[n] + (n + 1) * P]
                tm = pool.do(lambda e, blk=blk: e.affine_select(out=blk, in_=blk, pattern=[[-1, P]], compare_op=ALU.is_ge, fill=MASKED,
                                                                base=0, channel_multiplier=1), after=[ti])
            state["consts"] = state["masks"] = tm
            c = Carver()
            xin = c.new(NT, D)
            rows = c.new(len(groups), P)
            at = 0
            for g, names in enumerate(groups):
                r = 0
                for name, n in names:
                    src = t[name]
                    if name == "mod_b":
                        src = src[g - 1:g, :]
                    nd = len(src.shape)
                    src = (src.rearrange("(n p) -> n p", p=P) if nd == 1 else src.rearrange("a (n p) -> (a n) p", p=P) if nd == 2
                           else src.rearrange("a b (n p) -> (a b n) p", p=P))
                    tl = sp.load(rows[r:r + n, g, :], src, s_tab, counts)
                    r += n
            sp.load(rope_c[:, :], t["rope_cos"], s_tab, counts)
            tl = sp.load(rope_s[:, :], t["rope_sin"], s_tab, counts)
            if stream.plan is not None:
                for _ in range(NRAW):
                    stream.load_next()
            xl = sp.load(xin, t["x"][0].rearrange("(n p) d -> p n d", p=P), s_in, counts)
            b, fr = take_pair()
            for g, names in enumerate(groups):
                n = sum(k for _, k in names)
                tt = pe.do(lambda e, g=g, n=n, at=at: e.transpose(psum[:, b, at:at + n], rows[0:n, g, :], ident[0:n, 0:n]), after=[tl, tm])
                at += n
            tv = act.do(lambda e: e.copy(vec[:, 0:at], psum[:, b, 0:at]), after=[tt])
            free_pair(b, [tv])
            state["vec"] = tv
            state["c_act"] = act.do(lambda e: e.activation(v("c_act", 0, KD), v("c", 0, KD), ACT.Silu), after=[tv])
            x_ready = []
            for j in range(KD):
                if j % 2 == 0:
                    b, fr = take_pair()
                for n in range(NT):
                    tt = pe.do(lambda e, j=j, n=n, b=b: e.transpose(psum[:, b + j % 2, n * P:(n + 1) * P], xin[:, n, j * P:(j + 1) * P], ident[:, :]),
                               after=[xl, fr, tm], signal=n == NT - 1)
                tx = act.do(lambda e, j=j, b=b: e.copy(xT[:, j, :], psum[:, b + j % 2, :]), after=[tt])
                if j % 2:
                    free_pair(b, [tx])
                x_ready.append([tx, tx])
            state["area_free"] = fence()
            if stream.plan is not None:
                while stream.n_split < 1:
                    stream.split_next()
                stream.turn()
            norm = modulated(0, 0, 0.5, x_ready)
            norm.squares(0)
            norm.gather(0)
            norm.spread(0)
            norm.broadcast(0)
            norm.begin(0)
            norm = ffn(0, 0, norm, x_ready, lambda: modulated(0, 1, 1.0, x_ready))
            n = RNN // P
            lam, dec = v("lru_lambda", 0, n), v("decay", 0, n)
            e0, s0, s2, p0 = (small[:, 16 + 16 * i:16 + 16 * i + n] for i in range(4))
            a = act.do(lambda e: e.activation(e0, lam, ACT.Abs), after=[tv])
            a = act.do(lambda e: e.activation(e0, e0, ACT.Exp, scale=-1.0), after=[a])
            d = dve.do(lambda e: e.tensor_scalar(s0, e0, 2.0, None, ALU.add), after=[a])
            d = dve.do(lambda e: e.reciprocal(s0, s0), after=[d])
            d = dve.do(lambda e: e.tensor_tensor(s0, s0, e0, ALU.mult), after=[d])
            d = dve.do(lambda e: e.tensor_tensor(s2, s0, s0, ALU.mult), after=[d])
            TERMS = 9
            d = dve.do(lambda e: e.tensor_scalar(p0, s2, 1.0 / (2 * TERMS - 1), 1.0 / (2 * TERMS - 3), ALU.mult, ALU.add), after=[d])
            for i in range(TERMS - 3, -1, -1):
                d = dve.do(lambda e: e.tensor_tensor(p0, p0, s2, ALU.mult), after=[d])
                d = dve.do(lambda e, i=i: e.tensor_scalar(p0, p0, 1.0 / (2 * i + 1), None, ALU.add), after=[d])
            d = dve.do(lambda e: e.tensor_tensor(p0, p0, s0, ALU.mult), after=[d])
            d = dve.do(lambda e: e.tensor_scalar(s2, lam, -1.0, 0.0, ALU.mult, ALU.max), after=[d])
            d = dve.do(lambda e: e.scalar_tensor_tensor(p0, p0, 2.0, s2, ALU.mult, ALU.add), after=[d])
            state["decay"] = dve.do(lambda e: e.tensor_scalar(dec, p0, -8.0, None, ALU.mult), after=[d])
            norm = stick_breaking(norm, x_ready, lambda: modulated(0, 2, 0.5, x_ready))
            norm = ffn(0, 1, norm, x_ready, lambda: modulated(1, 0, 0.5, x_ready))
            norm = ffn(1, 0, norm, x_ready, lambda: modulated(1, 1, 1.0, x_ready))
            norm = rglru(norm, x_ready, lambda: modulated(1, 2, 0.5, x_ready))
            norm = ffn(1, 1, norm, x_ready, lambda: Norm(x_ready, xT, lambda j: v("final_norm_g", j), split=False))
            x_ready = norm.out
            second = Norm(x_ready, H, lambda j: v("norm_g_2", j))
            norm.during(2)
            second.squares(0)
            second.gather(0)
            norm.during(5)
            second.spread(0)
            second.broadcast(0)
            second.begin(0)
            norm = hybrid(0, second, x_ready, lambda: Norm(x_ready, H, lambda j: v("norm_g_2", KD + j)))
            norm = hybrid(1, norm, x_ready, lambda: Norm(x_ready, xT, lambda j: v("final_norm_g_2", j), split=False))
            norm.finish()
            c = Carver()
            c.at = 5 * S
            y = c.new(NT, D)
            for n in range(NT):
                b, fr = take_pair()
                for j in range(KD):
                    tt = pe.do(lambda e, j=j, n=n, b=b: e.transpose(flat[:, b * 512 + j * P:b * 512 + (j + 1) * P], xT[:, j, n * P:(n + 1) * P], ident[:, :]),
                               after=[norm.out[j][n // HT], fr], signal=j == KD - 1)
                ty = act.do(lambda e, n=n, b=b: e.copy(y[:, n, :], flat[:, b * 512:(b + 2) * 512]), after=[tt])
                free_pair(b, [ty])
                to = sp.load(out[0, n * P:(n + 1) * P, :], y[:, n, :], s_out, counts, after=[ty])
            sp.wait([to])

        stream = Stream(None, None, 0)
        program()
        asked = stream.asked
        for q in (pe, act, dve, pool, sp):
            q.value, q.items, q.waited = 0, [], {}
        counts.clear()
        state.clear()
        pairs[0] = 0
        bank_free[:] = [[] for _ in range(8)]
        stream = Stream(asked, mod_panels(), KD)
        program()

        block = ctx.enter_context(nc.Block())

        @block.sync
        def _(e):
            sp.play(e)

        @block.tensor
        def _(e):
            pe.play(e)

        @block.scalar
        def _(e):
            act.play(e)

        @block.vector
        def _(e):
            dve.play(e)

        @block.gpsimd
        def _(e):
            pool.play(e)


_INS = ["x", "c", "mod_w", "mod_b", "norm_g", "ffn_w_gu", "ffn_w_down", "sb_w_qkv", "sb_w_o", "lru_w_in", "lru_conv_w",
        "lru_conv_b", "lru_w_r", "lru_b_r", "lru_w_i", "lru_b_i", "lru_lambda", "lru_w_out", "final_norm_g",
        "norm_g_2", "w_in_2", "w_br_a_2", "w_br_b_2", "w_br_c_2", "w_out_2", "final_norm_g_2"]


def rope_constants(seq, head_dim=64, theta=10000.0):
    half = head_dim // 2
    inv_freq = (np.float32(1.0) / (np.float32(theta) ** (np.arange(0, head_dim, 2, dtype=np.float32) / np.float32(head_dim)))).astype(np.float32)
    ang = (inv_freq[:, None] * np.arange(seq, dtype=np.float32)[None, :]).astype(np.float32)
    c, s = np.cos(ang), np.sin(ang)
    return np.tile(c, (4, 1)).astype(np.float32), np.concatenate([-s, s, -s, s]).astype(np.float32)


def kernel(**inputs):
    import numpy as _np
    import concourse.bacc as _bacc
    from concourse import mybir as _mybir
    from concourse.bass_utils import run_bass_kernel_spmd as _run

    nc = _bacc.Bacc("TRN2", target_bir_lowering=False, num_devices=1)
    arrays, aps = {}, {}
    for name in _INS:
        a = _np.ascontiguousarray(inputs[name])
        arrays[f"in_{name}"] = a
        aps[name] = nc.dram_tensor(f"in_{name}", a.shape, _mybir.dt.from_np(a.dtype), kind="ExternalInput").ap()
    shape = inputs["x"].shape
    for name, a in zip(("rope_cos", "rope_sin"), rope_constants(shape[1])):
        arrays[name] = a
        aps[name] = nc.dram_tensor(name, a.shape, _mybir.dt.from_np(a.dtype), kind="ExternalInput").ap()
    out = nc.dram_tensor("out_0", shape, _mybir.dt.from_np(_np.dtype("float32")), kind="ExternalOutput").ap()
    build(nc, aps, out)
    r = _run(nc, [arrays], core_ids=[0])
    return r.results[0]["out_0"]
```
